# Optimizing a Trainium2 kernel written in Bass

```python
import jax
import jax.numpy as jnp
from jax import lax
import numpy as np
import math
import jax, jax.numpy as jnp

D_MODEL = 1024
BATCH = 1
SEQ = 256
DEPTH = 2

MEM_LEN = 256
BRANCH_W = D_MODEL
NH_M = 4
DV_M = BRANCH_W // NH_M
DQK_M = DV_M // 2
MLSTM_CHUNK = 64
CONV_K = 4
SGU_GROUPS = 4
SGU_CHUNK = 128
D_SGU = BRANCH_W
NH_X = 4
DH_X = BRANCH_W // NH_X
N_BRANCH = 3
DFF = 256 * ((8 * D_MODEL // 3 + 255) // 256)
N_NORMS = 7
EPS = 1e-6
NEG_INIT = -1e30

W_IN_SIZES = (2 * NH_M * DQK_M, NH_M * DV_M, NH_M * DV_M, NH_M, NH_M, D_SGU, D_SGU, NH_X * DH_X, N_BRANCH * BRANCH_W)
W_IN_COLS = sum(W_IN_SIZES)


def rmsnorm(x, g):
    xf = x.astype(jnp.float32)
    y = xf * lax.rsqrt(jnp.mean(xf * xf, axis=-1, keepdims=True) + EPS)
    return (y * g.astype(jnp.float32)).astype(x.dtype)

def layernorm(x, g, b=None):
    xf = x.astype(jnp.float32)
    mu = jnp.mean(xf, axis=-1, keepdims=True)
    xc = xf - mu
    y = xc * lax.rsqrt(jnp.mean(xc * xc, axis=-1, keepdims=True) + EPS) * g.astype(jnp.float32)
    if b is not None:
        y = y + b.astype(jnp.float32)
    return y.astype(x.dtype)

def swiglu(x, w_gu, w_d):
    a, b = jnp.split(x @ w_gu, 2, axis=-1)
    return (jax.nn.silu(a) * b) @ w_d

def split_cols(z):
    idx = [int(i) for i in np.cumsum(W_IN_SIZES)[:-1]]
    return jnp.split(z, idx, axis=-1)

def causal_dwconv(x, w, b):
    c = x.shape[-1]
    y = lax.conv_general_dilated(x, w[:, None, :].astype(x.dtype), window_strides=(1,),
                                 padding=[(CONV_K - 1, 0)],
                                 dimension_numbers=("NWC", "WIO", "NWC"),
                                 feature_group_count=c)
    return y + b

def mlstm_chunkwise(q, k, v, i_pre, f_pre):
    B_, S_, H, DK = q.shape
    DVv = v.shape[-1]
    NC = S_ // MLSTM_CHUNK
    f32 = jnp.float32

    def to_chunks(t):
        t = t.astype(f32).reshape((B_, NC, MLSTM_CHUNK, H) + t.shape[3:])
        return jnp.moveaxis(t, (1, 3), (0, 2))

    q_c = to_chunks(q)
    k_c = to_chunks(k) * (DK ** -0.5)
    v_c = to_chunks(v)
    i_c = to_chunks(i_pre)
    lf_c = jax.nn.log_sigmoid(to_chunks(f_pre))
    causal = jnp.tril(jnp.ones((MLSTM_CHUNK, MLSTM_CHUNK), dtype=bool))

    def step(carry, xs):
        C, n, m = carry
        qc, kc, vc, ic, fc = xs
        b = jnp.cumsum(fc, axis=-1)
        g = b[..., -1]
        log_d = jnp.where(causal, b[..., :, None] - b[..., None, :] + ic[..., None, :], -jnp.inf)
        m_inter = b + m[..., None]
        m_t = jnp.maximum(m_inter, jnp.max(log_d, axis=-1))
        d = jnp.exp(log_d - m_t[..., None])
        s = jnp.einsum("bhtd,bhsd->bhts", qc, kc) * d
        inter = jnp.exp(m_inter - m_t)
        num = jnp.einsum("bhts,bhsv->bhtv", s, vc) + inter[..., None] * jnp.einsum("bhtd,bhdv->bhtv", qc, C)
        den = jnp.sum(s, axis=-1) + inter * jnp.einsum("bhtd,bhd->bht", qc, n)
        h = num / jnp.maximum(jnp.abs(den), jnp.exp(-m_t))[..., None]
        a = g[..., None] - b + ic
        m_new = jnp.maximum(g + m, jnp.max(a, axis=-1))
        w = jnp.exp(a - m_new[..., None])
        decay = jnp.exp(g + m - m_new)
        C = decay[..., None, None] * C + jnp.einsum("bhs,bhsd,bhsv->bhdv", w, kc, vc)
        n = decay[..., None] * n + jnp.einsum("bhs,bhsd->bhd", w, kc)
        return (C, n, m_new), h

    init = (jnp.zeros((B_, H, DK, DVv), f32), jnp.zeros((B_, H, DK), f32),
            jnp.full((B_, H), NEG_INIT, f32))
    _, h = lax.scan(step, init, (q_c, k_c, v_c, i_c, lf_c))
    h = jnp.moveaxis(h, (0, 2), (1, 3)).reshape(B_, S_, H, DVv)
    return h.astype(v.dtype)

def spatial_gating(u, v, ln_g, ln_b, w_s, b_s):
    B_, S_, _ = u.shape
    nc = S_ // SGU_CHUNK
    dg = D_SGU // SGU_GROUPS
    shp = (B_, nc, SGU_CHUNK, SGU_GROUPS, dg)
    vn = layernorm(v.reshape(shp), ln_g.reshape(SGU_GROUPS, dg), ln_b.reshape(SGU_GROUPS, dg))
    w_causal = jnp.tril(w_s)
    mixed = jnp.einsum("gts,bcsgd->bctgd", w_causal, vn) + b_s.T[:, :, None]
    return (u.reshape(shp) * mixed).reshape(B_, S_, D_SGU)

def memory_cross_attention(xq, mem_n, w_mkv):
    B_, S_, _ = xq.shape
    q = xq.reshape(B_, S_, NH_X, DH_X)
    k, v = jnp.split(mem_n @ w_mkv, 2, axis=-1)
    k = k.reshape(B_, -1, NH_X, DH_X)
    v = v.reshape(B_, -1, NH_X, DH_X)
    s = jnp.einsum("bshd,bmhd->bhsm", q, k).astype(jnp.float32) * (DH_X ** -0.5)
    p = jax.nn.softmax(s, axis=-1).astype(v.dtype)
    return jnp.einsum("bhsm,bmhd->bshd", p, v).reshape(B_, S_, NH_X * DH_X)

def first_inputs(seed: int = 0) -> dict:
    key = jax.random.key(seed)
    ks = jax.random.split(key, 18)
    nrm = jax.random.normal
    f32 = jnp.float32
    return {
        "x": nrm(ks[0], (BATCH, SEQ, D_MODEL), f32),
        "mem": nrm(ks[1], (BATCH, MEM_LEN, D_MODEL), f32),
        "norm_g": 1.0 + 0.05 * nrm(ks[2], (DEPTH, N_NORMS, D_MODEL), f32),
        "w_ffn_gu": nrm(ks[3], (DEPTH, 2, D_MODEL, 2 * DFF), f32) * D_MODEL ** -0.5,
        "w_ffn_down": nrm(ks[4], (DEPTH, 2, DFF, D_MODEL), f32) * DFF ** -0.5,
        "w_in": nrm(ks[5], (DEPTH, D_MODEL, W_IN_COLS), f32) * D_MODEL ** -0.5,
        "conv_w": nrm(ks[6], (DEPTH, CONV_K, 2 * NH_M * DQK_M), f32) * CONV_K ** -0.5,
        "conv_b": 0.02 * nrm(ks[7], (DEPTH, 2 * NH_M * DQK_M), f32),
        "b_i": 0.1 * nrm(ks[8], (DEPTH, NH_M), f32),
        "b_f": 3.0 + 0.5 * nrm(ks[9], (DEPTH, NH_M), f32),
        "mlstm_norm_g": 1.0 + 0.05 * nrm(ks[10], (DEPTH, NH_M * DV_M), f32),
        "sgu_ln_g": 1.0 + 0.05 * nrm(ks[11], (DEPTH, D_SGU), f32),
        "sgu_ln_b": 0.02 * nrm(ks[12], (DEPTH, D_SGU), f32),
        "sgu_w_s": nrm(ks[13], (DEPTH, SGU_GROUPS, SGU_CHUNK, SGU_CHUNK), f32) * SGU_CHUNK ** -0.5,
        "sgu_b_s": 1.0 + 0.1 * nrm(ks[14], (DEPTH, SGU_GROUPS, SGU_CHUNK), f32),
        "w_mkv": nrm(ks[15], (DEPTH, D_MODEL, 2 * NH_X * DH_X), f32) * D_MODEL ** -0.5,
        "w_branch": nrm(ks[16], (DEPTH, N_BRANCH, BRANCH_W, D_MODEL), f32) * BRANCH_W ** -0.5,
        "w_out": nrm(ks[17], (DEPTH, D_MODEL, D_MODEL), f32) * D_MODEL ** -0.5,
    }

def first_block(x, mem, norm_g, w_ffn_gu, w_ffn_down, w_in, conv_w, conv_b, b_i, b_f,
              mlstm_norm_g, sgu_ln_g, sgu_ln_b, sgu_w_s, sgu_b_s, w_mkv, w_branch, w_out):
    h = x
    bs = x.shape[:2]
    for l in range(DEPTH):
        g = norm_g[l]
        f = swiglu(rmsnorm(h, g[0]), w_ffn_gu[l, 0], w_ffn_down[l, 0])
        h = h + 0.5 * rmsnorm(f, g[1])

        xn = rmsnorm(h, g[2])
        z = xn @ w_in[l]
        zqk, zv, zo, zi, zf, zu, zsv, zxq, zg = split_cols(z)

        qk = jax.nn.silu(causal_dwconv(zqk, conv_w[l], conv_b[l]))
        q, k = jnp.split(qk, 2, axis=-1)
        y_m = mlstm_chunkwise(q.reshape(bs + (NH_M, DQK_M)), k.reshape(bs + (NH_M, DQK_M)),
                              zv.reshape(bs + (NH_M, DV_M)), zi + b_i[l], zf + b_f[l])
        y_m = layernorm(y_m, mlstm_norm_g[l].reshape(NH_M, DV_M)).reshape(bs + (NH_M * DV_M,))
        y_m = y_m * jax.nn.sigmoid(zo)

        y_s = spatial_gating(jax.nn.gelu(zu), jax.nn.gelu(zsv), sgu_ln_g[l], sgu_ln_b[l],
                             sgu_w_s[l], sgu_b_s[l])

        y_x = memory_cross_attention(zxq, rmsnorm(mem, g[6]), w_mkv[l])

        gates = jax.nn.sigmoid(zg).reshape(bs + (N_BRANCH, D_MODEL))
        merged = (gates[..., 0, :] * (y_m @ w_branch[l, 0])
                  + gates[..., 1, :] * (y_s @ w_branch[l, 1])
                  + gates[..., 2, :] * (y_x @ w_branch[l, 2]))
        y = merged @ w_out[l]
        h = h + rmsnorm(y, g[3])

        f = swiglu(rmsnorm(h, g[4]), w_ffn_gu[l, 1], w_ffn_down[l, 1])
        h = h + 0.5 * rmsnorm(f, g[5])
    return h


GRID_W = 64
CTX_LEN = 256
NORM_EPS = 1e-6
FFN_DIM = 4 * D_MODEL

HEAD_DIM = 64
RWKV_DIM = D_MODEL // 2
RWKV_HEADS = RWKV_DIM // HEAD_DIM
DECAY_LORA = 64
AAA_LORA = 64
GATE_LORA = 128
RWKV_COLS = 3 * RWKV_DIM + DECAY_LORA + AAA_LORA + GATE_LORA
RWKV_GN_EPS = 64e-5
DIFF_V = 2 * HEAD_DIM
DIFF_HEADS = (D_MODEL // 2) // DIFF_V
DIFF_QK = DIFF_HEADS * 2 * HEAD_DIM
DIFF_COLS = 2 * DIFF_QK + DIFF_HEADS * DIFF_V
HYB_IN = RWKV_COLS + DIFF_COLS
MIX_WIDTH = RWKV_DIM + DIFF_HEADS * DIFF_V
Q_BLOCK = 128
ROPE_BASE = 10000.0
ROPE_AXIS = HEAD_DIM // 2

D_INNER = 2 * D_MODEL
SSD_HEAD_DIM = 64
SSD_HEADS = D_INNER // SSD_HEAD_DIM
SSD_GROUPS = 8
SSD_HPG = SSD_HEADS // SSD_GROUPS
D_STATE = 128
CONV_W = 5
CONV_DIM = D_INNER + 2 * SSD_GROUPS * D_STATE
SSD_IN = D_INNER + CONV_DIM + SSD_HEADS
CHUNK = 128

N_EVEN = (DEPTH + 1) // 2
N_ODD = DEPTH // 2


def rmsnorm_2(x, g, eps=NORM_EPS):
    xf = x.astype(jnp.float32)
    y = xf * lax.rsqrt(jnp.mean(xf * xf, axis=-1, keepdims=True) + eps)
    return (y * g.astype(jnp.float32)).astype(x.dtype)

def centred_shift(p):
    prev = jnp.pad(p[:, :-1], ((0, 0), (1, 0), (0, 0)))
    nxt = jnp.pad(p[:, 1:], ((0, 0), (0, 1), (0, 0)))
    return 0.5 * (prev + nxt)

def dwconv_centred(x, w, b):
    k = w.shape[0]
    out = lax.conv_general_dilated(x, w[:, None, :].astype(x.dtype), window_strides=(1,),
                                   padding=[(k // 2, k // 2)],
                                   dimension_numbers=('NWC', 'WIO', 'NWC'),
                                   feature_group_count=x.shape[-1])
    return out + b

def axial_angles(t_len):
    n_rows = t_len // GRID_W
    rows = jnp.broadcast_to(jnp.arange(n_rows)[:, None], (n_rows, GRID_W)).reshape(-1)
    cols = jnp.broadcast_to(jnp.arange(GRID_W)[None, :], (n_rows, GRID_W)).reshape(-1)
    inv = ROPE_BASE ** (-jnp.arange(0, ROPE_AXIS, 2, dtype=jnp.float32) / ROPE_AXIS)
    return rows.astype(jnp.float32)[:, None] * inv, cols.astype(jnp.float32)[:, None] * inv

def rope_half(x, ang):
    h = ROPE_AXIS // 2
    x1, x2 = x[..., :h], x[..., h:]
    cos, sin = jnp.cos(ang).astype(x.dtype), jnp.sin(ang).astype(x.dtype)
    return jnp.concatenate([x1 * cos - x2 * sin, x2 * cos + x1 * sin], axis=-1)

def rope_2d(x, ang_r, ang_c):
    ar = ang_r[:, None, None, :]
    ac = ang_c[:, None, None, :]
    return jnp.concatenate([rope_half(x[..., :ROPE_AXIS], ar), rope_half(x[..., ROPE_AXIS:], ac)], axis=-1)

def rwkv_prepare(p, mu, w0, w_up, a0, a_up, g_up, k_k, k_a):
    bsz, t_len = p.shape[:2]
    p = p + (centred_shift(p) - p) * mu
    r, k, v, wd, ad, gd = jnp.split(p, [RWKV_DIM, 2 * RWKV_DIM, 3 * RWKV_DIM,
                                        3 * RWKV_DIM + DECAY_LORA,
                                        3 * RWKV_DIM + DECAY_LORA + AAA_LORA], axis=-1)
    hd = lambda t: t.reshape(bsz, t_len, RWKV_HEADS, HEAD_DIM)
    kkf = hd(k * k_k).astype(jnp.float32)
    kk = kkf * lax.rsqrt(jnp.sum(kkf * kkf, axis=-1, keepdims=True) + 1e-12)
    g = jax.nn.sigmoid(gd) @ g_up
    dirs = []
    for d in range(2):
        wlog = -jax.nn.softplus(-(w0[d] + jnp.tanh(wd) @ w_up[d])) - 0.5
        decay = jnp.exp(-jnp.exp(wlog.astype(jnp.float32)))
        a = jax.nn.sigmoid(a0[d] + ad @ a_up[d])
        kmod = k * (1.0 + (a - 1.0) * k_a)
        dirs.append((hd(decay), hd(kmod), kk * hd(a).astype(jnp.float32)))
    return hd(r), hd(v), kk, g, dirs

def wkv_scan(r, decay, k, v, kk, b, s0, reverse):
    xs = tuple(jnp.moveaxis(t.astype(jnp.float32), 1, 0) for t in (r, decay, k, v, kk, b))

    def step(s, inp):
        r_t, w_t, k_t, v_t, kk_t, b_t = inp
        sa = jnp.einsum('bhvk,bhk->bhv', s, -kk_t)
        s = s * w_t[:, :, None, :] + sa[..., None] * b_t[:, :, None, :] + v_t[..., None] * k_t[:, :, None, :]
        return s, jnp.einsum('bhvk,bhk->bhv', s, r_t)

    s, ys = lax.scan(step, s0, xs, reverse=reverse)
    return jnp.moveaxis(ys, 0, 1), s

def wkv_bidir(prep, s0s):
    r, v, kk, _, dirs = prep
    (df, kf, bf), (db, kb, bb) = dirs
    yf, sf = wkv_scan(r, df, kf, v, kk, bf, s0s[0], False)
    yb, sb = wkv_scan(r, db, kb, v, kk, bb, s0s[1], True)
    return yf + yb, sf, sb

def rwkv_output(y, prep, r_k, ln_w, ln_b):
    r, v, _, g, dirs = prep
    bsz, t_len = r.shape[:2]
    mean = jnp.mean(y, axis=-1, keepdims=True)
    var = jnp.mean(jnp.square(y - mean), axis=-1, keepdims=True)
    yn = ((y - mean) * lax.rsqrt(var + RWKV_GN_EPS)).reshape(bsz, t_len, RWKV_DIM)
    yn = (yn * ln_w + ln_b).astype(r.dtype)
    k_bonus = 0.5 * (dirs[0][1] + dirs[1][1])
    bonus = (jnp.sum(r * k_bonus * r_k, axis=-1, keepdims=True) * v).reshape(bsz, t_len, RWKV_DIM)
    return (yn + bonus) * g

def diff_combine(s, lam, v):
    p = jax.nn.softmax(s.astype(jnp.float32), axis=-1)
    w = p[:, :, 0] - lam * p[:, :, 1]
    return jnp.einsum('bhqk,bhkd->bhqd', w.astype(v.dtype), v)

def diff_attn_latent(q_rot, q_plain, k_rot, k_ctx, v_all, lam):
    bsz, t_len = q_rot.shape[:2]
    nblk = t_len // Q_BLOCK
    to_blocks = lambda q: q.reshape(bsz, nblk, Q_BLOCK, DIFF_HEADS, 2, HEAD_DIM).transpose(1, 0, 3, 4, 2, 5)
    kr = k_rot.transpose(0, 2, 3, 1, 4)
    kc = k_ctx.transpose(0, 2, 3, 1, 4)
    vt = v_all.transpose(0, 2, 1, 3)
    scale = HEAD_DIM ** -0.5

    def block(qs):
        qr, qp = qs
        s = jnp.concatenate([jnp.einsum('bhmqd,bhmkd->bhmqk', qr, kr),
                             jnp.einsum('bhmqd,bhmkd->bhmqk', qp, kc)], axis=-1) * scale
        return diff_combine(s, lam, vt)

    o = lax.map(block, (to_blocks(q_rot), to_blocks(q_plain)))
    return o.transpose(1, 0, 3, 2, 4).reshape(bsz, t_len, DIFF_HEADS, DIFF_V)

def hybrid_mixer(h_lat, h_ctx, ang_r, ang_c, lam_init, ctx_out, w_in, w_out, mu, w0, w_up, a0, a_up,
                 g_up, k_k, k_a, r_k, ln_w, ln_b, lq1, lk1, lq2, lk2, subln_g):
    bsz, t_len = h_lat.shape[:2]
    l_ctx = h_ctx.shape[1]
    p_lat = h_lat @ w_in
    p_ctx = h_ctx @ w_in

    rc = rwkv_prepare(p_ctx[..., :RWKV_COLS], mu, w0, w_up, a0, a_up, g_up, k_k, k_a)
    rl = rwkv_prepare(p_lat[..., :RWKV_COLS], mu, w0, w_up, a0, a_up, g_up, k_k, k_a)
    s_zero = jnp.zeros((bsz, RWKV_HEADS, HEAD_DIM, HEAD_DIM), jnp.float32)
    yc, sf, sb = wkv_bidir(rc, (s_zero, s_zero))
    yl, _, _ = wkv_bidir(rl, (sf, sb))
    a_lat = rwkv_output(yl, rl, r_k, ln_w, ln_b)

    lam = (jnp.exp(jnp.sum(lq1 * lk1).astype(jnp.float32)) - jnp.exp(jnp.sum(lq2 * lk2).astype(jnp.float32))
           + lam_init)
    def qkv(p, n):
        d = p[..., RWKV_COLS:]
        q = d[..., :DIFF_QK].reshape(bsz, n, DIFF_HEADS, 2, HEAD_DIM)
        k = d[..., DIFF_QK:2 * DIFF_QK].reshape(bsz, n, DIFF_HEADS, 2, HEAD_DIM)
        v = d[..., 2 * DIFF_QK:].reshape(bsz, n, DIFF_HEADS, DIFF_V)
        return q, k, v
    ql, kl, vl = qkv(p_lat, t_len)
    qc, kc, vc = qkv(p_ctx, l_ctx)
    o_l = diff_attn_latent(rope_2d(ql, ang_r, ang_c), ql, rope_2d(kl, ang_r, ang_c), kc,
                           jnp.concatenate([vl, vc], axis=1), lam)
    subln = lambda o, n: (rmsnorm_2(o, subln_g) * (1.0 - lam_init)).reshape(bsz, n, DIFF_HEADS * DIFF_V)
    out_lat = jnp.concatenate([a_lat, subln(o_l, t_len)], axis=-1) @ w_out
    if not ctx_out:
        return out_lat, None
    a_ctx = rwkv_output(yc, rc, r_k, ln_w, ln_b)
    s_c = jnp.einsum('bqhmd,bkhmd->bhmqk', qc, kc) * (HEAD_DIM ** -0.5)
    o_c = diff_combine(s_c, lam, vc.transpose(0, 2, 1, 3)).transpose(0, 2, 1, 3)
    out_ctx = jnp.concatenate([a_ctx, subln(o_c, l_ctx)], axis=-1) @ w_out
    return out_lat, out_ctx

def ssd_scan(x, dt, a, bm, cm, h0):
    bsz, t_len = x.shape[:2]
    nc = t_len // CHUNK
    chunks = lambda t: jnp.moveaxis(t.reshape((bsz, nc, CHUNK) + t.shape[2:]), 1, 0)
    idx = jnp.arange(CHUNK)
    mask = (idx[:, None] >= idx[None, :])[:, :, None, None]

    def step(h, inp):
        xc, dtc, bc, cc = inp
        cs = jnp.cumsum(dtc * a, axis=1)
        seg = cs[:, :, None] - cs[:, None, :]
        lmat = jnp.exp(jnp.where(mask, seg, -jnp.inf))
        xdt = xc * dtc[..., None]
        cb = jnp.einsum('blgn,bsgn->blsg', cc, bc)
        y_diag = jnp.einsum('blsg,blsgh,bsghp->blghp', cb, lmat, xdt)
        y_off = jnp.einsum('blgn,bghpn->blghp', cc, h) * jnp.exp(cs)[..., None]
        h_new = (h * jnp.exp(cs[:, -1])[..., None, None]
                 + jnp.einsum('bsgn,bsgh,bsghp->bghpn', bc, jnp.exp(cs[:, -1:] - cs), xdt))
        return h_new, y_diag + y_off

    h, ys = lax.scan(step, h0, (chunks(x), chunks(dt), chunks(bm), chunks(cm)))
    return jnp.moveaxis(ys, 0, 1).reshape(x.shape), h

def ssd_mixer(h_lat, h_ctx, ctx_out, w_in, conv_w, conv_b, dt_bias, a_log, d_skip, norm_g, w_out):
    bsz = h_lat.shape[0]

    def prep(h):
        n = h.shape[1]
        p = h @ w_in
        z, xbc, dt = jnp.split(p, [D_INNER, D_INNER + CONV_DIM], axis=-1)
        xbc = jax.nn.silu(dwconv_centred(xbc, conv_w, conv_b))
        xs, bm, cm = jnp.split(xbc, [D_INNER, D_INNER + SSD_GROUPS * D_STATE], axis=-1)
        f = jnp.float32
        return (z, xs.reshape(bsz, n, SSD_GROUPS, SSD_HPG, SSD_HEAD_DIM).astype(f),
                bm.reshape(bsz, n, SSD_GROUPS, D_STATE).astype(f),
                cm.reshape(bsz, n, SSD_GROUPS, D_STATE).astype(f),
                dt.reshape(bsz, n, SSD_GROUPS, SSD_HPG).astype(f))

    def run(pr, h0s):
        _, xs, bm, cm, dt = pr
        y = d_skip.reshape(SSD_GROUPS, SSD_HPG).astype(jnp.float32)[..., None] * xs
        flip = lambda t: jnp.flip(t, axis=1)
        finals = []
        for d in range(2):
            dtd = jax.nn.softplus(dt + dt_bias[d].reshape(SSD_GROUPS, SSD_HPG).astype(jnp.float32))
            a = -jnp.exp(a_log[d].reshape(SSD_GROUPS, SSD_HPG).astype(jnp.float32))
            if d == 0:
                yd, hd = ssd_scan(xs, dtd, a, bm, cm, h0s[0])
            else:
                yd, hd = ssd_scan(flip(xs), flip(dtd), a, flip(bm), flip(cm), h0s[1])
                yd = flip(yd)
            y = y + yd
            finals.append(hd)
        return y, finals

    def out(y, z):
        n = z.shape[1]
        yg = y.reshape(bsz, n, D_INNER).astype(z.dtype) * jax.nn.silu(z)
        yn = rmsnorm_2(yg.reshape(bsz, n, SSD_GROUPS, D_INNER // SSD_GROUPS),
                     norm_g.reshape(SSD_GROUPS, D_INNER // SSD_GROUPS))
        return yn.reshape(bsz, n, D_INNER) @ w_out

    pc = prep(h_ctx)
    h_zero = jnp.zeros((bsz, SSD_GROUPS, SSD_HPG, SSD_HEAD_DIM, D_STATE), jnp.float32)
    yc, finals = run(pc, (h_zero, h_zero))
    pl = prep(h_lat)
    yl, _ = run(pl, finals)
    out_lat = out(yl, pl[0])
    out_ctx = out(yc, pc[0]) if ctx_out else None
    return out_lat, out_ctx

def sq_relu_mlp(h, w1, w2):
    return jnp.square(jax.nn.relu(h @ w1)) @ w2

def second_inputs(seed: int = 0) -> dict:
    key = jax.random.key(seed)
    ks = iter(jax.random.split(key, 48))
    f32 = jnp.float32
    nrm = lambda shape, s: jax.random.normal(next(ks), shape, f32) * s
    D = D_MODEL
    dt0 = jnp.exp(jax.random.uniform(next(ks), (N_ODD, 2, SSD_HEADS), f32)
                  * (math.log(0.1) - math.log(0.001)) + math.log(0.001))
    return {
        "x": nrm((BATCH, SEQ, D), 1.0),
        "c": nrm((BATCH, D), 1.0),
        "ctx": nrm((BATCH, CTX_LEN, D), 1.0),
        "c_ctx": nrm((D,), 1.0),
        "ada_w": nrm((DEPTH, D, 6 * D), 0.5 * D ** -0.5),
        "ada_b": nrm((DEPTH, 6 * D), 0.02),
        "norm1_g": 1.0 + nrm((DEPTH, D), 0.02),
        "norm2_g": 1.0 + nrm((DEPTH, D), 0.02),
        "mlp_w1": nrm((DEPTH, D, FFN_DIM), D ** -0.5),
        "mlp_w2": nrm((DEPTH, FFN_DIM, D), FFN_DIM ** -0.5),
        "hy_w_in": nrm((N_EVEN, D, HYB_IN), D ** -0.5),
        "hy_w_out": nrm((N_EVEN, MIX_WIDTH, D), MIX_WIDTH ** -0.5),
        "rwkv_mu": jax.random.uniform(next(ks), (N_EVEN, RWKV_COLS), f32),
        "rwkv_w0": nrm((N_EVEN, 2, RWKV_DIM), 0.3),
        "rwkv_w_up": nrm((N_EVEN, 2, DECAY_LORA, RWKV_DIM), 0.5 * DECAY_LORA ** -0.5),
        "rwkv_a0": nrm((N_EVEN, 2, RWKV_DIM), 0.3),
        "rwkv_a_up": nrm((N_EVEN, 2, AAA_LORA, RWKV_DIM), 0.5 * AAA_LORA ** -0.5),
        "rwkv_g_up": nrm((N_EVEN, GATE_LORA, RWKV_DIM), GATE_LORA ** -0.5),
        "rwkv_k_k": 0.85 + nrm((N_EVEN, RWKV_DIM), 0.02),
        "rwkv_k_a": 1.0 + nrm((N_EVEN, RWKV_DIM), 0.02),
        "rwkv_r_k": nrm((N_EVEN, RWKV_HEADS, HEAD_DIM), 0.1),
        "rwkv_ln_w": 1.0 + nrm((N_EVEN, RWKV_DIM), 0.02),
        "rwkv_ln_b": nrm((N_EVEN, RWKV_DIM), 0.02),
        "diff_lq1": nrm((N_EVEN, HEAD_DIM), 0.1),
        "diff_lk1": nrm((N_EVEN, HEAD_DIM), 0.1),
        "diff_lq2": nrm((N_EVEN, HEAD_DIM), 0.1),
        "diff_lk2": nrm((N_EVEN, HEAD_DIM), 0.1),
        "diff_subln_g": 1.0 + nrm((N_EVEN, DIFF_V), 0.02),
        "ssd_w_in": nrm((N_ODD, D, SSD_IN), D ** -0.5),
        "ssd_conv_w": nrm((N_ODD, CONV_W, CONV_DIM), CONV_W ** -0.5),
        "ssd_conv_b": nrm((N_ODD, CONV_DIM), 0.02),
        "ssd_dt_bias": dt0 + jnp.log(-jnp.expm1(-dt0)),
        "ssd_a_log": jnp.log(jax.random.uniform(next(ks), (N_ODD, 2, SSD_HEADS), f32, 1.0, 16.0)),
        "ssd_d": 1.0 + nrm((N_ODD, SSD_HEADS), 0.1),
        "ssd_norm_g": 1.0 + nrm((N_ODD, D_INNER), 0.02),
        "ssd_w_out": nrm((N_ODD, D_INNER, D), D_INNER ** -0.5),
        "norm_f_g": 1.0 + nrm((D,), 0.02),
    }

def second_block(x, c, ctx, c_ctx, ada_w, ada_b, norm1_g, norm2_g, mlp_w1, mlp_w2, hy_w_in, hy_w_out,
              rwkv_mu, rwkv_w0, rwkv_w_up, rwkv_a0, rwkv_a_up, rwkv_g_up, rwkv_k_k, rwkv_k_a, rwkv_r_k,
              rwkv_ln_w, rwkv_ln_b, diff_lq1, diff_lk1, diff_lq2, diff_lk2, diff_subln_g,
              ssd_w_in, ssd_conv_w, ssd_conv_b, ssd_dt_bias, ssd_a_log, ssd_d, ssd_norm_g, ssd_w_out,
              norm_f_g):
    t_len = x.shape[1]
    ang_r, ang_c = axial_angles(t_len)
    xl, xc = x, ctx
    for li in range(DEPTH):
        last = li == DEPTH - 1
        mod_l = jnp.split((jax.nn.silu(c) @ ada_w[li] + ada_b[li])[:, None, :], 6, axis=-1)
        mod_c = jnp.split(jax.nn.silu(c_ctx) @ ada_w[li] + ada_b[li], 6, axis=-1)
        hl = rmsnorm_2(xl, norm1_g[li]) * (1.0 + mod_l[1]) + mod_l[0]
        hc = rmsnorm_2(xc, norm1_g[li]) * (1.0 + mod_c[1]) + mod_c[0]
        if li % 2 == 0:
            e = li // 2
            lam_init = 0.8 - 0.6 * math.exp(-0.3 * li)
            ol, oc = hybrid_mixer(hl, hc, ang_r, ang_c, lam_init, not last, hy_w_in[e], hy_w_out[e],
                                  rwkv_mu[e], rwkv_w0[e], rwkv_w_up[e], rwkv_a0[e], rwkv_a_up[e],
                                  rwkv_g_up[e], rwkv_k_k[e], rwkv_k_a[e], rwkv_r_k[e], rwkv_ln_w[e],
                                  rwkv_ln_b[e], diff_lq1[e], diff_lk1[e], diff_lq2[e], diff_lk2[e],
                                  diff_subln_g[e])
        else:
            o = li // 2
            ol, oc = ssd_mixer(hl, hc, not last, ssd_w_in[o], ssd_conv_w[o], ssd_conv_b[o],
                               ssd_dt_bias[o], ssd_a_log[o], ssd_d[o], ssd_norm_g[o], ssd_w_out[o])
        xl = xl + mod_l[2] * ol
        hl = rmsnorm_2(xl, norm2_g[li]) * (1.0 + mod_l[4]) + mod_l[3]
        xl = xl + mod_l[5] * sq_relu_mlp(hl, mlp_w1[li], mlp_w2[li])
        if not last:
            xc = xc + mod_c[2] * oc
            hc = rmsnorm_2(xc, norm2_g[li]) * (1.0 + mod_c[4]) + mod_c[3]
            xc = xc + mod_c[5] * sq_relu_mlp(hc, mlp_w1[li], mlp_w2[li])
    return rmsnorm_2(xl, norm_f_g)


_first_inputs = second_inputs


def second_inputs(seed=0):
    import zlib

    import numpy as np

    out = dict(_first_inputs(seed))
    spreads = {}
    factors = {'norm1_g': 5.753,
     'norm2_g': 25.999,
     'rwkv_w0': 18.084,
     'rwkv_w_up': 21.011,
     'rwkv_a0': 2.932,
     'rwkv_k_k': 200.0,
     'rwkv_k_a': 8.0,
     'rwkv_ln_w': 200.0,
     'rwkv_ln_b': 200.0,
     'diff_lq1': 8.0,
     'diff_lk1': 22.35,
     'diff_lk2': 11.941,
     'diff_subln_g': 200.0,
     'ssd_conv_b': 200.0,
     'ssd_d': 200.0,
     'ssd_norm_g': 200.0,
     'ssd_a_log': 3.533,
     'ssd_dt_bias': 2.779}
    for name, (base, spread) in spreads.items():
        noise = np.random.default_rng([zlib.crc32(name.encode()), seed]).standard_normal(out[name].shape)
        drawn = base * np.exp(spread * noise) if base else spread * noise
        out[name] = __import__('jax').numpy.asarray(drawn.astype(out[name].dtype))
    for name, factor in factors.items():
        out[name] = (out[name] * factor).astype(out[name].dtype)
    return out


_narrow_inputs = second_inputs


def second_inputs(seed=0):
    out = dict(_narrow_inputs(seed))
    wider = {'rwkv_k_k': 12.0,
     'rwkv_ln_w': 4.47,
     'rwkv_ln_b': 4.41,
     'diff_subln_g': 3.58,
     'ssd_d': 10.1,
     'ssd_norm_g': 12.0}
    for name, times in wider.items():
        mean = out[name].mean()
        out[name] = (mean + times * (out[name] - mean)).astype(out[name].dtype)
    return out


def setup_inputs(seed=0):
    out = dict(first_inputs(seed))
    for name, value in second_inputs(seed + 1).items():
        if name != "x":
            out[name + "_2"] = value
    return out


def reference(
    x, mem, norm_g, w_ffn_gu, w_ffn_down, w_in, conv_w, conv_b, b_i, b_f, mlstm_norm_g,
    sgu_ln_g, sgu_ln_b, sgu_w_s, sgu_b_s, w_mkv, w_branch, w_out, c_2, ctx_2, c_ctx_2, ada_w_2,
    ada_b_2, norm1_g_2, norm2_g_2, mlp_w1_2, mlp_w2_2, hy_w_in_2, hy_w_out_2, rwkv_mu_2,
    rwkv_w0_2, rwkv_w_up_2, rwkv_a0_2, rwkv_a_up_2, rwkv_g_up_2, rwkv_k_k_2, rwkv_k_a_2,
    rwkv_r_k_2, rwkv_ln_w_2, rwkv_ln_b_2, diff_lq1_2, diff_lk1_2, diff_lq2_2, diff_lk2_2,
    diff_subln_g_2, ssd_w_in_2, ssd_conv_w_2, ssd_conv_b_2, ssd_dt_bias_2, ssd_a_log_2, ssd_d_2,
    ssd_norm_g_2, ssd_w_out_2, norm_f_g_2,
):
    x = first_block(
        x, mem, norm_g, w_ffn_gu, w_ffn_down, w_in, conv_w, conv_b, b_i, b_f, mlstm_norm_g,
        sgu_ln_g, sgu_ln_b, sgu_w_s, sgu_b_s, w_mkv, w_branch, w_out,
    )
    return second_block(
        x, c_2, ctx_2, c_ctx_2, ada_w_2, ada_b_2, norm1_g_2, norm2_g_2, mlp_w1_2, mlp_w2_2,
        hy_w_in_2, hy_w_out_2, rwkv_mu_2, rwkv_w0_2, rwkv_w_up_2, rwkv_a0_2, rwkv_a_up_2,
        rwkv_g_up_2, rwkv_k_k_2, rwkv_k_a_2, rwkv_r_k_2, rwkv_ln_w_2, rwkv_ln_b_2, diff_lq1_2,
        diff_lk1_2, diff_lq2_2, diff_lk2_2, diff_subln_g_2, ssd_w_in_2, ssd_conv_w_2,
        ssd_conv_b_2, ssd_dt_bias_2, ssd_a_log_2, ssd_d_2, ssd_norm_g_2, ssd_w_out_2,
        norm_f_g_2,
    )


_drawn_inputs = setup_inputs


def setup_inputs(seed=0):
    import zlib

    import numpy as np

    out = dict(_drawn_inputs(seed))
    spreads = {}
    factors = {'b_i': 8.0, 'norm_f_g_2': 3.006}
    for name, (base, spread) in spreads.items():
        noise = np.random.default_rng([zlib.crc32(name.encode()), seed]).standard_normal(out[name].shape)
        drawn = base * np.exp(spread * noise) if base else spread * noise
        out[name] = jnp.asarray(drawn.astype(out[name].dtype))
    for name, factor in factors.items():
        out[name] = (out[name] * factor).astype(out[name].dtype)
    return out
```

```python
import math
from contextlib import ExitStack

import concourse.bass as bass
import numpy as np
from concourse import mybir

F32 = mybir.dt.float32
ALU = mybir.AluOpType
ACT = mybir.ActivationFunctionType
AX = mybir.AxisListType.X

P = 128
D = 1024
KD = D // P
SEQ = 256
NT = SEQ // P
DEPTH = 2
EPS = 1e-6
BANK = 512
RING = 2
CHUNK = KD * BANK


class Core:

    def __init__(self, nc, block, ctx):
        self.nc, self.block, self.ctx = nc, block, ctx
        self.steps_done = ctx.enter_context(nc.semaphore("steps_done"))
        self.steps = 0
        self.weights_arrived = [ctx.enter_context(nc.semaphore(f"weights_arrived_{i}")) for i in range(RING)]
        self.multiplied = ctx.enter_context(nc.semaphore("chunks_multiplied"))
        self.arrivals = [0] * RING
        self.taken_by_scalar = ctx.enter_context(nc.semaphore("products_taken_by_scalar"))
        self.taken_by_vector = ctx.enter_context(nc.semaphore("products_taken_by_vector"))
        self.params_arrived = ctx.enter_context(nc.semaphore("params_arrived"))
        self.chunks = 0
        self.taken = 2
        self.params = 0
        self.ring = self.sb("weight_ring", [P, RING, CHUNK])
        self.ps = ctx.enter_context(nc.psum_tensor("banks", [P, 8, BANK], F32))
        self.half = 0

    def sb(self, name, shape):
        return self.ctx.enter_context(self.nc.sbuf_tensor(name, shape, F32))

    def load(self, dst, src):
        at = self.steps

        @self.block.gpsimd
        def _(pool):
            pool.wait_ge(self.steps_done, at)
            pool.dma_start(dst, src).then_inc(self.params_arrived, 16)
        self.params += 1

    def loaded(self):
        n = 16 * self.params

        @self.block.tensor
        def _(pe):
            pe.wait_ge(self.params_arrived, n)

        @self.block.vector
        def _(v):
            v.wait_ge(self.params_arrived, n)

        @self.block.scalar
        def _(s):
            s.wait_ge(self.params_arrived, n)

        @self.block.gpsimd
        def _(g):
            g.wait_ge(self.params_arrived, n)

    def prime(self):
        @self.block.tensor
        def _(pe):
            pe.sem_inc(self.multiplied, 2)

        @self.block.scalar
        def _(s):
            s.sem_inc(self.taken_by_scalar, 2)

        @self.block.vector
        def _(v):
            v.sem_inc(self.taken_by_vector, 2)

    def weights(self, chunk, shape):
        w = self.ring[:, chunk % RING, 0:int(np.prod(shape))]
        return w.rearrange("p (k n) -> p k n", n=shape[-1])

    def stream(self, count, source, shape):
        before = list(self.arrivals)
        n0 = self.chunks
        parts = len(source(0))
        loops = count // RING if count // RING >= 2 else 0

        @self.block.sync
        def _(sp):
            def load(s, i):
                chunk = n0 + s
                done = chunk - RING + 3
                sp.wait_ge(self.multiplied, done if i is None else i * RING + done)
                for cols, src in source(s if i is None else i * RING + s):
                    dst = self.weights(chunk, shape)
                    dst = dst if cols is None else dst[:, cols[0], cols[1]]
                    sp.dma_start(dst, src).then_inc(self.weights_arrived[chunk % RING], 16)
            if loops:
                with sp.Fori(0, loops) as i:
                    for s in range(RING):
                        load(s, i)
            for s in range(loops * RING, count):
                load(s, None)
        for s in range(count):
            self.arrivals[(n0 + s) % RING] += 16 * parts
        return before, n0, parts, loops

    def gemm(self, count, source, shape, product, take_scalar, take_vector, after_scalar=False):
        nc, at, g0 = self.nc, self.steps, self.taken
        before, n0, parts, loops = self.stream(count, source, shape)

        @self.block.tensor
        def _(pe):
            pe.wait_ge(self.steps_done, at)

            def multiply(s, i):
                slot = (n0 + s) % RING
                arrived = before[slot] + 16 * parts * (s // RING + 1)
                pe.wait_ge(self.weights_arrived[slot], arrived if i is None else i * (16 * parts) + arrived)
                free = g0 + s - 1
                pe.wait_ge(self.taken_by_scalar, free if i is None else i * RING + free)
                pe.wait_ge(self.taken_by_vector, free if i is None else i * RING + free)
                product(s % 2 * 4, self.weights(n0 + s, shape), nc.tensor).then_inc(self.multiplied, 1)
            if loops:
                with pe.Fori(0, loops) as i:
                    for s in range(RING):
                        multiply(s, i)
            for s in range(loops * RING, count):
                multiply(s, None)

        @self.block.scalar
        def _(s):
            s.wait_ge(self.steps_done, at)

            def empty(chunk, i):
                ready = n0 + chunk + 3
                s.wait_ge(self.multiplied, ready if i is None else i * RING + ready)
                last = take_scalar(chunk if i is None else i * RING + chunk, chunk % 2, s)
                if last is None:
                    s.sem_inc(self.taken_by_scalar, 1)
                else:
                    last.then_inc(self.taken_by_scalar, 1)
            if loops:
                with s.Fori(0, loops) as i:
                    for chunk in range(RING):
                        empty(chunk, i)
            for chunk in range(loops * RING, count):
                empty(chunk, None)

        @self.block.vector
        def _(v):
            v.wait_ge(self.steps_done, at)

            def empty(chunk, i):
                ready = n0 + chunk + 3
                v.wait_ge(self.multiplied, ready if i is None else i * RING + ready)
                if after_scalar:
                    made = g0 + chunk + 1
                    v.wait_ge(self.taken_by_scalar, made if i is None else i * RING + made)
                last = take_vector(chunk if i is None else i * RING + chunk, chunk % 2, v)
                if last is None:
                    v.sem_inc(self.taken_by_vector, 1)
                else:
                    last.then_inc(self.taken_by_vector, 1)
            if loops:
                with v.Fori(0, loops) as i:
                    for chunk in range(RING):
                        empty(chunk, i)
            for chunk in range(loops * RING, count):
                empty(chunk, None)
        self.chunks += count
        self.taken += count
        n = self.taken

        @self.block.tensor
        def _(pe):
            pe.wait_ge(self.taken_by_scalar, n)
            pe.wait_ge(self.taken_by_vector, n)

        @self.block.scalar
        def _(s):
            s.wait_ge(self.taken_by_scalar, n)
            s.wait_ge(self.taken_by_vector, n)

        @self.block.vector
        def _(v):
            v.wait_ge(self.taken_by_scalar, n)
            v.wait_ge(self.taken_by_vector, n)

        @self.block.gpsimd
        def _(g):
            g.wait_ge(self.taken_by_scalar, n)
            g.wait_ge(self.taken_by_vector, n)

    def gemm_token_major(self, x, tiles, count, source, width, take_scalar, take_vector, after_scalar=False):
        def product(banks, w, pe):
            for n, t in enumerate(tiles):
                for k in range(KD):
                    last = pe.matmul(self.ps[:, banks + n, 0:width], x[:, k, t * P:(t + 1) * P],
                                     w[:, k, :], start=(k == 0), stop=(k == KD - 1))
            return last
        self.gemm(count, source, (KD, width), product, take_scalar, take_vector, after_scalar)

    def gemm_feature_major(self, x, tokens, count, source, width, take_scalar, take_vector, after_scalar=False):
        def product(banks, w, pe):
            for j in range(width // P):
                at = j * tokens
                out = self.ps[:, banks + at // BANK, at % BANK:at % BANK + tokens]
                for k in range(KD):
                    last = pe.matmul(out, w[:, k, j * P:(j + 1) * P], x[:, k, 0:tokens],
                                     start=(k == 0), stop=(k == KD - 1))
            return last
        self.gemm(count, source, (KD, width), product, take_scalar, take_vector, after_scalar)

    def gemm_rows(self, x, k_chunks, tiles, w_rows):
        nc, at = self.nc, self.steps
        w_v = w_rows.rearrange("(k p) n -> p k n", p=P)
        groups = [(k, min(4, k_chunks - k)) for k in range(0, k_chunks, 4)]
        for first, size in groups:
            _, n0, _, _ = self.stream(1, lambda i: [((slice(0, size), slice(0, D)), w_v[:, first:first + size, :])],
                                      (4, D))
            arrived = self.arrivals[n0 % RING]

            @self.block.tensor
            def _(pe):
                pe.wait_ge(self.steps_done, at)
                pe.wait_ge(self.weights_arrived[n0 % RING], arrived)
                w = self.weights(n0, (4, D))
                for j in range(size):
                    k = first + j
                    for n, t in enumerate(tiles):
                        for half in range(2):
                            last = nc.tensor.matmul(self.ps[:, 2 * n + half, :], x[:, k, t * P:(t + 1) * P],
                                                    w[:, j, half * BANK:(half + 1) * BANK],
                                                    start=(k == 0), stop=(k == k_chunks - 1))
                last.then_inc(self.multiplied, 1)
            self.chunks += 1
        n = self.chunks + 2

        @self.block.scalar
        def _(s):
            s.wait_ge(self.multiplied, n)

        @self.block.vector
        def _(v):
            v.wait_ge(self.multiplied, n)

    def take_rows(self, out, tiles):
        ps = self.ps

        @self.block.scalar
        def _(s):
            s.wait_ge(self.steps_done, self.steps)
            for t in range(tiles):
                last = s.activation(out[:, t, 0:BANK], ps[:, 2 * t, :], ACT.Copy)
            last.then_inc(self.steps_done, 1)
        @self.block.vector
        def _(v):
            v.wait_ge(self.steps_done, self.steps)
            for t in range(tiles):
                last = v.tensor_copy(out[:, t, BANK:D], ps[:, 2 * t + 1, :])
            last.then_inc(self.steps_done, 1)
        self.steps += 2

    def transposes(self, quads):
        ident, ps = self.ident, self.ps
        batches = [quads[n:n + 4] for n in range(0, len(quads), 4)]

        def banks_of(n, which):
            for b, (srcs, dst) in enumerate(batches[n]):
                if b % 2 == which:
                    m = srcs[0].shape[-1]
                    yield ps[0:m, n % 2 * 4 + b, 0:len(srcs) * P].rearrange("p (j t) -> p j t", t=P), dst

        for n in range(len(batches) + 1):
            at = self.steps
            if n < len(batches):
                @self.block.tensor
                def _(pe):
                    pe.wait_ge(self.steps_done, at)
                    for b, (srcs, _) in enumerate(batches[n]):
                        for j, src in enumerate(srcs):
                            out = ps[0:src.shape[-1], n % 2 * 4 + b, j * P:(j + 1) * P]
                            last = pe.transpose(out, src, ident[:, :])
                    last.then_inc(self.steps_done, 1)
                self.steps += 1
            if n:
                @self.block.scalar
                def _(s):
                    s.wait_ge(self.steps_done, at)
                    for src, dst in banks_of(n - 1, 0):
                        last = s.activation(dst, src, ACT.Copy)
                    last.then_inc(self.steps_done, 1)
                self.steps += 1
            if n and len(batches[n - 1]) > 1:
                @self.block.vector
                def _(v):
                    v.wait_ge(self.steps_done, at)
                    for src, dst in banks_of(n - 1, 1):
                        last = v.tensor_copy(dst, src)
                    last.then_inc(self.steps_done, 1)
                self.steps += 1

    def to_feature_major(self, x, dst, tiles, first=0, kd=KD):
        self.transposes([([x(t, k + j) for j in range(4)], dst[:, k:k + 4, (first + t) * P:(first + t + 1) * P])
                         for t in range(tiles) for k in range(0, kd, 4)])

    def rstd(self, ss, scale, eps):

        @self.block.vector
        def _(v):
            v.wait_ge(self.steps_done, self.steps)
            v.tensor_scalar(ss, ss, scale, eps, ALU.mult, ALU.add).then_inc(self.steps_done, 1)
        self.steps += 1

        @self.block.scalar
        def _(s):
            s.wait_ge(self.steps_done, self.steps)
            s.activation(ss, ss, ACT.Sqrt).then_inc(self.steps_done, 1)
        self.steps += 1

        @self.block.vector
        def _(v):
            v.wait_ge(self.steps_done, self.steps)
            v.reciprocal(ss, ss).then_inc(self.steps_done, 1)
        self.steps += 1

    def rmsnorm(self, xs, outs, gain, n=D, squared=None):
        ss = self.small[:, 0:len(xs)]

        @self.block.scalar
        def _(s):
            s.wait_ge(self.steps_done, self.steps)
            for j, (x, out) in enumerate(zip(xs, squared or outs)):
                last = s.activation(out, x, ACT.Square, accum_out=ss[:, j:j + 1])
            last.then_inc(self.steps_done, 1)
        self.steps += 1
        self.rstd(ss, 1.0 / n, EPS)

        @self.block.vector
        def _(v):
            v.wait_ge(self.steps_done, self.steps)
            for j, (x, out) in enumerate(zip(xs, outs)):
                last = v.scalar_tensor_tensor(out, x, ss[:, j:j + 1], gain, ALU.mult, ALU.mult)
            last.then_inc(self.steps_done, 1)
        self.steps += 1

    def log1p(self, e, out, z, z2):

        @self.block.vector
        def _(v):
            v.wait_ge(self.steps_done, self.steps)
            v.tensor_scalar(z, e, 2.0, None, ALU.add).then_inc(self.steps_done, 1)
        self.steps += 1

        @self.block.vector
        def _(v):
            v.wait_ge(self.steps_done, self.steps)
            v.reciprocal(z, z).then_inc(self.steps_done, 1)
        self.steps += 1

        @self.block.vector
        def _(v):
            v.wait_ge(self.steps_done, self.steps)
            v.tensor_tensor(z, z, e, ALU.mult).then_inc(self.steps_done, 1)
        self.steps += 1

        @self.block.vector
        def _(v):
            v.wait_ge(self.steps_done, self.steps)
            v.tensor_tensor(z2, z, z, ALU.mult).then_inc(self.steps_done, 1)
        self.steps += 1

        @self.block.vector
        def _(v):
            v.wait_ge(self.steps_done, self.steps)
            v.tensor_scalar(out, z2, 1.0 / 17, None, ALU.mult).then_inc(self.steps_done, 1)
        self.steps += 1
        for odd in (15, 13, 11, 9, 7, 5, 3):

            @self.block.vector
            def _(v):
                v.wait_ge(self.steps_done, self.steps)
                v.scalar_tensor_tensor(out, out, 1.0 / odd, z2, ALU.add, ALU.mult).then_inc(self.steps_done, 1)
            self.steps += 1

        @self.block.vector
        def _(v):
            v.wait_ge(self.steps_done, self.steps)
            v.scalar_tensor_tensor(out, out, 1.0, z, ALU.add, ALU.mult).then_inc(self.steps_done, 1)
        self.steps += 1

        @self.block.vector
        def _(v):
            v.wait_ge(self.steps_done, self.steps)
            v.tensor_scalar(out, out, 2.0, None, ALU.mult).then_inc(self.steps_done, 1)
        self.steps += 1

    def softplus(self, x, out, t1, t2, t3):

        @self.block.scalar
        def _(s):
            s.wait_ge(self.steps_done, self.steps)
            s.activation(t1, x, ACT.Abs).then_inc(self.steps_done, 1)
        self.steps += 1

        @self.block.scalar
        def _(s):
            s.wait_ge(self.steps_done, self.steps)
            s.activation(t2, t1, ACT.Exp, scale=-1.0).then_inc(self.steps_done, 1)
        self.steps += 1
        self.log1p(t2, out, t1, t3)

        @self.block.vector
        def _(v):
            v.wait_ge(self.steps_done, self.steps)
            v.scalar_tensor_tensor(out, x, 0.0, out, ALU.max, ALU.add).then_inc(self.steps_done, 1)
        self.steps += 1


def cols(buf, offset, *dims):
    n = int(np.prod(dims))
    flat = buf[:, offset:offset + n]
    if len(dims) == 1:
        return flat
    names = "abcd"[:len(dims)]
    sizes = {names[i]: dims[i] for i in range(1, len(dims))}
    return flat.rearrange(f"p ({' '.join(names)}) -> p {' '.join(names)}", **sizes)


def column_chunks(w, first, width=BANK):
    w_v = w.rearrange("(k p) n -> p k n", p=P)
    return lambda i: [(None, w_v[:, :, bass.ds(i * width + first, width)])]


def make_constants(c):
    c.ident = c.sb("identity", [P, P])
    c.ones = c.sb("ones", [P, P])
    c.upto = c.sb("mask_row_upto_column", [P, P])
    c.onward = c.sb("mask_row_from_column_on", [P, P])
    c.after = c.sb("mask_row_after_column", [P, NT, SEQ])
    c.future = c.sb("minus_big_where_key_after_query", [P, NT, SEQ])

    @c.block.gpsimd
    def _(g):
        g.wait_ge(c.steps_done, c.steps)
        g.memset(c.ident[:, :], 0.0)
        g.memset(c.ones[:, :], 1.0)
        g.memset(c.upto[:, :], 1.0)
        g.memset(c.onward[:, :], 1.0)
        g.memset(c.after[:, :, :], 1.0)
        g.memset(c.future[:, :, :], 0.0).then_inc(c.steps_done, 1)
    c.steps += 1

    @c.block.gpsimd
    def _(g):
        g.wait_ge(c.steps_done, c.steps)
        g.affine_select(out=c.ident[:, :], in_=c.ident[:, :], compare_op=ALU.not_equal, fill=1.0, base=0,
                        pattern=[[-1, P]], channel_multiplier=1)
        g.affine_select(out=c.upto[:, :], in_=c.upto[:, :], compare_op=ALU.is_ge, fill=0.0, base=0,
                        pattern=[[1, P]], channel_multiplier=-1)
        g.affine_select(out=c.onward[:, :], in_=c.onward[:, :], compare_op=ALU.is_ge, fill=0.0, base=0,
                        pattern=[[-1, P]], channel_multiplier=1)
        g.affine_select(out=c.after[:, :, :], in_=c.after[:, :, :], compare_op=ALU.is_gt, fill=0.0, base=0,
                        pattern=[[P, NT], [-1, SEQ]], channel_multiplier=1)
        g.affine_select(out=c.future[:, :, :], in_=c.future[:, :, :], compare_op=ALU.is_ge, fill=-1e30,
                        base=0, pattern=[[P, NT], [-1, SEQ]], channel_multiplier=1).then_inc(c.steps_done, 1)
    c.steps += 1


def copy_halves(c, dst):
    def scalar(i, half, s):
        last = None
        for n in dst.scalar:
            last = s.activation(dst.place(i, n), dst.bank(half * 4 + n), ACT.Copy)
        return last

    def vector(i, half, v):
        last = None
        for n in dst.vector:
            last = v.tensor_copy(dst.place(i, n), dst.bank(half * 4 + n))
        return last
    return scalar, vector


class Copies:

    def __init__(self, c, place, banks, width=BANK):
        self.place = place
        self.scalar = [n for n in range(banks) if n % 2 == 0]
        self.vector = [n for n in range(banks) if n % 2 == 1]
        self.bank = lambda b: c.ps[:, b, 0:width]


def token_copies(c, dst, tiles, width=BANK):
    return copy_halves(c, Copies(c, lambda i, n: dst[:, tiles[n], bass.ds(i * width, width)], len(tiles), width))


def swiglu(c, x_t, w_gu, w_down, out):
    dff = w_down.shape[0]
    k_hidden = dff // P
    hidden = cols(c.z, 0, k_hidden, SEQ)
    act = cols(c.work, 0, 2, 2 * SEQ)
    w_v = w_gu.rearrange("(k p) n -> p k n", p=P)

    def source(i):
        return [((slice(0, KD), slice(0, 2 * P)), w_v[:, :, bass.ds(i * (2 * P), 2 * P)]),
                ((slice(0, KD), slice(2 * P, 4 * P)), w_v[:, :, bass.ds(i * (2 * P) + dff, 2 * P)])]

    def scalar(i, half, s):
        return s.activation(act[:, half, :], c.ps[:, half * 4, :], ACT.Silu)

    def vector(i, half, v):
        dst = hidden[:, bass.ds(i * 2, 2), :]
        return v.tensor_tensor(dst, act[:, half, :].rearrange("p (j t) -> p j t", t=SEQ),
                               c.ps[:, half * 4 + 1, :].rearrange("p (j t) -> p j t", t=SEQ), ALU.mult)
    c.gemm_feature_major(x_t, SEQ, dff // (2 * P), source, BANK, scalar, vector, after_scalar=True)
    c.gemm_rows(hidden, k_hidden, range(NT), w_down)
    c.take_rows(out, NT)


def add_normed(c, h, y, gain, scale):
    squared = [c.x_t[:, 2 * t:2 * t + 2, :].rearrange("p k n -> p (k n)") for t in range(NT)]
    c.rmsnorm([y[:, t, :] for t in range(NT)], [y[:, t, :] for t in range(NT)], gain, squared=squared)

    @c.block.vector
    def _(v):
        v.wait_ge(c.steps_done, c.steps)
        for t in range(NT):
            last = v.scalar_tensor_tensor(h[:, t, :], y[:, t, :], scale, h[:, t, :], ALU.mult, ALU.add)
        last.then_inc(c.steps_done, 1)
    c.steps += 1


def mlstm(c, qk_t, v_tok, o_tok, gates, out, gain):
    heads, dv = 4, 256
    scale = float(P) ** -0.5
    w = c.work
    r = cols(w, 2048, heads, NT, SEQ)
    di = cols(w, 4096, heads, NT, P)
    ld = cols(w, 5120, heads, SEQ)
    dm = cols(w, 6144, heads, SEQ)
    s_t = cols(w, 7168, heads, NT, P)
    sm = c.small
    lf, t1, t2, t3 = (cols(sm, 16 + 8 * n, NT, heads) for n in range(4))
    negf = cols(sm, 48, NT, heads)
    mx, den, em, rs = (cols(sm, 56 + 4 * n, heads) for n in range(4))
    stats = cols(sm, 72, heads, 6)
    mv = cols(sm, 96, heads, 2)

    @c.block.vector
    def _(v):
        v.wait_ge(c.steps_done, c.steps)
        v.tensor_scalar(negf, gates[:, :, 4:8], -1.0, None, ALU.mult).then_inc(c.steps_done, 1)
    c.steps += 1
    c.softplus(negf, lf, t1, t2, t3)

    @c.block.vector
    def _(v):
        v.wait_ge(c.steps_done, c.steps)
        v.tensor_scalar(lf, lf, -1.0, None, ALU.mult).then_inc(c.steps_done, 1)
    @c.block.scalar
    def _(s):
        s.wait_ge(c.steps_done, c.steps)
        s.activation(o_tok, o_tok, ACT.Sigmoid).then_inc(c.steps_done, 1)
    c.steps += 2

    @c.block.vector
    def _(v):
        v.wait_ge(c.steps_done, c.steps)
        for h in range(heads):
            for j in range(NT):
                v.tensor_scalar(r[:, h, j, :], c.after[:, j, :], lf[:, j, h:h + 1], None, ALU.mult)
                last = v.tensor_scalar(di[:, h, j, :], c.ident[:, :], gates[:, j, h:h + 1], None, ALU.mult)
        last.then_inc(c.steps_done, 1)
    c.steps += 1
    for t in range(NT):
        n = (t + 1) * P

        def bank(first, h, cut=n):
            return c.ps[:, first + h // 2, h % 2 * SEQ:h % 2 * SEQ + cut]

        def four(first, cut=n):
            return c.ps[:, first:first + 2, :].rearrange("p b (h s) -> p (b h) s", s=SEQ)[:, :, 0:cut]

        @c.block.tensor
        def _(pe):
            pe.wait_ge(c.steps_done, c.steps)
            for h in range(heads):
                for j in range(t + 1):
                    pe.matmul(bank(0, h), c.upto[:, :] if j == t else c.ones[:, :], r[:, h, j, 0:n],
                              start=(j == 0), stop=False)
                for j in range(t + 1):
                    pe.matmul(bank(0, h)[:, j * P:(j + 1) * P], c.ones[:, :], di[:, h, j, :],
                              start=False, stop=(j == t))
            for h in range(heads):
                last = pe.matmul(bank(2, h), qk_t[:, h, t * P:(t + 1) * P], qk_t[:, heads + h, 0:n],
                                 start=True, stop=True)
            last.then_inc(c.steps_done, 1)
        c.steps += 1

        @c.block.vector
        def _(v):
            v.wait_ge(c.steps_done, c.steps)
            v.tensor_tensor(
ld[:, :, 0:n], four(0), c.future[:, t:t + 1, 0:n].broadcast_to([P, heads, n]), ALU.add).then_inc(c.steps_done, 1)
        c.steps += 1

        @c.block.vector
        def _(v):
            v.wait_ge(c.steps_done, c.steps)
            v.reduce_max(mx, ld[:, :, 0:n], AX).then_inc(c.steps_done, 1)
        c.steps += 1

        @c.block.vector
        def _(v):
            v.wait_ge(c.steps_done, c.steps)
            v.tensor_scalar(mx, mx, -1.0, None, ALU.mult).then_inc(c.steps_done, 1)
        c.steps += 1

        @c.block.scalar
        def _(s):
            s.wait_ge(c.steps_done, c.steps)
            for h in range(heads):
                s.activation(dm[:, h, 0:n], ld[:, h, 0:n], ACT.Exp, bias=mx[:, h:h + 1])
            s.activation(em, mx, ACT.Exp).then_inc(c.steps_done, 1)
        c.steps += 1

        @c.block.vector
        def _(v):
            v.wait_ge(c.steps_done, c.steps)
            for h in range(heads):
                last = v.scalar_tensor_tensor(ld[:, h, 0:n], bank(2, h), scale, dm[:, h, 0:n],
                                              ALU.mult, ALU.mult, accum_out=den[:, h:h + 1])
            last.then_inc(c.steps_done, 1)
        c.steps += 1

        @c.block.scalar
        def _(s):
            s.wait_ge(c.steps_done, c.steps)
            s.activation(den, den, ACT.Abs).then_inc(c.steps_done, 1)
        c.steps += 1

        @c.block.vector
        def _(v):
            v.wait_ge(c.steps_done, c.steps)
            v.tensor_tensor(den, den, em, ALU.max).then_inc(c.steps_done, 1)
        c.steps += 1

        @c.block.vector
        def _(v):
            v.wait_ge(c.steps_done, c.steps)
            v.reciprocal(den, den).then_inc(c.steps_done, 1)
        c.steps += 1
        c.transposes([([ld[:, h, j * P:(j + 1) * P] for j in range(t + 1)], s_t[:, h, 0:t + 1, :])
                      for h in range(heads)])

        @c.block.tensor
        def _(pe):
            pe.wait_ge(c.steps_done, c.steps)
            for h in range(heads):
                for j in range(t + 1):
                    last = pe.matmul(bank(4, h, dv), s_t[:, h, j, :], v_tok[:, j, h * dv:(h + 1) * dv],
                                     start=(j == 0), stop=(j == t))
            last.then_inc(c.steps_done, 1)
        c.steps += 1
        y = out[:, t, :].rearrange("p (h d) -> p h d", d=dv)
        heads_layernorm(c, lambda h: bank(4, h, dv), [den[:, h:h + 1] for h in range(heads)],
                        [y[:, h, :] for h in range(heads)], stats, mv, rs)

        @c.block.vector
        def _(v):
            v.wait_ge(c.steps_done, c.steps)
            v.tensor_tensor(out[:, t, :], out[:, t, :], gain, ALU.mult).then_inc(c.steps_done, 1)
        c.steps += 1

        @c.block.vector
        def _(v):
            v.wait_ge(c.steps_done, c.steps)
            v.tensor_tensor(out[:, t, :], out[:, t, :], o_tok[:, t, :], ALU.mult).then_inc(c.steps_done, 1)
        c.steps += 1


def heads_layernorm(c, src, scales, dsts, stats, mv, rs, eps=EPS):
    n = len(dsts)
    if scales is not None:

        @c.block.vector
        def _(v):
            v.wait_ge(c.steps_done, c.steps)
            for h in range(n):
                last = v.tensor_scalar(dsts[h], src(h), scales[h], None, ALU.mult)
            last.then_inc(c.steps_done, 1)
        c.steps += 1
        src = lambda h: dsts[h]

    @c.block.vector
    def _(v):
        v.wait_ge(c.steps_done, c.steps)
        for h in range(n):
            last = v.bn_stats(stats[:, h, :], src(h))
        last.then_inc(c.steps_done, 1)
    c.steps += 1

    @c.block.vector
    def _(v):
        v.wait_ge(c.steps_done, c.steps)
        for h in range(n):
            last = v.bn_aggr(mv[:, h, :], stats[:, h, :])
        last.then_inc(c.steps_done, 1)
    c.steps += 1

    @c.block.vector
    def _(v):
        v.wait_ge(c.steps_done, c.steps)
        v.tensor_scalar(rs, mv[:, :, 1], eps, None, ALU.add).then_inc(c.steps_done, 1)
    c.steps += 1

    @c.block.scalar
    def _(s):
        s.wait_ge(c.steps_done, c.steps)
        s.activation(rs, rs, ACT.Sqrt).then_inc(c.steps_done, 1)
    c.steps += 1

    @c.block.vector
    def _(v):
        v.wait_ge(c.steps_done, c.steps)
        v.reciprocal(rs, rs).then_inc(c.steps_done, 1)
    c.steps += 1

    @c.block.vector
    def _(v):
        v.wait_ge(c.steps_done, c.steps)
        for h in range(n):
            last = v.tensor_scalar(dsts[h], src(h), mv[:, h, 0:1], rs[:, h:h + 1], ALU.subtract, ALU.mult)
        last.then_inc(c.steps_done, 1)
    c.steps += 1


def spatial_gating(c, us, out, w_t, bias, gain, shift):
    groups, dg = 4, 256
    u, v_tok = us[:, :, 0:D], us[:, :, D:2 * D]
    sm = c.small
    stats = cols(sm, 72, NT * groups, 6)
    mv = cols(sm, 120, NT * groups, 2)
    rs = cols(sm, 136, NT * groups)

    @c.block.scalar
    def _(s):
        s.wait_ge(c.steps_done, c.steps)
        s.activation(us, us, ACT.Gelu_apprx_tanh).then_inc(c.steps_done, 1)
    @c.block.gpsimd
    def _(g):
        g.wait_ge(c.steps_done, c.steps)
        g.affine_select(out=w_t, in_=w_t, compare_op=ALU.is_ge, fill=0.0, base=0,
                        pattern=[[0, groups], [1, P]], channel_multiplier=-1).then_inc(c.steps_done, 1)
    c.steps += 2
    pieces = [v_tok[:, t, g * dg:(g + 1) * dg] for t in range(NT) for g in range(groups)]
    heads_layernorm(c, lambda h: pieces[h], None, pieces, stats, mv, rs)

    @c.block.vector
    def _(v):
        v.wait_ge(c.steps_done, c.steps)
        v.tensor_tensor(v_tok, v_tok, gain.unsqueeze(1).broadcast_to([P, NT, D]), ALU.mult).then_inc(c.steps_done, 1)
    c.steps += 1

    @c.block.vector
    def _(v):
        v.wait_ge(c.steps_done, c.steps)
        v.tensor_tensor(v_tok, v_tok, shift.unsqueeze(1).broadcast_to([P, NT, D]), ALU.add).then_inc(c.steps_done, 1)
    c.steps += 1

    @c.block.tensor
    def _(pe):
        pe.wait_ge(c.steps_done, c.steps)
        for t in range(NT):
            for g in range(groups):
                last = pe.matmul(c.ps[:, t * 2 + g // 2, g % 2 * dg:(g % 2 + 1) * dg], w_t[:, g, :],
                                 v_tok[:, t, g * dg:(g + 1) * dg], start=True, stop=True)
        last.then_inc(c.steps_done, 1)
    c.steps += 1

    @c.block.vector
    def _(v):
        v.wait_ge(c.steps_done, c.steps)
        for t in range(NT):
            for g in range(groups):
                ch = slice(g * dg, (g + 1) * dg)
                last = v.scalar_tensor_tensor(out[:, t, ch], c.ps[:, t * 2 + g // 2, g % 2 * dg:(g % 2 + 1) * dg],
                                              bias[:, g:g + 1], u[:, t, ch], ALU.add, ALU.mult)
        last.then_inc(c.steps_done, 1)
    c.steps += 1


def memory_attention(c, q_t, k_t, v_tok, out):
    heads, dh = 4, 256
    scale = float(dh) ** -0.5
    p = cols(c.work, 0, heads, SEQ)
    p_t = cols(c.work, 1024, heads, NT, P)
    mx, total = cols(c.small, 56, heads), cols(c.small, 60, heads)
    for t in range(NT):
        def bank(first, h):
            return c.ps[:, first + h // 2, h % 2 * SEQ:(h % 2 + 1) * SEQ]

        @c.block.tensor
        def _(pe):
            pe.wait_ge(c.steps_done, c.steps)
            for h in range(heads):
                for j in range(2):
                    last = pe.matmul(bank(0, h), q_t[:, 2 * h + j, t * P:(t + 1) * P], k_t[:, 2 * h + j, :],
                                     start=(j == 0), stop=(j == 1))
            last.then_inc(c.steps_done, 1)
        c.steps += 1

        @c.block.vector
        def _(v):
            v.wait_ge(c.steps_done, c.steps)
            v.reduce_max(
mx, c.ps[:, 0:2, :].rearrange("p b (h s) -> p (b h) s", s=SEQ), AX).then_inc(c.steps_done, 1)
        c.steps += 1

        @c.block.vector
        def _(v):
            v.wait_ge(c.steps_done, c.steps)
            v.tensor_scalar(mx, mx, -scale, None, ALU.mult).then_inc(c.steps_done, 1)
        c.steps += 1

        @c.block.scalar
        def _(s):
            s.wait_ge(c.steps_done, c.steps)
            for h in range(heads):
                last = s.activation(p[:, h, :], bank(0, h), ACT.Exp, bias=mx[:, h:h + 1], scale=scale,
                                    accum_out=total[:, h:h + 1])
            last.then_inc(c.steps_done, 1)
        c.steps += 1

        @c.block.vector
        def _(v):
            v.wait_ge(c.steps_done, c.steps)
            v.reciprocal(total, total).then_inc(c.steps_done, 1)
        c.steps += 1
        c.transposes([([p[:, h, j * P:(j + 1) * P] for j in range(NT)], p_t[:, h, :, :]) for h in range(heads)])

        @c.block.tensor
        def _(pe):
            pe.wait_ge(c.steps_done, c.steps)
            for h in range(heads):
                for j in range(NT):
                    last = pe.matmul(bank(4, h), p_t[:, h, j, :], v_tok[:, j, h * dh:(h + 1) * dh],
                                     start=(j == 0), stop=(j == NT - 1))
            last.then_inc(c.steps_done, 1)
        c.steps += 1

        @c.block.vector
        def _(v):
            v.wait_ge(c.steps_done, c.steps)
            for h in range(heads):
                last = v.tensor_scalar(out[:, t, h * dh:(h + 1) * dh], bank(4, h), total[:, h:h + 1], None,
                                       ALU.mult)
            last.then_inc(c.steps_done, 1)
        c.steps += 1


def first_block(c, a):
    h, x_t = c.h, c.x_t
    h_tiles = [h[:, t, :] for t in range(NT)]
    y = cols(c.work, 9728, NT, D)
    y_tiles = [y[:, t, :] for t in range(NT)]
    gain = [c.par[:, n * D:(n + 1) * D] for n in range(4)]
    z = c.z

    for layer in range(DEPTH):
        g = a["norm_g"][layer]

        def feed_forward(which, n_in, n_out):
            c.load(gain[0], g[n_in, :].partition_broadcast(P))
            c.load(gain[1], g[n_out, :].partition_broadcast(P))
            c.loaded()
            c.rmsnorm(h_tiles, y_tiles, gain[0])
            c.to_feature_major(lambda t, k: y[:, t, k * P:(k + 1) * P], x_t, NT)
            swiglu(c, x_t, a["w_ffn_gu"][layer, which], a["w_ffn_down"][layer, which], y)
            add_normed(c, h, y, gain[1], 0.5)

        feed_forward(0, 0, 1)

        vo = cols(z, 0, NT, 2 * D)
        us = cols(z, 4096, NT, 2 * D)
        xq_t = cols(z, 8192, KD, SEQ)
        gates = cols(z, 10240, NT, 3 * D)
        qk_pad = cols(z, 16384, KD, 3 + SEQ)
        w_in = a["w_in"][layer]
        i_f = cols(c.small, 0, NT, 8)
        b_if = cols(c.small, 160, 8)
        conv_w = cols(c.small, 168, KD, 4)
        conv_b = cols(c.small, 200, KD)
        c.load(gain[0], g[2, :].partition_broadcast(P))
        c.load(gain[1], a["mlstm_norm_g"][layer, :].partition_broadcast(P))
        c.load(gain[2], a["sgu_ln_g"][layer, :].partition_broadcast(P))
        c.load(gain[3], a["sgu_ln_b"][layer, :].partition_broadcast(P))
        c.load(b_if[:, 0:4], a["b_i"][layer, :].partition_broadcast(P))
        c.load(b_if[:, 4:8], a["b_f"][layer, :].partition_broadcast(P))
        c.load(conv_w, a["conv_w"][layer])
        c.load(conv_b, a["conv_b"][layer])
        c.loaded()
        c.rmsnorm(h_tiles, y_tiles, gain[0])
        c.to_feature_major(lambda t, k: y[:, t, k * P:(k + 1) * P], x_t, NT)

        @c.block.vector
        def _(v):
            v.wait_ge(c.steps_done, c.steps)
            v.memset(qk_pad[:, :, 0:3], 0.0).then_inc(c.steps_done, 1)
        c.steps += 1

        def feature_copies(dst, first=0):
            def place(i, n):
                return dst[:, bass.ds(i * 4 + 2 * n, 2), first:first + SEQ]
            cp = Copies(c, place, 2)
            cp.bank = lambda b: c.ps[:, b, :].rearrange("p (j t) -> p j t", t=SEQ)
            return copy_halves(c, cp)
        c.gemm_feature_major(x_t, SEQ, 2, column_chunks(w_in, 0), BANK, *feature_copies(qk_pad, 3))
        c.gemm_token_major(x_t, range(NT), 4, column_chunks(w_in, D), BANK, *token_copies(c, vo, range(NT)))
        c.gemm_token_major(x_t, range(NT), 1, column_chunks(w_in, 3 * D, 8), 8,
                           *token_copies(c, i_f, range(NT), 8))
        c.gemm_token_major(x_t, range(NT), 4, column_chunks(w_in, 3 * D + 8), BANK,
                           *token_copies(c, us, range(NT)))
        c.gemm_feature_major(x_t, SEQ, 2, column_chunks(w_in, 5 * D + 8), BANK, *feature_copies(xq_t))
        c.gemm_token_major(x_t, range(NT), 6, column_chunks(w_in, 6 * D + 8), BANK,
                           *token_copies(c, gates, range(NT)))

        qk_t = cols(c.work, 0, KD, SEQ)
        for tap in range(4):

            @c.block.vector
            def _(v):
                v.wait_ge(c.steps_done, c.steps)
                for k in range(KD):
                    src, weight = qk_pad[:, k, tap:tap + SEQ], conv_w[:, k, tap:tap + 1]
                    if tap == 0:
                        last = v.tensor_scalar(qk_t[:, k, :], src, weight, None, ALU.mult)
                    else:
                        last = v.scalar_tensor_tensor(qk_t[:, k, :], src, weight, qk_t[:, k, :],
                                                      ALU.mult, ALU.add)
                last.then_inc(c.steps_done, 1)
            c.steps += 1

        @c.block.scalar
        def _(s):
            s.wait_ge(c.steps_done, c.steps)
            for k in range(KD):
                last = s.activation(qk_t[:, k, :], qk_t[:, k, :], ACT.Silu, bias=conv_b[:, k:k + 1])
            last.then_inc(c.steps_done, 1)
        @c.block.vector
        def _(v):
            v.wait_ge(c.steps_done, c.steps)
            v.tensor_tensor(
i_f, i_f, b_if.unsqueeze(1).broadcast_to([P, NT, 8]), ALU.add).then_inc(c.steps_done, 1)
        c.steps += 2

        @c.block.scalar
        def _(s):
            s.wait_ge(c.steps_done, c.steps)
            s.activation(gates, gates, ACT.Sigmoid).then_inc(c.steps_done, 1)
        c.steps += 1
        v_tok, o_tok = vo[:, :, 0:D], vo[:, :, D:2 * D]
        mlstm(c, qk_t, v_tok, o_tok, i_f, y, gain[1])
        merged = cols(c.work, 5632, NT, D)
        branch = cols(c.work, 7680, NT, D)

        def merge(which):
            c.to_feature_major(lambda t, k: y[:, t, k * P:(k + 1) * P], x_t, NT)
            dst = merged if which == 0 else branch
            c.gemm_token_major(x_t, range(NT), 2, column_chunks(a["w_branch"][layer, which], 0), BANK,
                               *token_copies(c, dst, range(NT)))

            @c.block.vector
            def _(v):
                v.wait_ge(c.steps_done, c.steps)
                v.tensor_tensor(dst, dst, gates[:, :, which * D:(which + 1) * D], ALU.mult).then_inc(c.steps_done, 1)
            c.steps += 1
            if which:

                @c.block.vector
                def _(v):
                    v.wait_ge(c.steps_done, c.steps)
                    v.tensor_tensor(merged, merged, branch, ALU.add).then_inc(c.steps_done, 1)
                c.steps += 1
        merge(0)

        w_t, bias = cols(c.work, 0, 4, P), cols(c.small, 144, 4)
        c.load(w_t, a["sgu_w_s"][layer])
        c.load(bias, a["sgu_b_s"][layer])
        c.load(gain[0], g[6, :].partition_broadcast(P))
        c.load(gain[1], g[3, :].partition_broadcast(P))
        c.loaded()
        spatial_gating(c, us, y, w_t, bias, gain[2], gain[3])
        merge(1)

        mem = cols(z, 0, NT, D)
        k_t = cols(z, 2048, KD, SEQ)
        v_mem = cols(z, 4096, NT, D)
        c.load(mem, a["mem"].rearrange("o (t p) d -> p (o t) d", p=P))
        c.loaded()
        mem_tiles = [mem[:, t, :] for t in range(NT)]
        c.rmsnorm(mem_tiles, y_tiles, gain[0])
        c.to_feature_major(lambda t, k: y[:, t, k * P:(k + 1) * P], x_t, NT)
        w_mkv = a["w_mkv"][layer]
        c.gemm_feature_major(x_t, SEQ, 2, column_chunks(w_mkv, 0), BANK, *feature_copies(k_t))
        c.gemm_token_major(x_t, range(NT), 2, column_chunks(w_mkv, D), BANK, *token_copies(c, v_mem, range(NT)))
        memory_attention(c, xq_t, k_t, v_mem, y)
        merge(2)
        c.to_feature_major(lambda t, k: merged[:, t, k * P:(k + 1) * P], x_t, NT)
        c.gemm_token_major(x_t, range(NT), 2, column_chunks(a["w_out"][layer], 0), BANK,
                           *token_copies(c, y, range(NT)))
        add_normed(c, h, y, gain[1], 1.0)
        feed_forward(1, 4, 5)


HEADS, HD = 8, 64
RW = HEADS * HD
HYB = 3328
Q_AT = 1792
SSD_G, SSD_HEADS, SSD_P = 8, 32, 64
D_IN = 2 * D
ROWS = 2 * NT
LEVELS = 7

LAYOUTS = {
    "conv_w": lambda w: w.reshape(DEPTH, 4, KD, P).transpose(0, 3, 2, 1),
    "conv_b": lambda b: b.reshape(DEPTH, KD, P).transpose(0, 2, 1),
    "sgu_w_s": lambda w: w.transpose(0, 3, 1, 2),
    "sgu_b_s": lambda b: b.transpose(0, 2, 1),
    "c_2": lambda v: v.reshape(KD, P).T,
    "c_ctx_2": lambda v: v.reshape(KD, P).T,
    "ssd_conv_w_2": lambda w: w.reshape(5, 32, P).transpose(2, 1, 0),
    "ssd_conv_b_2": lambda b: b.reshape(32, P).T,
    "rwkv_r_k_2": lambda v: v.reshape(1, RW),
}


def shape_constants():
    j, t = np.arange(P)[:, None], np.arange(P)[None, :]
    shift = 0.5 * (abs(j - t) == 1)
    from_next = 0.5 * ((j == 0) & (t == P - 1))
    from_before = 0.5 * ((j == P - 1) & (t == 0))
    mid = P // 2
    sum_forward = 1.0 * (j <= t) - 1.0 * (j < mid)
    sum_backward = 1.0 * (j >= t) - 1.0 * (j >= mid)
    strictly_before = 1.0 * (j < t)
    halves = 1.0 * ((t == 0) & (j < mid)) + 1.0 * ((t == 1) & (j >= mid))
    merges = [1.0 * ((j >> (n + 1) == t >> (n + 1)) & (j >> n != t >> n)) for n in range(LEVELS)]
    tok = np.arange(SEQ)
    inv = np.float32(10000.0) ** (-np.arange(0, 32, 2, dtype=np.float32) / np.float32(32))
    row = (tok // 64).astype(np.float32)[:, None] * inv
    col = (tok % 64).astype(np.float32)[:, None] * inv
    cos = np.concatenate([np.cos(row), np.cos(row), np.cos(col), np.cos(col)], 1)
    sin = np.concatenate([-np.sin(row), np.sin(row), -np.sin(col), np.sin(col)], 1)
    rope = np.stack([cos, sin], 1).reshape(NT, P, 2, HD).transpose(1, 0, 2, 3)
    return {
        "shifts": np.stack([shift, from_next, from_before], 1).astype(np.float32),
        "sums": np.stack([sum_forward, sum_backward, strictly_before, halves], 1).astype(np.float32),
        "sums_before": np.stack([sum_forward - (j == t), sum_backward - (j == t)], 1).astype(np.float32),
        "merges": np.stack(merges, 1).astype(np.float32),
        "rope": rope.astype(np.float32),
    }


def modulation(c, a, layer, first, count, dst, tiles):
    spread = c.x_t[:, :, 0:SEQ]
    cond = cols(c.small, 0, 2, KD)
    c.load(cond[:, 0, :], a["c_2"])
    c.load(cond[:, 1, :], a["c_ctx_2"])
    c.loaded()

    @c.block.scalar
    def _(s):
        s.wait_ge(c.steps_done, c.steps)
        s.activation(cond, cond, ACT.Silu).then_inc(c.steps_done, 1)
    c.steps += 1

    @c.block.vector
    def _(v):
        v.wait_ge(c.steps_done, c.steps)
        for n in range(2):
            last = v.tensor_copy(spread[:, :, n * P:(n + 1) * P], cond[:, n, :].unsqueeze(2).broadcast_to([P, KD, P]))
        last.then_inc(c.steps_done, 1)
    c.steps += 1
    c.gemm_token_major(spread, tiles, count, column_chunks(a["ada_w_2"][layer], first), BANK,
                       *token_copies(c, dst, tiles))


def tiles_of(x, n=NT):
    return [x[:, t, :] for t in range(n)]


def modulated_norm(c, x, out, gain, shift, scale):

    @c.block.vector
    def _(v):
        v.wait_ge(c.steps_done, c.steps)
        v.scalar_tensor_tensor(scale, scale, 1.0, gain, ALU.add, ALU.mult).then_inc(c.steps_done, 1)
    c.steps += 1
    c.rmsnorm(x, out, scale)

    @c.block.vector
    def _(v):
        v.wait_ge(c.steps_done, c.steps)
        for o in out:
            last = v.tensor_tensor(o, o, shift, ALU.add)
        last.then_inc(c.steps_done, 1)
    c.steps += 1


def heads_of(x, n=HEADS):
    if len(x.shape) == 2:
        return x.rearrange("p (h d) -> p h d", h=n)
    return x.rearrange("p t (h d) -> p t h d", h=n)


def rwkv(c, a, rows):
    ps, small, w, x_t = c.ps, c.small, c.work, cols_of(c.x_t)
    kk = cols(c.z, ROWS * HYB, ROWS, RW)
    y_all = cols(c.z, ROWS * HYB + 2048, ROWS, RW)
    low_t = cols(c.z, ROWS * HYB + 4096, ROWS, P)
    up = [cols(x_t, 3456, RW), cols(c.z, ROWS * HYB + 4608, RW)]
    merges = cols(x_t, 2560, LEVELS, P)
    state = cols(x_t, 1536, 2, HEADS, HD)[0:HD]
    inv_t = cols(x_t, 0, HEADS, P)
    u = cols(x_t, 1024, RW)
    sums_before = c.after[:, 1, :].rearrange("p (a t) -> p a t", t=P)
    sums = c.future[:, :, :].rearrange("p a (b t) -> p (a b) t", t=P)
    w0 = [c.par[:, n * RW:(n + 1) * RW] for n in range(2)]
    a0 = [c.par[:, (2 + n) * RW:(3 + n) * RW] for n in range(2)]
    k_k, k_a, r_k, g_up = (c.par[:, n * RW:(n + 1) * RW] for n in range(4, 8))

    n_mix = Q_AT
    quarter = n_mix // 4
    delta = cols(w, 0, ROWS, n_mix)
    mu = cols(w, ROWS * n_mix, n_mix)
    shifts = cols(w, ROWS * n_mix + n_mix, 3, P)
    c.load(mu, a["rwkv_mu_2"][0, :].partition_broadcast(P))
    c.load(shifts, a["shifts"])
    c.load(merges, a["merges"])
    c.load(sums, a["sums"])
    c.load(sums_before, a["sums_before"])
    for d in range(2):
        c.load(w0[d], a["rwkv_w0_2"][0, d, :].partition_broadcast(P))
        c.load(a0[d], a["rwkv_a0_2"][0, d, :].partition_broadcast(P))
        c.load(up[d][0:HD, :], a["rwkv_w_up_2"][0, d])
        c.load(up[d][HD:P, :], a["rwkv_a_up_2"][0, d])
    c.load(k_k, a["rwkv_k_k_2"][0, :].partition_broadcast(P))
    c.load(k_a, a["rwkv_k_a_2"][0, :].partition_broadcast(P))
    c.load(r_k, a["rwkv_r_k_2"][0, :].partition_broadcast(P))
    c.load(g_up, a["rwkv_g_up_2"][0])
    c.loaded()
    mixed = rows[:, :, 0:n_mix]
    for seq in range(2):

        @c.block.tensor
        def _(pe):
            pe.wait_ge(c.steps_done, c.steps)
            for t in range(NT):
                tile, other = seq * NT + t, seq * NT + 1 - t
                for q in range(4):
                    part = slice(q * quarter, (q + 1) * quarter)
                    out = ps[:, t * 4 + q, 0:quarter]
                    pe.matmul(out, shifts[:, 0, :], rows[:, tile, part], start=True, stop=False)
                    last = pe.matmul(out, shifts[:, 1 + t, :], rows[:, other, part], start=False, stop=True)
            last.then_inc(c.steps_done, 1)
        c.steps += 1

        @c.block.vector
        def _(v):
            v.wait_ge(c.steps_done, c.steps)
            for t in range(NT):
                tile = seq * NT + t
                out = delta[:, tile, :].rearrange("p (q n) -> p q n", q=4)
                last = v.tensor_tensor(out, ps[:, t * 4:t * 4 + 4, 0:quarter],
                                       rows[:, tile, 0:n_mix].rearrange("p (q n) -> p q n", q=4), ALU.subtract)
            last.then_inc(c.steps_done, 1)
        c.steps += 1

    @c.block.vector
    def _(v):
        v.wait_ge(c.steps_done, c.steps)
        v.tensor_tensor(delta, delta, mu.unsqueeze(1).broadcast_to([P, ROWS, n_mix]), ALU.mult).then_inc(c.steps_done, 1)
    c.steps += 1

    @c.block.vector
    def _(v):
        v.wait_ge(c.steps_done, c.steps)
        v.tensor_tensor(mixed, mixed, delta, ALU.add).then_inc(c.steps_done, 1)
    c.steps += 1
    r, k, v_tok = (rows[:, :, n * RW:(n + 1) * RW] for n in range(3))
    low = rows[:, :, 3 * RW:3 * RW + P]
    gd = rows[:, :, 3 * RW + P:3 * RW + 2 * P]

    square = cols(w, 0, ROWS, RW)
    ss = cols(small, 0, ROWS, HEADS)

    @c.block.vector
    def _(v):
        v.wait_ge(c.steps_done, c.steps)
        v.tensor_tensor(kk, k, k_k.unsqueeze(1).broadcast_to([P, ROWS, RW]), ALU.mult).then_inc(c.steps_done, 1)
    @c.block.scalar
    def _(s):
        s.wait_ge(c.steps_done, c.steps)
        s.activation(low[:, :, 0:HD], low[:, :, 0:HD], ACT.Tanh).then_inc(c.steps_done, 1)
    c.steps += 2

    @c.block.vector
    def _(v):
        v.wait_ge(c.steps_done, c.steps)
        v.tensor_tensor(square, kk, kk, ALU.mult).then_inc(c.steps_done, 1)
    c.steps += 1

    @c.block.vector
    def _(v):
        v.wait_ge(c.steps_done, c.steps)
        v.reduce_sum(ss, heads_of(square), AX).then_inc(c.steps_done, 1)
    c.steps += 1
    c.rstd(ss, 1.0, 1e-12)

    @c.block.vector
    def _(v):
        v.wait_ge(c.steps_done, c.steps)
        v.tensor_tensor(heads_of(kk), heads_of(kk),
                        ss.unsqueeze(3).broadcast_to([P, ROWS, HEADS, HD]), ALU.mult).then_inc(c.steps_done, 1)
    c.steps += 1
    c.transposes([([low[:, t, :] for t in range(ROWS)], low_t)])

    bonus = cols(small, 32, 2, ROWS, HEADS)
    ends = cols(small, 96, HEADS, 2)[0:HD]
    alpha, beta, kappa, rho = (cols(w, n * RW, RW) for n in range(4))
    alpha_t, beta_t, kappa_t, rho_t = (cols(w, 2048 + n * D, HEADS, P)[0:HD] for n in range(4))
    lower = cols(w, 6144, HEADS, P)
    g1_t, g2_t, g3_t = (cols(w, 7168 + n * D, HEADS, P) for n in range(3))
    inv = cols(w, 10240, HEADS, P)
    minus_gv = cols(w, 11264, RW)
    level = cols(w, 2048, HEADS, P)
    half = cols(w, 3072, HEADS, P)
    minus_w = cols(w, 4096, HEADS, P)[0:HD]

    def two_banks(first, parts=P):
        return ps[0:parts, first:first + 2, :].rearrange("p b (h t) -> p (b h) t", t=P)

    def over_heads(mask):
        return mask.unsqueeze(1).broadcast_to([P, HEADS, P])

    def by_head(first, lhs, rhs, pe, n=P, parts=P, start=True, stop=True):
        for h in range(HEADS):
            per = BANK // n
            out = ps[0:parts, first + h // per, h % per * n:(h % per + 1) * n]
            last = pe.matmul(out, lhs(h), rhs(h), start=start, stop=stop)
        return last

    def chunk(d, tile, first_of_scan, first_of_tile):
        strict, strict_t, incl_t = ((c.after[:, 0, 0:P], sums[:, 2, :], c.upto[:, :]) if d == 0 else
                                    (sums[:, 2, :], c.after[:, 0, 0:P], c.onward[:, :]))
        e_in, e_out, e_ex, lw = (cols(w, 7168 + n * RW, RW) for n in range(4))
        aa, kmod, t1 = (cols(w, 9216 + n * RW, RW) for n in range(3))
        v_t = v_tok[:, tile, :]

        @c.block.tensor
        def _(pe):
            pe.wait_ge(c.steps_done, c.steps)
            pe.matmul(ps[:, 0, :], low_t[0:HD, tile, :], up[d][0:HD, :], start=True, stop=True)
            pe.matmul(ps[:, 1, :], low_t[HD:P, tile, :], up[d][HD:P, :], start=True, stop=True).then_inc(c.steps_done, 1)
        c.steps += 1

        @c.block.vector
        def _(v):
            v.wait_ge(c.steps_done, c.steps)
            v.tensor_tensor(lw, ps[:, 0, :], w0[d], ALU.add)
            v.tensor_tensor(aa, ps[:, 1, :], a0[d], ALU.add).then_inc(c.steps_done, 1)
        c.steps += 1


        @c.block.scalar
        def _(s):
            s.wait_ge(c.steps_done, c.steps)
            s.activation(lw, lw, ACT.Sigmoid)
            s.activation(aa, aa, ACT.Sigmoid).then_inc(c.steps_done, 1)
        c.steps += 1

        @c.block.vector
        def _(v):
            v.wait_ge(c.steps_done, c.steps)
            v.tensor_scalar(lw, lw, -math.exp(-0.5), None, ALU.mult)
            v.tensor_tensor(beta, kk[:, tile, :], aa, ALU.mult)
            v.scalar_tensor_tensor(t1, aa, -1.0, k_a, ALU.add, ALU.mult).then_inc(c.steps_done, 1)
        c.steps += 1

        @c.block.tensor
        def _(pe):
            pe.wait_ge(c.steps_done, c.steps)
            pe.matmul(ps[:, 0, :], sums[:, d, :], lw, start=True, stop=True)
            pe.matmul(ps[:, 2, :], sums_before[:, d, :], lw, start=True, stop=True)
            for h in range(HEADS):
                last = pe.matmul(ps[0:HD, 1, 2 * h:2 * h + 2], lw[:, h * HD:(h + 1) * HD], sums[:, 3, 0:2],
                                 start=True, stop=True)
            last.then_inc(c.steps_done, 1)
        @c.block.vector
        def _(v):
            v.wait_ge(c.steps_done, c.steps)
            v.scalar_tensor_tensor(kmod, t1, 1.0, k[:, tile, :], ALU.add, ALU.mult).then_inc(c.steps_done, 1)
        c.steps += 2

        @c.block.scalar
        def _(s):
            s.wait_ge(c.steps_done, c.steps)
            s.activation(e_in, ps[:, 0, :], ACT.Exp)
            s.activation(e_out, ps[:, 0, :], ACT.Exp, scale=-1.0)
            s.activation(e_ex, ps[:, 2, :], ACT.Exp)
            s.activation(ends, ps[0:HD, 1, 0:2 * HEADS].rearrange("p (h e) -> p h e", e=2), ACT.Exp).then_inc(c.steps_done, 1)
        c.steps += 1

        @c.block.vector
        def _(v):
            v.wait_ge(c.steps_done, c.steps)
            v.tensor_tensor(alpha, kk[:, tile, :], e_ex, ALU.mult)
            v.tensor_tensor(beta, beta, e_out, ALU.mult)
            v.tensor_tensor(kappa, kmod, e_out, ALU.mult)
            v.tensor_tensor(rho, r[:, tile, :], e_in, ALU.mult)
            v.tensor_tensor(t1, kmod, r_k, ALU.mult).then_inc(c.steps_done, 1)
        c.steps += 1

        @c.block.vector
        def _(v):
            v.wait_ge(c.steps_done, c.steps)
            v.tensor_tensor(t1, t1, r[:, tile, :], ALU.mult).then_inc(c.steps_done, 1)
        c.steps += 1

        @c.block.vector
        def _(v):
            v.wait_ge(c.steps_done, c.steps)
            v.reduce_sum(bonus[:, d, tile, :], heads_of(t1), AX).then_inc(c.steps_done, 1)
        c.steps += 1
        c.transposes([([src[:, (q + j) * HD:(q + j + 1) * HD] for j in range(4)], dst[:, q:q + 4, :])
                      for src, dst in ((alpha, alpha_t), (beta, beta_t), (kappa, kappa_t), (rho, rho_t))
                      for q in (0, 4)])

        @c.block.tensor
        def _(pe):
            pe.wait_ge(c.steps_done, c.steps)
            by_head(0, lambda h: alpha_t[:, h, :], lambda h: beta_t[:, h, :], pe)
            by_head(2, lambda h: kappa_t[:, h, :], lambda h: alpha_t[:, h, :], pe)
            by_head(4, lambda h: beta_t[:, h, :], lambda h: rho_t[:, h, :], pe)
            by_head(6, lambda h: kappa_t[:, h, :], lambda h: rho_t[:, h, :], pe).then_inc(c.steps_done, 1)
        c.steps += 1

        @c.block.vector
        def _(v):
            v.wait_ge(c.steps_done, c.steps)
            v.tensor_tensor(lower, two_banks(0), over_heads(strict), ALU.mult)
            v.tensor_tensor(g1_t, two_banks(2), over_heads(strict_t), ALU.mult)
            v.tensor_tensor(g2_t, two_banks(4), over_heads(incl_t), ALU.mult)
            v.tensor_tensor(g3_t, two_banks(6), over_heads(incl_t), ALU.mult).then_inc(c.steps_done, 1)
        c.steps += 1


        @c.block.vector
        def _(v):
            v.wait_ge(c.steps_done, c.steps)
            v.tensor_tensor(level, lower, over_heads(merges[:, 0, :]), ALU.mult).then_inc(c.steps_done, 1)
        @c.block.tensor
        def _(pe):
            pe.wait_ge(c.steps_done, c.steps)
            by_head(4, lambda h: g1_t[:, h, :], lambda h: v_t[:, h * HD:(h + 1) * HD],
                    pe, n=HD).then_inc(c.steps_done, 1)
        c.steps += 2

        @c.block.tensor
        def _(pe):
            pe.wait_ge(c.steps_done, c.steps)
            by_head(0, lambda h: level[:, h, :], lambda h: c.ident[:, :], pe).then_inc(c.steps_done, 1)
        @c.block.vector
        def _(v):
            v.wait_ge(c.steps_done, c.steps)
            v.tensor_tensor(inv, over_heads(c.ident[:, :]), level, ALU.subtract).then_inc(c.steps_done, 1)
        @c.block.scalar
        def _(s):
            s.wait_ge(c.steps_done, c.steps)
            s.mul(minus_gv, ps[:, 4, :], -1.0).then_inc(c.steps_done, 1)
        c.steps += 3

        @c.block.vector
        def _(v):
            v.wait_ge(c.steps_done, c.steps)
            v.tensor_tensor(inv_t, over_heads(c.ident[:, :]), two_banks(0), ALU.subtract).then_inc(c.steps_done, 1)
        c.steps += 1
        for n in range(1, LEVELS):

            @c.block.vector
            def _(v):
                v.wait_ge(c.steps_done, c.steps)
                v.tensor_tensor(level, lower, over_heads(merges[:, n, :]), ALU.mult).then_inc(c.steps_done, 1)
            c.steps += 1

            @c.block.tensor
            def _(pe):
                pe.wait_ge(c.steps_done, c.steps)
                by_head(0, lambda h: level[:, h, :], lambda h: inv_t[:, h, :], pe).then_inc(c.steps_done, 1)
            c.steps += 1

            @c.block.scalar
            def _(s):
                s.wait_ge(c.steps_done, c.steps)
                s.activation(half, two_banks(0), ACT.Copy).then_inc(c.steps_done, 1)
            c.steps += 1

            @c.block.tensor
            def _(pe):
                pe.wait_ge(c.steps_done, c.steps)
                last = by_head(4, lambda h: inv[:, h, :], lambda h: half[:, h, :], pe)
                if n < LEVELS - 1:
                    last = by_head(2, lambda h: half[:, h, :], lambda h: inv[:, h, :], pe)
                last.then_inc(c.steps_done, 1)
            c.steps += 1

            @c.block.vector
            def _(v):
                v.wait_ge(c.steps_done, c.steps)
                last = v.tensor_tensor(inv_t, inv_t, two_banks(4), ALU.subtract)
                if n < LEVELS - 1:
                    last = v.tensor_tensor(inv, inv, two_banks(2), ALU.subtract)
                last.then_inc(c.steps_done, 1)
            c.steps += 1


        @c.block.tensor
        def _(pe):
            pe.wait_ge(c.steps_done, c.steps)
            by_head(0, lambda h: alpha[:, h * HD:(h + 1) * HD], lambda h: inv_t[:, h, :],
                    pe, parts=HD).then_inc(c.steps_done, 1)
        c.steps += 1

        @c.block.scalar
        def _(s):
            s.wait_ge(c.steps_done, c.steps)
            s.mul(minus_w, two_banks(0, HD), -1.0).then_inc(c.steps_done, 1)
        c.steps += 1

        before = state[:, d, :, :]
        starts, ending = ends[:, :, d:d + 1], ends[:, :, 1 - d:2 - d]
        if not first_of_scan:

            @c.block.vector
            def _(v):
                v.wait_ge(c.steps_done, c.steps)
                v.tensor_tensor(before, before, starts.broadcast_to([HD, HEADS, HD]), ALU.mult).then_inc(c.steps_done, 1)
            c.steps += 1

        @c.block.tensor
        def _(pe):
            pe.wait_ge(c.steps_done, c.steps)
            for h in range(HEADS):
                out, part = ps[:, 2, h * HD:(h + 1) * HD], slice(h * HD, (h + 1) * HD)
                last = pe.matmul(out, inv_t[:, h, :], minus_gv[:, part], start=True, stop=first_of_scan)
                if not first_of_scan:
                    last = pe.matmul(out, minus_w[:, h, :], before[:, h, :], start=False, stop=True)
            last.then_inc(c.steps_done, 1)
        c.steps += 1

        @c.block.scalar
        def _(s):
            s.wait_ge(c.steps_done, c.steps)
            s.activation(u, ps[:, 2, :], ACT.Copy).then_inc(c.steps_done, 1)
        c.steps += 1

        @c.block.tensor
        def _(pe):
            pe.wait_ge(c.steps_done, c.steps)
            for h in range(HEADS):
                part = slice(h * HD, (h + 1) * HD)
                out = ps[:, 3, part]
                if not first_of_scan:
                    pe.matmul(out, rho_t[:, h, :], before[:, h, :], start=True, stop=False)
                pe.matmul(out, g2_t[:, h, :], u[:, part], start=first_of_scan, stop=False)
                pe.matmul(out, g3_t[:, h, :], v_t[:, part], start=False, stop=True)
            for h in range(HEADS):
                part = slice(h * HD, (h + 1) * HD)
                out = ps[0:HD, 4, part]
                pe.matmul(out, beta[:, part], u[:, part], start=True, stop=False)
                last = pe.matmul(out, kappa[:, part], v_t[:, part], start=False, stop=True)
            last.then_inc(c.steps_done, 1)
        c.steps += 1
        gained = ps[0:HD, 4, :].rearrange("p (h d) -> p h d", d=HD)

        @c.block.vector
        def _(v):
            v.wait_ge(c.steps_done, c.steps)
            if first_of_tile:
                v.tensor_copy(y_all[:, tile, :], ps[:, 3, :])
            else:
                v.tensor_tensor(y_all[:, tile, :], y_all[:, tile, :], ps[:, 3, :], ALU.add)
            if first_of_scan:
                v.tensor_tensor(before, gained, ending.broadcast_to([HD, HEADS, HD]), ALU.mult).then_inc(c.steps_done, 1)
                return
            v.tensor_tensor(before, before, gained, ALU.add).then_inc(c.steps_done, 1)
        c.steps += 1
        if not first_of_scan:

            @c.block.vector
            def _(v):
                v.wait_ge(c.steps_done, c.steps)
                v.tensor_tensor(before, before, ending.broadcast_to([HD, HEADS, HD]), ALU.mult).then_inc(c.steps_done, 1)
            c.steps += 1

    for d, order in enumerate(((2, 3, 0, 1), (3, 2, 1, 0))):
        for n, tile in enumerate(order):
            chunk(d, tile, n == 0, d == 0)

    ln_w, ln_b = k_k, k_a
    c.load(ln_w, a["rwkv_ln_w_2"][0, :].partition_broadcast(P))
    c.load(ln_b, a["rwkv_ln_b_2"][0, :].partition_broadcast(P))
    c.loaded()
    y_h = heads_of(y_all)
    gd_t = cols(w, 2048, ROWS, P)

    def over_width(x):
        return x.unsqueeze(3).broadcast_to([P, ROWS, HEADS, HD])

    def over_rows(x):
        return x.unsqueeze(1).broadcast_to([P, ROWS, RW])

    @c.block.vector
    def _(v):
        v.wait_ge(c.steps_done, c.steps)
        v.reduce_sum(ss, y_h, AX).then_inc(c.steps_done, 1)
    @c.block.scalar
    def _(s):
        s.wait_ge(c.steps_done, c.steps)
        s.activation(gd, gd, ACT.Sigmoid).then_inc(c.steps_done, 1)
    c.steps += 2

    @c.block.vector
    def _(v):
        v.wait_ge(c.steps_done, c.steps)
        v.tensor_scalar(ss, ss, 1.0 / HD, None, ALU.mult).then_inc(c.steps_done, 1)
    c.steps += 1

    @c.block.vector
    def _(v):
        v.wait_ge(c.steps_done, c.steps)
        v.tensor_tensor(y_h, y_h, over_width(ss), ALU.subtract).then_inc(c.steps_done, 1)
    c.steps += 1

    @c.block.vector
    def _(v):
        v.wait_ge(c.steps_done, c.steps)
        v.tensor_tensor(square, y_all, y_all, ALU.mult).then_inc(c.steps_done, 1)
    c.steps += 1

    @c.block.vector
    def _(v):
        v.wait_ge(c.steps_done, c.steps)
        v.reduce_sum(ss, heads_of(square), AX).then_inc(c.steps_done, 1)
    c.steps += 1
    c.rstd(ss, 1.0 / HD, 64e-5)
    c.transposes([([gd[:, t, :] for t in range(ROWS)], gd_t)])

    @c.block.tensor
    def _(pe):
        pe.wait_ge(c.steps_done, c.steps)
        for t in range(ROWS):
            last = pe.matmul(ps[:, t, :], gd_t[:, t, :], g_up, start=True, stop=True)
        last.then_inc(c.steps_done, 1)
    @c.block.vector
    def _(v):
        v.wait_ge(c.steps_done, c.steps)
        v.tensor_tensor(y_h, y_h, over_width(ss), ALU.mult).then_inc(c.steps_done, 1)
    c.steps += 2

    @c.block.vector
    def _(v):
        v.wait_ge(c.steps_done, c.steps)
        v.tensor_tensor(y_all, y_all, over_rows(ln_w), ALU.mult).then_inc(c.steps_done, 1)
    c.steps += 1

    @c.block.vector
    def _(v):
        v.wait_ge(c.steps_done, c.steps)
        v.tensor_tensor(bonus[:, 0], bonus[:, 0], bonus[:, 1], ALU.add).then_inc(c.steps_done, 1)
    c.steps += 1

    @c.block.vector
    def _(v):
        v.wait_ge(c.steps_done, c.steps)
        v.tensor_scalar(bonus[:, 0], bonus[:, 0], 0.5, None, ALU.mult).then_inc(c.steps_done, 1)
    c.steps += 1

    @c.block.vector
    def _(v):
        v.wait_ge(c.steps_done, c.steps)
        v.tensor_tensor(y_all, y_all, over_rows(ln_b), ALU.add).then_inc(c.steps_done, 1)
    c.steps += 1

    @c.block.vector
    def _(v):
        v.wait_ge(c.steps_done, c.steps)
        v.tensor_tensor(heads_of(square), heads_of(v_tok), over_width(bonus[:, 0]), ALU.mult).then_inc(c.steps_done, 1)
    c.steps += 1

    @c.block.vector
    def _(v):
        v.wait_ge(c.steps_done, c.steps)
        v.tensor_tensor(y_all, y_all, square, ALU.add).then_inc(c.steps_done, 1)
    c.steps += 1

    @c.block.vector
    def _(v):
        v.wait_ge(c.steps_done, c.steps)
        v.tensor_tensor(y_all, y_all, ps[:, 0:ROWS, :], ALU.mult).then_inc(c.steps_done, 1)
    c.steps += 1
    return y_all


def cols_of(buf):
    return buf[:, :, :].rearrange("p a b -> p (a b)")


def differential_attention(c, a, rows):
    lam_init = 0.8 - 0.6 * math.exp(-0.3 * 0)
    scale = HD ** -0.5
    ps, small, w, x_t = c.ps, c.small, c.work, cols_of(c.x_t)
    q, k, v_tok = (rows[:, :, Q_AT + n * RW:Q_AT + (n + 1) * RW] for n in range(3))
    qr_t, qp_t, qc_t, kr_t, kc_t = (cols(w, n * 2048, HEADS, SEQ)[0:HD] for n in range(5))
    q_rot, k_rot, swapped = cols(x_t, 0, NT, RW), cols(x_t, 1024, NT, RW), cols(x_t, 2048, NT, RW)
    rope = cols(x_t, 3072, NT, 2, HD)
    lq = cols(small, 256, 4, HD)
    sub_g = cols(c.par, 0, P)
    for n, name in enumerate(("diff_lq1_2", "diff_lk1_2", "diff_lq2_2", "diff_lk2_2")):
        c.load(lq[:, n, :], a[name][0, :].partition_broadcast(P))
    c.load(rope, a["rope"])
    c.load(sub_g, a["diff_subln_g_2"][0, :].partition_broadcast(P))
    c.loaded()
    lam2 = cols(small, 0, 2)
    lam = cols(small, 2, 1)

    @c.block.vector
    def _(v):
        v.wait_ge(c.steps_done, c.steps)
        v.tensor_tensor(lq[:, 0:4:2, :], lq[:, 0:4:2, :], lq[:, 1:4:2, :], ALU.mult).then_inc(c.steps_done, 1)
    c.steps += 1

    @c.block.vector
    def _(v):
        v.wait_ge(c.steps_done, c.steps)
        v.reduce_sum(lam2, lq[:, 0:4:2, :], AX).then_inc(c.steps_done, 1)
    c.steps += 1

    @c.block.scalar
    def _(s):
        s.wait_ge(c.steps_done, c.steps)
        s.activation(lam2, lam2, ACT.Exp).then_inc(c.steps_done, 1)
    c.steps += 1

    @c.block.vector
    def _(v):
        v.wait_ge(c.steps_done, c.steps)
        v.tensor_tensor(lam, lam2[:, 0:1], lam2[:, 1:2], ALU.subtract).then_inc(c.steps_done, 1)
    c.steps += 1

    @c.block.vector
    def _(v):
        v.wait_ge(c.steps_done, c.steps)
        v.tensor_scalar(lam, lam, -1.0, -lam_init, ALU.mult, ALU.add).then_inc(c.steps_done, 1)
    c.steps += 1

    for src, dst in ((q, q_rot), (k, k_rot)):
        for t in range(NT):
            x = src[:, t, :].rearrange("p (b s i) -> p b s i", s=2, i=16)
            sw = swapped[:, t, :].rearrange("p (b s i) -> p b s i", s=2, i=16)
            cos = rope[:, t, 0:1, :].broadcast_to([P, HEADS, HD])
            sin = rope[:, t, 1:2, :].broadcast_to([P, HEADS, HD])
            x_h, d_h, s_h = heads_of(src[:, t, :]), heads_of(dst[:, t, :]), heads_of(swapped[:, t, :])

            @c.block.vector
            def _(v):
                v.wait_ge(c.steps_done, c.steps)
                v.tensor_copy(sw[:, :, 0, :], x[:, :, 1, :])
                v.tensor_copy(sw[:, :, 1, :], x[:, :, 0, :])
                v.tensor_tensor(d_h, x_h, cos, ALU.mult).then_inc(c.steps_done, 1)
            c.steps += 1

            @c.block.vector
            def _(v):
                v.wait_ge(c.steps_done, c.steps)
                v.tensor_tensor(s_h, s_h, sin, ALU.mult).then_inc(c.steps_done, 1)
            c.steps += 1

            @c.block.vector
            def _(v):
                v.wait_ge(c.steps_done, c.steps)
                v.tensor_tensor(dst[:, t, :], dst[:, t, :], swapped[:, t, :], ALU.add).then_inc(c.steps_done, 1)
            c.steps += 1

    c.transposes([([src(t)[:, (b + j) * HD:(b + j + 1) * HD] for j in range(4)],
                   dst[:, b:b + 4, t * P:(t + 1) * P])
                  for src, dst in ((lambda t: q_rot[:, t, :], qr_t), (lambda t: q[:, t, :], qp_t),
                                   (lambda t: q[:, NT + t, :], qc_t), (lambda t: k_rot[:, t, :], kr_t),
                                   (lambda t: k[:, NT + t, :], kc_t))
                  for t in range(NT) for b in (0, 4)])

    p_all = cols(x_t, 0, HEADS, 2 * SEQ)
    heads = HEADS // 2
    p_t = cols(c.z, ROWS * HYB, heads, ROWS, P)
    mx, total = cols(small, 8, HEADS), cols(small, 16, HEADS)
    mx2, total2 = mx, total
    for tile in range(ROWS):
        main = tile < NT
        tokens = slice(tile % NT * P, (tile % NT + 1) * P)
        keys = ROWS if main else NT
        n = keys * P
        first = 0 if main else NT

        @c.block.tensor
        def _(pe):
            pe.wait_ge(c.steps_done, c.steps)
            for b in range(HEADS):
                if main:
                    pe.matmul(ps[:, b, 0:SEQ], qr_t[:, b, tokens], kr_t[:, b, :], start=True, stop=True)
                    last = pe.matmul(ps[:, b, SEQ:2 * SEQ], qp_t[:, b, tokens], kc_t[:, b, :],
                                     start=True, stop=True)
                else:
                    last = pe.matmul(ps[:, b, 0:SEQ], qc_t[:, b, tokens], kc_t[:, b, :], start=True, stop=True)
            last.then_inc(c.steps_done, 1)
        c.steps += 1

        @c.block.vector
        def _(v):
            v.wait_ge(c.steps_done, c.steps)
            v.reduce_max(mx, ps[:, :, 0:n], AX).then_inc(c.steps_done, 1)
        c.steps += 1

        @c.block.vector
        def _(v):
            v.wait_ge(c.steps_done, c.steps)
            v.tensor_scalar(mx, mx, -scale, None, ALU.mult).then_inc(c.steps_done, 1)
        c.steps += 1

        @c.block.scalar
        def _(s):
            s.wait_ge(c.steps_done, c.steps)
            for b in range(HEADS):
                last = s.activation(p_all[:, b, 0:n], ps[:, b, 0:n], ACT.Exp, bias=mx[:, b:b + 1], scale=scale,
                                    accum_out=total[:, b:b + 1])
            last.then_inc(c.steps_done, 1)
        c.steps += 1

        @c.block.vector
        def _(v):
            v.wait_ge(c.steps_done, c.steps)
            v.reciprocal(total, total).then_inc(c.steps_done, 1)
        c.steps += 1
        pairs = total.rearrange("p (h m) -> p h m", m=2)

        @c.block.vector
        def _(v):
            v.wait_ge(c.steps_done, c.steps)
            v.tensor_scalar(pairs[:, :, 1], pairs[:, :, 1], lam, None, ALU.mult).then_inc(c.steps_done, 1)
        c.steps += 1

        @c.block.vector
        def _(v):
            v.wait_ge(c.steps_done, c.steps)
            for h in range(heads):
                last = v.tensor_scalar(p_all[:, 2 * h, 0:n], p_all[:, 2 * h, 0:n], total[:, 2 * h:2 * h + 1],
                                       None, ALU.mult)
            last.then_inc(c.steps_done, 1)
        c.steps += 1

        @c.block.vector
        def _(v):
            v.wait_ge(c.steps_done, c.steps)
            for h in range(heads):
                last = v.scalar_tensor_tensor(p_all[:, 2 * h, 0:n], p_all[:, 2 * h + 1, 0:n],
                                              total[:, 2 * h + 1:2 * h + 2], p_all[:, 2 * h, 0:n],
                                              ALU.mult, ALU.add)
            last.then_inc(c.steps_done, 1)
        c.steps += 1
        c.transposes([([p_all[:, 2 * h, j * P:(j + 1) * P] for j in range(keys)], p_t[:, h, 0:keys, :])
                      for h in range(heads)])

        @c.block.tensor
        def _(pe):
            pe.wait_ge(c.steps_done, c.steps)
            for h in range(heads):
                for j in range(keys):
                    last = pe.matmul(ps[:, 4, h * P:(h + 1) * P], p_t[:, h, j, :],
                                     v_tok[:, first + j, h * P:(h + 1) * P], start=(j == 0), stop=(j == keys - 1))
            last.then_inc(c.steps_done, 1)
        c.steps += 1

        @c.block.vector
        def _(v):
            v.wait_ge(c.steps_done, c.steps)
            v.tensor_copy(q[:, tile, :], ps[:, 4, :]).then_inc(c.steps_done, 1)
        c.steps += 1

    square = cols(w, 0, ROWS, RW)
    ss = cols(small, 32, ROWS, heads)
    q_h = heads_of(q, heads)

    @c.block.vector
    def _(v):
        v.wait_ge(c.steps_done, c.steps)
        v.tensor_tensor(square, q, q, ALU.mult).then_inc(c.steps_done, 1)
    c.steps += 1

    @c.block.vector
    def _(v):
        v.wait_ge(c.steps_done, c.steps)
        v.reduce_sum(ss, heads_of(square, heads), AX).then_inc(c.steps_done, 1)
    c.steps += 1
    c.rstd(ss, 1.0 / P, EPS)

    @c.block.vector
    def _(v):
        v.wait_ge(c.steps_done, c.steps)
        v.tensor_scalar(ss, ss, 1.0 - lam_init, None, ALU.mult).then_inc(c.steps_done, 1)
    c.steps += 1

    @c.block.vector
    def _(v):
        v.wait_ge(c.steps_done, c.steps)
        v.tensor_tensor(q_h, q_h, ss.unsqueeze(3).broadcast_to([P, ROWS, heads, P]), ALU.mult).then_inc(c.steps_done, 1)
    c.steps += 1
    for t in range(ROWS):

        @c.block.vector
        def _(v):
            v.wait_ge(c.steps_done, c.steps)
            v.tensor_tensor(q_h[:, t], q_h[:, t], sub_g.unsqueeze(1).broadcast_to([P, heads, P]),
                            ALU.mult).then_inc(c.steps_done, 1)
        c.steps += 1
    return q


def hybrid_mixer(c, a, out):
    rows = cols(c.z, 0, ROWS, HYB)
    c.gemm_token_major(c.x_t, range(ROWS), 6, column_chunks(a["hy_w_in_2"][0], 0), BANK,
                       *token_copies(c, rows, range(ROWS)))
    n = HYB - 6 * BANK
    c.gemm_token_major(c.x_t, range(ROWS), 1, column_chunks(a["hy_w_in_2"][0], 6 * BANK, n), n,
                       *token_copies(c, rows[:, :, 6 * BANK:], range(ROWS), n))
    y = rwkv(c, a, rows)
    o = differential_attention(c, a, rows)
    c.to_feature_major(lambda t, k: y[:, t, k * P:(k + 1) * P] if k < 4 else o[:, t, (k - 4) * P:(k - 3) * P],
                       c.x_t, ROWS)
    c.gemm_token_major(c.x_t, range(ROWS), 2, column_chunks(a["hy_w_out_2"][0], 0), BANK,
                       *token_copies(c, out, range(ROWS)))


def ssd_mixer(c, a, out):
    ps, small, w = c.ps, c.small, c.work
    x_t = c.x_t
    xs = cols(c.z, 0, ROWS, D_IN)
    b_tok = cols(c.z, 8192, ROWS, D)
    b_t = cols(c.z, 12288, SSD_G, SEQ)
    c_t = cols(c.z, 14336, SSD_G, SEQ)
    z = cols(w, 0, NT, D_IN)
    pad = cols(w, 4096, 4, 2, SEQ + 4)
    conv = cols(w, 6176, 4, 2, SEQ)
    w_in = a["ssd_w_in_2"][0]
    taps = cols(c.par, 0, 32, 5)
    conv_b = cols(c.par, 160, 32)
    dt_bias = cols(c.par, 192, 2, SSD_HEADS)
    decay_rate = cols(c.par, 256, 2, SSD_HEADS)
    d_skip = cols(c.par, 320, SSD_HEADS)
    dt_raw = cols(small, 0, ROWS, SSD_HEADS)
    c.load(taps, a["ssd_conv_w_2"])
    c.load(conv_b, a["ssd_conv_b_2"])
    for d in range(2):
        c.load(dt_bias[:, d, :], a["ssd_dt_bias_2"][0, d, :].partition_broadcast(P))
        c.load(decay_rate[:, d, :], a["ssd_a_log_2"][0, d, :].partition_broadcast(P))
    c.load(d_skip, a["ssd_d_2"][0, :].partition_broadcast(P))
    c.loaded()

    @c.block.vector
    def _(v):
        v.wait_ge(c.steps_done, c.steps)
        v.memset(pad, 0.0).then_inc(c.steps_done, 1)
    c.steps += 1
    for i in range(8):
        seqs = 2 if i < 6 else 1
        tokens = seqs * SEQ
        per_bank = BANK // tokens

        def place(_, n):
            return pad[:, n * per_bank:(n + 1) * per_bank, 0:seqs, 2:2 + SEQ]
        cp = Copies(c, place, 4 // per_bank)
        cp.bank = lambda b: ps[:, b, :].rearrange("p (g s t) -> p g s t", g=per_bank, s=seqs)
        c.gemm_feature_major(x_t, tokens, 1, column_chunks(w_in, D_IN + i * BANK), BANK, *copy_halves(c, cp))
        for tap in range(5):

            @c.block.vector
            def _(v):
                v.wait_ge(c.steps_done, c.steps)
                for g in range(4):
                    src, weight = pad[:, g, 0:seqs, tap:tap + SEQ], taps[:, i * 4 + g, tap:tap + 1]
                    dst = conv[:, g, 0:seqs, :]
                    if tap == 0:
                        last = v.tensor_scalar(dst, src, weight, None, ALU.mult)
                    else:
                        last = v.scalar_tensor_tensor(dst, src, weight, dst, ALU.mult, ALU.add)
                last.then_inc(c.steps_done, 1)
            c.steps += 1

        @c.block.scalar
        def _(s):
            s.wait_ge(c.steps_done, c.steps)
            for g in range(4):
                ch = i * 4 + g
                dst = conv[:, g, 0:seqs, :] if i < 6 else c_t[:, (i - 6) * 4 + g, :].unsqueeze(1)
                last = s.activation(dst, conv[:, g, 0:seqs, :], ACT.Silu, bias=conv_b[:, ch:ch + 1])
            last.then_inc(c.steps_done, 1)
        c.steps += 1
        if i in (4, 5):

            @c.block.vector
            def _(v):
                v.wait_ge(c.steps_done, c.steps)
                v.tensor_copy(b_t[:, (i - 4) * 4:(i - 3) * 4, :], conv[:, :, 0, :]).then_inc(c.steps_done, 1)
            c.steps += 1
        if i < 6:
            dst, at = (xs, i * BANK) if i < 4 else (b_tok, (i - 4) * BANK)
            c.transposes([([conv[:, g, t // NT, t % NT * P:(t % NT + 1) * P] for g in range(4)],
                           dst[:, t, at:at + BANK].rearrange("p (g n) -> p g n", g=4)) for t in range(ROWS)])
    c.gemm_token_major(x_t, range(ROWS), 1, column_chunks(w_in, 6144, SSD_HEADS), SSD_HEADS,
                       *token_copies(c, dt_raw, range(ROWS), SSD_HEADS))
    c.gemm_token_major(x_t, range(NT), 4, column_chunks(w_in, 0), BANK, *token_copies(c, z, range(NT)))
    y = cols(w, 4096, NT, D_IN)
    state = cols(w, 8192, SSD_HEADS, SSD_P)
    cb = cols(w, 10240, SSD_G, P)
    free = cols_of(c.x_t)
    xdt, xw = cols(free, 0, SSD_HEADS, SSD_P), cols(free, 2048, SSD_HEADS, SSD_P)
    seg_l = cols(c.par, 1024, 8, P)
    seg_e = cols(c.par, 2048, 8, P)
    dt = cols(small, 128, ROWS, SSD_HEADS)
    dta = cols(small, 256, ROWS, SSD_HEADS)
    ex = cols(small, 384, 3, SSD_HEADS)
    before = cols_of(c.future)[:, 2 * P:3 * P]
    t1, t2, t3 = (cols(c.par, 3072 + n * P, ROWS, SSD_HEADS) for n in range(3))
    raw = cols(c.par, 3072 + 3 * P, ROWS, SSD_HEADS)

    def over_width(x):
        return x.unsqueeze(2).broadcast_to([P, SSD_HEADS, SSD_P])

    def as_heads(x):
        return x.rearrange("p (h d) -> p h d", d=SSD_P)

    def four_banks(first):
        return ps[:, first:first + 4, :].rearrange("p b (h d) -> p (b h) d", d=SSD_P)

    @c.block.scalar
    def _(s):
        s.wait_ge(c.steps_done, c.steps)
        s.activation(z, z, ACT.Silu).then_inc(c.steps_done, 1)
    c.steps += 1

    @c.block.scalar
    def _(s):
        s.wait_ge(c.steps_done, c.steps)
        s.activation(decay_rate, decay_rate, ACT.Exp).then_inc(c.steps_done, 1)
    c.steps += 1

    @c.block.vector
    def _(v):
        v.wait_ge(c.steps_done, c.steps)
        v.tensor_scalar(decay_rate, decay_rate, -1.0, None, ALU.mult).then_inc(c.steps_done, 1)
    c.steps += 1

    @c.block.vector
    def _(v):
        v.wait_ge(c.steps_done, c.steps)
        for t in range(NT):
            last = v.tensor_tensor(as_heads(y[:, t, :]), as_heads(xs[:, t, :]), over_width(d_skip), ALU.mult)
        last.then_inc(c.steps_done, 1)
    c.steps += 1

    for d, order in enumerate(((2, 3, 0, 1), (3, 2, 1, 0))):
        after, incl = (c.after[:, 0, 0:P], c.upto[:, :]) if d == 0 else (before, c.onward[:, :])

        @c.block.vector
        def _(v):
            v.wait_ge(c.steps_done, c.steps)
            v.tensor_tensor(
raw, dt_raw, dt_bias[:, d:d + 1, :].broadcast_to([P, ROWS, SSD_HEADS]), ALU.add).then_inc(c.steps_done, 1)
        c.steps += 1
        c.softplus(raw, dt, t1, t2, t3)

        @c.block.vector
        def _(v):
            v.wait_ge(c.steps_done, c.steps)
            v.tensor_tensor(
dta, dt, decay_rate[:, d:d + 1, :].broadcast_to([P, ROWS, SSD_HEADS]), ALU.mult).then_inc(c.steps_done, 1)
        c.steps += 1
        for n, tile in enumerate(order):
            x_h = as_heads(xs[:, tile, :])

            @c.block.tensor
            def _(pe):
                pe.wait_ge(c.steps_done, c.steps)
                pe.matmul(ps[:, 0, 0:SSD_HEADS], after, dta[:, tile, :], start=True, stop=True)
                pe.matmul(ps[:, 0, SSD_HEADS:2 * SSD_HEADS], incl, dta[:, tile, :], start=True, stop=True)
                pe.matmul(ps[:, 0, 2 * SSD_HEADS:3 * SSD_HEADS], c.ones[:, :], dta[:, tile, :],
                          start=True, stop=True).then_inc(c.steps_done, 1)
            @c.block.vector
            def _(v):
                v.wait_ge(c.steps_done, c.steps)
                v.tensor_tensor(xdt, x_h, over_width(dt[:, tile, :]), ALU.mult).then_inc(c.steps_done, 1)
            c.steps += 2

            @c.block.scalar
            def _(s):
                s.wait_ge(c.steps_done, c.steps)
                s.activation(
ex, ps[:, 0, 0:3 * SSD_HEADS].rearrange("p (k h) -> p k h", k=3), ACT.Exp).then_inc(c.steps_done, 1)
            c.steps += 1

            @c.block.vector
            def _(v):
                v.wait_ge(c.steps_done, c.steps)
                v.tensor_tensor(xw, xdt, over_width(ex[:, 0, :]), ALU.mult).then_inc(c.steps_done, 1)
            c.steps += 1
            if tile < NT:
                y_h = as_heads(y[:, tile, :])
                tokens = slice(tile * P, (tile + 1) * P)

                @c.block.tensor
                def _(pe):
                    pe.wait_ge(c.steps_done, c.steps)
                    for g in range(SSD_G):
                        pe.matmul(ps[:, 4 + g // 4, g % 4 * P:(g % 4 + 1) * P], b_t[:, g, tokens],
                                  c_t[:, g, tokens], start=True, stop=True)
                    for g in range(SSD_G):
                        last = pe.matmul(ps[:, g // 2, g % 2 * SEQ:(g % 2 + 1) * SEQ], c_t[:, g, tokens],
                                         state[:, g * 4:(g + 1) * 4, :].rearrange("p h d -> p (h d)"),
                                         start=True, stop=True)
                    last.then_inc(c.steps_done, 1)
                c.steps += 1

                @c.block.vector
                def _(v):
                    v.wait_ge(c.steps_done, c.steps)
                    v.tensor_tensor(
cb, ps[:, 4:6, :].rearrange("p b (g l) -> p (b g) l", l=P),
incl.unsqueeze(1).broadcast_to([P, SSD_G, P]), ALU.mult).then_inc(c.steps_done, 1)
                c.steps += 1
                off = cols(c.par, 1024, SSD_HEADS, SSD_P)

                @c.block.vector
                def _(v):
                    v.wait_ge(c.steps_done, c.steps)
                    v.tensor_tensor(off, four_banks(0), over_width(ex[:, 1, :]), ALU.mult).then_inc(c.steps_done, 1)
                c.steps += 1

                @c.block.vector
                def _(v):
                    v.wait_ge(c.steps_done, c.steps)
                    v.tensor_tensor(y_h, y_h, off, ALU.add).then_inc(c.steps_done, 1)
                c.steps += 1
                for part in range(4):
                    heads = slice(part * 8, part * 8 + 8)

                    @c.block.vector
                    def _(v):
                        v.wait_ge(c.steps_done, c.steps)
                        v.tensor_tensor(
    seg_l, after.unsqueeze(1).broadcast_to([P, 8, P]),
    dta[:, tile, heads].unsqueeze(2).broadcast_to([P, 8, P]), ALU.mult).then_inc(c.steps_done, 1)
                    c.steps += 1

                    @c.block.tensor
                    def _(pe):
                        pe.wait_ge(c.steps_done, c.steps)
                        for h in range(8):
                            last = pe.matmul(ps[:, 4 + h // 4, h % 4 * P:(h % 4 + 1) * P], seg_l[:, h, :], incl,
                                             start=True, stop=True)
                        last.then_inc(c.steps_done, 1)
                    c.steps += 1

                    @c.block.scalar
                    def _(s):
                        s.wait_ge(c.steps_done, c.steps)
                        s.activation(
    seg_e, ps[:, 4:6, :].rearrange("p b (h l) -> p (b h) l", l=P), ACT.Exp).then_inc(c.steps_done, 1)
                    c.steps += 1

                    @c.block.vector
                    def _(v):
                        v.wait_ge(c.steps_done, c.steps)
                        v.tensor_tensor(
    seg_e.rearrange("p (g h) l -> p g h l", g=2), seg_e.rearrange("p (g h) l -> p g h l", g=2),
    cb[:, 2 * part:2 * part + 2, :].unsqueeze(2).broadcast_to([P, 2, 4, P]), ALU.mult).then_inc(c.steps_done, 1)
                    c.steps += 1

                    @c.block.tensor
                    def _(pe):
                        pe.wait_ge(c.steps_done, c.steps)
                        for h in range(8):
                            last = pe.matmul(ps[:, part, h * SSD_P:(h + 1) * SSD_P], seg_e[:, h, :],
                                             xdt[:, part * 8 + h, :], start=True, stop=True)
                        last.then_inc(c.steps_done, 1)
                    c.steps += 1

                @c.block.vector
                def _(v):
                    v.wait_ge(c.steps_done, c.steps)
                    v.tensor_tensor(y_h, y_h, four_banks(0), ALU.add).then_inc(c.steps_done, 1)
                c.steps += 1
            if n < len(order) - 1:

                @c.block.tensor
                def _(pe):
                    pe.wait_ge(c.steps_done, c.steps)
                    for g in range(SSD_G):
                        last = pe.matmul(ps[:, g // 2, g % 2 * SEQ:(g % 2 + 1) * SEQ],
                                         b_tok[:, tile, g * P:(g + 1) * P],
                                         xw[:, g * 4:(g + 1) * 4, :].rearrange("p h d -> p (h d)"),
                                         start=True, stop=True)
                    last.then_inc(c.steps_done, 1)
                c.steps += 1
                if n == 0:

                    @c.block.vector
                    def _(v):
                        v.wait_ge(c.steps_done, c.steps)
                        v.tensor_copy(state, four_banks(0)).then_inc(c.steps_done, 1)
                    c.steps += 1
                else:

                    @c.block.vector
                    def _(v):
                        v.wait_ge(c.steps_done, c.steps)
                        v.tensor_tensor(state, state, over_width(ex[:, 2, :]), ALU.mult).then_inc(c.steps_done, 1)
                    c.steps += 1

                    @c.block.vector
                    def _(v):
                        v.wait_ge(c.steps_done, c.steps)
                        v.tensor_tensor(state, state, four_banks(0), ALU.add).then_inc(c.steps_done, 1)
                    c.steps += 1

    gain = cols(c.par, 1024, D_IN)
    c.load(gain, a["ssd_norm_g_2"][0, :].partition_broadcast(P))
    c.loaded()
    ss = cols(small, 0, NT, SSD_G)
    square = cols(free, 0, NT, D_IN)
    y_g = y.rearrange("p t (g d) -> p t g d", g=SSD_G)

    @c.block.vector
    def _(v):
        v.wait_ge(c.steps_done, c.steps)
        v.tensor_tensor(y, y, z, ALU.mult).then_inc(c.steps_done, 1)
    c.steps += 1

    @c.block.vector
    def _(v):
        v.wait_ge(c.steps_done, c.steps)
        v.tensor_tensor(square, y, y, ALU.mult).then_inc(c.steps_done, 1)
    c.steps += 1

    @c.block.vector
    def _(v):
        v.wait_ge(c.steps_done, c.steps)
        v.reduce_sum(ss, square.rearrange("p t (g d) -> p t g d", g=SSD_G), AX).then_inc(c.steps_done, 1)
    c.steps += 1
    c.rstd(ss, 1.0 / 256, EPS)

    @c.block.vector
    def _(v):
        v.wait_ge(c.steps_done, c.steps)
        v.tensor_tensor(y_g, y_g, ss.unsqueeze(3).broadcast_to([P, NT, SSD_G, 256]), ALU.mult).then_inc(c.steps_done, 1)
    c.steps += 1

    @c.block.vector
    def _(v):
        v.wait_ge(c.steps_done, c.steps)
        v.tensor_tensor(y, y, gain.unsqueeze(1).broadcast_to([P, NT, D_IN]), ALU.mult).then_inc(c.steps_done, 1)
    c.steps += 1
    wide = cols(free, 0, D_IN // P, SEQ)
    c.to_feature_major(lambda t, k: y[:, t, k * P:(k + 1) * P], wide, NT, kd=D_IN // P)
    c.gemm_rows(wide, D_IN // P, range(NT), a["ssd_w_out_2"][0])
    c.take_rows(out, NT)


def second_block(c, a):
    y4 = cols(c.work, 7680, ROWS, D)
    gain = [c.par[:, n * D:(n + 1) * D] for n in range(4)]
    for layer in range(DEPTH):
        last_layer = layer == DEPTH - 1
        mods = cols(c.z, 0, 2, 2 * D)
        modulation(c, a, layer, 0, 4, mods, range(2))
        c.load(c.par[:, 0:2 * D], a["ada_b_2"][layer, 0:2 * D].partition_broadcast(P))
        c.load(gain[2], a["norm1_g_2"][layer, :].partition_broadcast(P))
        c.loaded()

        @c.block.vector
        def _(v):
            v.wait_ge(c.steps_done, c.steps)
            v.tensor_tensor(mods, mods, c.par[:, 0:2 * D].unsqueeze(1).broadcast_to(
[P, 2, 2 * D]), ALU.add).then_inc(c.steps_done, 1)
        c.steps += 1
        for n, x in enumerate((c.h, c.hc)):
            modulated_norm(c, tiles_of(x), tiles_of(y4[:, NT * n:NT * n + NT, :]), gain[2],
                           mods[:, n, 0:D], mods[:, n, D:2 * D])
        c.to_feature_major(lambda t, k: y4[:, t, k * P:(k + 1) * P], c.x_t, ROWS)
        if layer % 2 == 0:
            mixed = cols(c.work, 0, ROWS, D)
            hybrid_mixer(c, a, mixed)
        else:
            mixed = cols(c.work, 0, NT, D)
            ssd_mixer(c, a, mixed)

        seqs = 1 if last_layer else 2
        mods = cols(c.z, 0, 2, 3 * D)
        mod5 = cols(c.z, 16384, 2, D)
        modulation(c, a, layer, 2 * D, 6, mods, range(seqs))
        modulation(c, a, layer, 5 * D, 2, mod5, range(seqs))
        c.load(c.par[:, :], a["ada_b_2"][layer, 2 * D:6 * D].partition_broadcast(P))
        norm2 = cols(c.z, 8192, D)
        c.load(norm2, a["norm2_g_2"][layer, :].partition_broadcast(P))
        c.loaded()

        @c.block.vector
        def _(v):
            v.wait_ge(c.steps_done, c.steps)
            v.tensor_tensor(mods[:, 0:seqs], mods[:, 0:seqs],
                            c.par[:, 0:3 * D].unsqueeze(1).broadcast_to([P, seqs, 3 * D]), ALU.add)
            v.tensor_tensor(mod5[:, 0:seqs], mod5[:, 0:seqs],
                            gain[3].unsqueeze(1).broadcast_to([P, seqs, D]), ALU.add).then_inc(c.steps_done, 1)
        c.steps += 1
        streams = (c.h, c.hc)[:seqs]

        def add_scaled(out, by):

            @c.block.vector
            def _(v):
                v.wait_ge(c.steps_done, c.steps)
                for n in range(seqs):
                    o = out[:, NT * n:NT * n + NT, :]
                    last = v.tensor_tensor(o, o, by(n).unsqueeze(1).broadcast_to([P, NT, D]), ALU.mult)
                last.then_inc(c.steps_done, 1)
            c.steps += 1

            @c.block.vector
            def _(v):
                v.wait_ge(c.steps_done, c.steps)
                for n, x in enumerate(streams):
                    last = v.tensor_tensor(x[:, :, :], x[:, :, :], out[:, NT * n:NT * n + NT, :], ALU.add)
                last.then_inc(c.steps_done, 1)
            c.steps += 1
        add_scaled(mixed, lambda n: mods[:, n, 0:D])
        for n, x in enumerate(streams):
            modulated_norm(c, tiles_of(x), tiles_of(y4[:, NT * n:NT * n + NT, :]), norm2,
                           mods[:, n, D:2 * D], mods[:, n, 2 * D:3 * D])
        tiles = seqs * NT
        tokens = tiles * P
        c.to_feature_major(lambda t, k: y4[:, t, k * P:(k + 1) * P], c.x_t, tiles)

        k_hidden = 4 * KD
        hidden = cols(c.z, 0, k_hidden, tokens)
        banks = 4 * tokens // BANK

        def relu(i, half, s):
            src = c.ps[:, half * 4:half * 4 + banks, :].rearrange("p b n -> p (b n)")
            return s.activation(hidden[:, bass.ds(i * 4, 4), :].rearrange("p k n -> p (k n)"), src, ACT.Relu)

        def squared(i, half, v):
            part = hidden[:, bass.ds(i * 4, 4), :].rearrange("p k n -> p (k n)")
            return v.tensor_tensor(part, part, part, ALU.mult)
        c.gemm_feature_major(c.x_t, tokens, 8, column_chunks(a["mlp_w1_2"][layer], 0), BANK, relu, squared,
                             after_scalar=True)
        c.gemm_rows(hidden, k_hidden, range(tiles), a["mlp_w2_2"][layer])
        out = cols(c.work, 0, tiles, D)
        c.take_rows(out, tiles)
        add_scaled(out, lambda n: mod5[:, n, :])
    final_gain = c.par[:, 0:D]
    c.load(final_gain, a["norm_f_g_2"].partition_broadcast(P))
    c.loaded()
    result = cols(c.work, 0, NT, D)
    c.rmsnorm(tiles_of(c.h), tiles_of(result), final_gain)
    c.result = result


def program(nc, a, out):
    ctx = ExitStack()
    with ctx:
        block = ctx.enter_context(nc.Block())
        c = Core(nc, block, ctx)
        c.z = c.sb("wide", [P, 18560])
        c.h = c.sb("residual", [P, NT, D])
        c.hc = c.sb("context_residual", [P, NT, D])
        c.x_t = c.sb("input_feature_major", [P, KD, 2 * SEQ])
        c.par = c.sb("parameters", [P, 4 * D])
        c.small = c.sb("small", [P, 512])
        c.work = c.sb("work", [P, 11776])
        c.result_stored = ctx.enter_context(nc.semaphore("result_stored"))
        c.prime()
        c.load(c.h[:, :, :], a["x"].rearrange("o (t p) d -> p (o t) d", p=P))
        c.load(c.hc[:, :, :], a["ctx_2"].rearrange("o (t p) d -> p (o t) d", p=P))
        c.loaded()
        make_constants(c)
        first_block(c, a)
        second_block(c, a)
        last = c.steps

        @block.sync
        def _(sp):
            sp.wait_ge(c.steps_done, last)
            sp.dma_start(out.rearrange("o (t p) d -> p (o t) d", p=P), c.result).then_inc(c.result_stored, 16)
            sp.wait_ge(c.result_stored, 16)


def kernel(**inputs):
    import numpy as _np
    import concourse.bacc as _bacc
    from concourse import mybir as _mybir
    from concourse.bass_utils import run_bass_kernel_spmd as _run

    laid = {name: _np.asarray(value) for name, value in inputs.items()}
    for name, order in LAYOUTS.items():
        laid[name] = order(laid[name])
    laid.update(shape_constants())
    nc = _bacc.Bacc("TRN2", target_bir_lowering=False, num_devices=1)
    arrays, a = {}, {}
    for name, value in laid.items():
        value = _np.ascontiguousarray(value)
        arrays[f"in_{name}"] = value
        a[name] = nc.dram_tensor(f"in_{name}", value.shape, _mybir.dt.from_np(value.dtype),
                                 kind="ExternalInput").ap()
    out = nc.dram_tensor("out_0", (1, SEQ, D), _mybir.dt.float32, kind="ExternalOutput").ap()
    program(nc, a, out)
    r = _run(nc, [arrays], core_ids=[0])
    return r.results[0]["out_0"]
```

```python
import math
from contextlib import ExitStack

import concourse.bass as bass
import numpy as np
from concourse import mybir

F32 = mybir.dt.float32
F32R = mybir.dt.float32r
ALU = mybir.AluOpType
ACT = mybir.ActivationFunctionType
AX = mybir.AxisListType.X

P = 128
D = 1024
KD = D // P
SEQ = 256
NT = SEQ // P
DEPTH = 2
EPS = 1e-6
BANK = 512
UNITS = 4
UNIT = KD * BANK // UNITS


class Chain:

    def __init__(self, c, name):
        self.block, self.nc = c.block, c.nc
        self.steps_done = c.ctx.enter_context(c.nc.semaphore(name))
        self.steps = 0


class Core:

    def __init__(self, nc, block, ctx):
        self.nc, self.block, self.ctx = nc, block, ctx
        self.steps_done = ctx.enter_context(nc.semaphore("steps_done"))
        self.steps = 0
        self.raw_arrived = [ctx.enter_context(nc.semaphore(f"raw_weights_arrived_{u}")) for u in range(UNITS)]
        self.hi_made = ctx.enter_context(nc.semaphore("weights_hi_made"))
        self.lo_made = ctx.enter_context(nc.semaphore("weights_lo_made"))
        self.input_hi_made = ctx.enter_context(nc.semaphore("input_hi_made"))
        self.multiplied = ctx.enter_context(nc.semaphore("units_multiplied"))
        self.taken_by_scalar = ctx.enter_context(nc.semaphore("products_taken_by_scalar"))
        self.taken_by_vector = ctx.enter_context(nc.semaphore("products_taken_by_vector"))
        self.params_arrived = ctx.enter_context(nc.semaphore("params_arrived"))
        self.chunks = 0
        self.taken = 2
        self.params = 0
        self.inputs_split = 0
        self.raw = self.sb("raw_weights", [P, UNITS, UNIT])
        self.w_hi = self.sb("weights_hi", [P, 2, UNIT], F32R)
        self.w_lo = self.sb("weights_lo", [P, 2, UNIT], F32R)
        self.ps = ctx.enter_context(nc.psum_tensor("banks", [P, 8, BANK], F32))
        self.chains = [Chain(self, f"chain_{q}_steps_done") for q in range(2)]

    def sb(self, name, shape, dtype=F32):
        return self.ctx.enter_context(self.nc.sbuf_tensor(name, shape, dtype))

    def begin_chains(self):
        n = self.steps

        @self.block.tensor
        def _(pe):
            pe.wait_ge(self.steps_done, n)

        @self.block.vector
        def _(v):
            v.wait_ge(self.steps_done, n)

        @self.block.scalar
        def _(s):
            s.wait_ge(self.steps_done, n)

    def end_chains(self):
        for chain in self.chains:
            n = chain.steps

            @self.block.tensor
            def _(pe):
                pe.wait_ge(chain.steps_done, n)

            @self.block.vector
            def _(v):
                v.wait_ge(chain.steps_done, n)

            @self.block.scalar
            def _(s):
                s.wait_ge(chain.steps_done, n)

            @self.block.gpsimd
            def _(g):
                g.wait_ge(chain.steps_done, n)

    def load(self, dst, src):
        at = self.steps

        @self.block.gpsimd
        def _(pool):
            pool.wait_ge(self.steps_done, at)
            pool.dma_start(dst, src).then_inc(self.params_arrived, 16)
        self.params += 1

    def loaded(self):
        n = 16 * self.params

        @self.block.tensor
        def _(pe):
            pe.wait_ge(self.params_arrived, n)

        @self.block.vector
        def _(v):
            v.wait_ge(self.params_arrived, n)

        @self.block.scalar
        def _(s):
            s.wait_ge(self.params_arrived, n)

        @self.block.gpsimd
        def _(g):
            g.wait_ge(self.params_arrived, n)

    def prime(self):
        @self.block.tensor
        def _(pe):
            pe.sem_inc(self.multiplied, 2)

        @self.block.scalar
        def _(s):
            s.sem_inc(self.taken_by_scalar, 2)

        @self.block.vector
        def _(v):
            v.sem_inc(self.taken_by_vector, 2)
            v.sem_inc(self.lo_made, UNITS)

    def split_input(self, x, hi, lo):
        at, made = self.steps, self.inputs_split
        pieces = [slice(k, k + KD // 4) for k in range(0, KD, KD // 4)]

        @self.block.scalar
        def _(s):
            s.wait_ge(self.steps_done, at)
            for piece in pieces:
                s.activation(hi[:, piece, :], x[:, piece, :], ACT.Copy).then_inc(self.input_hi_made, 1)

        @self.block.vector
        def _(v):
            v.wait_ge(self.steps_done, at)
            for n, piece in enumerate(pieces):
                v.wait_ge(self.input_hi_made, made + n + 1)
                last = v.tensor_tensor(lo[:, piece, :], x[:, piece, :], hi[:, piece, :].bitcast(F32), ALU.subtract)
            last.then_inc(self.steps_done, 1)
        self.inputs_split += len(pieces)
        self.steps += 1
        self.x_hi, self.x_lo = hi, lo

    def unit(self, buf, shape):
        return buf[:, 0:int(np.prod(shape))].rearrange("p (k n) -> p k n", n=shape[-1])

    def load_units(self, sp, source, shape, chunk, unit):
        for u in range(UNITS):
            sp.wait_ge(self.lo_made, unit + u + 1)
            sp.dma_start(self.unit(self.raw[:, u, :], shape), source(u)).then_inc(self.raw_arrived[u], 16)

    def hi_unit(self, s, u, chunk, unit, x=None):
        s.wait_ge(self.raw_arrived[u], chunk * 16 + 16)
        s.wait_ge(self.multiplied, unit + u + 1)
        last = s.activation(self.w_hi[:, u % 2, :], self.raw[:, u, :], ACT.Copy)
        if x is not None:
            last = s.activation(self.stage_hi(u, x), x, ACT.Copy)
        last.then_inc(self.hi_made, 1)

    def lo_unit(self, v, u, unit, x=None):
        v.wait_ge(self.hi_made, unit + u + 1)
        last = v.tensor_tensor(self.w_lo[:, u % 2, :], self.raw[:, u, :], self.w_hi[:, u % 2, :].bitcast(F32),
                               ALU.subtract)
        if x is not None:
            last = v.tensor_tensor(self.stage_lo(u, x), x, self.stage_hi(u, x).bitcast(F32), ALU.subtract)
        last.then_inc(self.lo_made, 1)

    def stage_hi(self, u, x):
        return self.staged[:, u % 2, 0:1, 0:x.shape[-1]]

    def stage_lo(self, u, x):
        return self.staged[:, u % 2, 1:2, 0:x.shape[-1]]

    def three_products(self, pe, out, left_hi, left_lo, right_hi, right_lo, start, stop):
        pe.matmul(out, left_hi, right_hi, start=start, stop=False)
        pe.matmul(out, left_hi, right_lo, start=False, stop=False)
        return pe.matmul(out, left_lo, right_hi, start=False, stop=stop)

    def gemm(self, count, source, shape, product, take_scalar, take_vector, after_scalar=False):
        nc, at, g0 = self.nc, self.steps, self.taken
        c0, m0 = self.chunks, self.chunks * UNITS
        pairs = (count - 1) // 2 if count >= 5 else 0

        @self.block.sync
        def _(sp):
            if count > 1:
                with sp.Fori(0, count) as i:
                    self.load_units(sp, lambda u: source(i, u), shape, i + c0, i * UNITS + m0)
            else:
                self.load_units(sp, lambda u: source(0, u), shape, c0, m0)

        @self.block.tensor
        def _(pe):
            pe.wait_ge(self.steps_done, at)

            def multiply(chunk, half):
                pe.wait_ge(self.taken_by_scalar, chunk + (g0 - 1))
                pe.wait_ge(self.taken_by_vector, chunk + (g0 - 1))
                for u in range(UNITS):
                    pe.wait_ge(self.lo_made, chunk * UNITS + (m0 + u + 1 + UNITS))
                    product(half * 4, u, self.unit(self.w_hi[:, u % 2, :], shape),
                            self.unit(self.w_lo[:, u % 2, :], shape), nc.tensor).then_inc(self.multiplied, 1)
            multiply(0, 0)
            if pairs:
                with pe.Fori(0, pairs) as i:
                    multiply(i * 2 + 1, 1)
                    multiply(i * 2 + 2, 0)
            for chunk in range(1 + 2 * pairs, count):
                multiply(chunk, chunk % 2)

        @self.block.scalar
        def _(s):
            s.wait_ge(self.steps_done, at)

            def empty(chunk, half):
                s.wait_ge(self.multiplied, chunk * UNITS + (m0 + 2 + UNITS))
                last = take_scalar(chunk, half, s)
                if last is None:
                    s.sem_inc(self.taken_by_scalar, 1)
                else:
                    last.then_inc(self.taken_by_scalar, 1)

            def split_and_empty(chunk, half):
                for u in range(UNITS):
                    if u == UNITS // 2:
                        empty(chunk - 1, 1 - half)
                    self.hi_unit(s, u, chunk + c0, chunk * UNITS + m0)
            for u in range(UNITS):
                self.hi_unit(s, u, c0, m0)
            if pairs:
                with s.Fori(0, pairs) as i:
                    split_and_empty(i * 2 + 1, 1)
                    split_and_empty(i * 2 + 2, 0)
            for chunk in range(1 + 2 * pairs, count):
                split_and_empty(chunk, chunk % 2)
            empty(count - 1, (count - 1) % 2)

        @self.block.vector
        def _(v):
            v.wait_ge(self.steps_done, at)

            def empty(chunk, half):
                v.wait_ge(self.multiplied, chunk * UNITS + (m0 + 2 + UNITS))
                if after_scalar:
                    v.wait_ge(self.taken_by_scalar, chunk + (g0 + 1))
                last = take_vector(chunk, half, v)
                if last is None:
                    v.sem_inc(self.taken_by_vector, 1)
                else:
                    last.then_inc(self.taken_by_vector, 1)

            def split_and_empty(chunk, half):
                for u in range(UNITS):
                    if u == UNITS // 2:
                        empty(chunk - 1, 1 - half)
                    self.lo_unit(v, u, chunk * UNITS + m0)
            for u in range(UNITS):
                self.lo_unit(v, u, m0)
            if pairs:
                with v.Fori(0, pairs) as i:
                    split_and_empty(i * 2 + 1, 1)
                    split_and_empty(i * 2 + 2, 0)
            for chunk in range(1 + 2 * pairs, count):
                split_and_empty(chunk, chunk % 2)
            empty(count - 1, (count - 1) % 2)
        self.chunks += count
        self.taken += count
        n = self.taken

        @self.block.tensor
        def _(pe):
            pe.wait_ge(self.taken_by_scalar, n)
            pe.wait_ge(self.taken_by_vector, n)

        @self.block.scalar
        def _(s):
            s.wait_ge(self.taken_by_scalar, n)
            s.wait_ge(self.taken_by_vector, n)

        @self.block.vector
        def _(v):
            v.wait_ge(self.taken_by_scalar, n)
            v.wait_ge(self.taken_by_vector, n)

        @self.block.gpsimd
        def _(g):
            g.wait_ge(self.taken_by_scalar, n)
            g.wait_ge(self.taken_by_vector, n)

    def gemm_token_major(self, tiles, count, source, width, take_scalar, take_vector, after_scalar=False):
        per_unit = KD // UNITS

        def product(banks, u, hi, lo, pe):
            for n, t in enumerate(tiles):
                for j in range(per_unit):
                    k, tokens = u * per_unit + j, slice(t * P, (t + 1) * P)
                    last = self.three_products(pe, self.ps[:, banks + n, 0:width], self.x_hi[:, k, tokens],
                                               self.x_lo[:, k, tokens], hi[:, j, :], lo[:, j, :],
                                               k == 0, k == KD - 1)
            return last
        self.gemm(count, lambda i, u: source(i)[:, u * per_unit:(u + 1) * per_unit, :], (per_unit, width), product,
                  take_scalar, take_vector, after_scalar)

    def gemm_feature_major(self, tokens, count, source, take_scalar, take_vector, after_scalar=False):
        def product(banks, u, hi, lo, pe):
            at = u * tokens
            out = self.ps[:, banks + at // BANK, at % BANK:at % BANK + tokens]
            for k in range(KD):
                last = self.three_products(pe, out, hi[:, k, :], lo[:, k, :], self.x_hi[:, k, 0:tokens],
                                           self.x_lo[:, k, 0:tokens], k == 0, k == KD - 1)
            return last
        self.gemm(count, source, (KD, P), product, take_scalar, take_vector, after_scalar)

    def gemm_rows(self, x, k_chunks, tiles, w_rows, staged):
        nc, at = self.nc, self.steps
        self.staged = staged
        w_v = w_rows.rearrange("(k p) n -> p k n", p=P)
        full = k_chunks // UNITS
        tail = k_chunks % UNITS
        middle = full - 2 + bool(tail)
        c0, m0 = self.chunks, self.chunks * UNITS

        def piece(k):
            return x[:, bass.ds(k, 1), :]

        @self.block.sync
        def _(sp):
            with sp.Fori(0, full) as i:
                self.load_units(sp, lambda u: w_v[:, bass.ds(i * UNITS + u, 1), :], (1, D), i + c0,
                                i * UNITS + m0)
            if tail:
                self.load_units(sp, lambda u: w_v[:, full * UNITS + u // 2:full * UNITS + u // 2 + 1,
                                                  u % 2 * BANK:(u % 2 + 1) * BANK], (1, BANK), full + c0,
                                full * UNITS + m0)

        @self.block.tensor
        def _(pe):
            pe.wait_ge(self.steps_done, at)

            def multiply(chunk, first, last_chunk, halves):
                for u in range(UNITS):
                    pe.wait_ge(self.lo_made, chunk * UNITS + (m0 + u + 1 + UNITS))
                    for n, t in enumerate(tiles):
                        tokens = slice(t * P, (t + 1) * P)
                        for half in (range(2) if halves else (u % 2,)):
                            columns = slice(half * BANK, (half + 1) * BANK) if halves else slice(0, BANK)
                            last = self.three_products(
                                nc.tensor, self.ps[:, 2 * n + half, :], self.staged[:, u % 2, 0, tokens],
                                self.staged[:, u % 2, 1, tokens], self.w_hi[:, u % 2, columns],
                                self.w_lo[:, u % 2, columns], first and u == 0,
                                last_chunk and (u == UNITS - 1 or (not halves and u >= 2)))
                    last.then_inc(self.multiplied, 1)
            multiply(0, True, False, True)
            with pe.Fori(0, middle) as i:
                multiply(i + 1, False, False, True)
            multiply(middle + 1, False, True, not tail)

        @self.block.scalar
        def _(s):
            s.wait_ge(self.steps_done, at)
            with s.Fori(0, full) as i:
                for u in range(UNITS):
                    self.hi_unit(s, u, i + c0, i * UNITS + m0, piece(i * UNITS + u))
            if tail:
                for u in range(UNITS):
                    self.hi_unit(s, u, full + c0, full * UNITS + m0, piece(full * UNITS + u // 2))

        @self.block.vector
        def _(v):
            v.wait_ge(self.steps_done, at)
            with v.Fori(0, full) as i:
                for u in range(UNITS):
                    self.lo_unit(v, u, i * UNITS + m0, piece(i * UNITS + u))
            if tail:
                for u in range(UNITS):
                    self.lo_unit(v, u, full * UNITS + m0, piece(full * UNITS + u // 2))
        self.chunks += full + bool(tail)
        n = self.chunks * UNITS + 2

        @self.block.scalar
        def _(s):
            s.wait_ge(self.multiplied, n)

        @self.block.vector
        def _(v):
            v.wait_ge(self.multiplied, n)

    def take_rows(self, out, tiles):
        ps = self.ps

        @self.block.scalar
        def _(s):
            s.wait_ge(self.steps_done, self.steps)
            for t in range(tiles):
                last = s.activation(out[:, t, 0:BANK], ps[:, 2 * t, :], ACT.Copy)
            last.then_inc(self.steps_done, 1)
        @self.block.vector
        def _(v):
            v.wait_ge(self.steps_done, self.steps)
            for t in range(tiles):
                last = v.tensor_copy(out[:, t, BANK:D], ps[:, 2 * t + 1, :])
            last.then_inc(self.steps_done, 1)
        self.steps += 2

    def transposes(self, quads):
        ident, ps = self.ident, self.ps
        batches = [quads[n:n + 4] for n in range(0, len(quads), 4)]

        def banks_of(n, which):
            for b, (srcs, dst) in enumerate(batches[n]):
                if b % 2 == which:
                    m = srcs[0].shape[-1]
                    yield ps[0:m, n % 2 * 4 + b, 0:len(srcs) * P].rearrange("p (j t) -> p j t", t=P), dst

        for n in range(len(batches) + 1):
            at = self.steps
            if n < len(batches):
                @self.block.tensor
                def _(pe):
                    pe.wait_ge(self.steps_done, at)
                    for b, (srcs, _) in enumerate(batches[n]):
                        for j, src in enumerate(srcs):
                            out = ps[0:src.shape[-1], n % 2 * 4 + b, j * P:(j + 1) * P]
                            last = pe.transpose(out, src, ident[:, :])
                    last.then_inc(self.steps_done, 1)
                self.steps += 1
            if n:
                @self.block.scalar
                def _(s):
                    s.wait_ge(self.steps_done, at)
                    for src, dst in banks_of(n - 1, 0):
                        last = s.activation(dst, src, ACT.Copy)
                    last.then_inc(self.steps_done, 1)
                self.steps += 1
            if n and len(batches[n - 1]) > 1:
                @self.block.vector
                def _(v):
                    v.wait_ge(self.steps_done, at)
                    for src, dst in banks_of(n - 1, 1):
                        last = v.tensor_copy(dst, src)
                    last.then_inc(self.steps_done, 1)
                self.steps += 1

    def to_feature_major(self, x, dst, tiles, first=0, kd=KD):
        self.transposes([([x(t, k + j) for j in range(4)], dst[:, k:k + 4, (first + t) * P:(first + t + 1) * P])
                         for t in range(tiles) for k in range(0, kd, 4)])

    def rstd(self, ss, scale, eps):

        @self.block.vector
        def _(v):
            v.wait_ge(self.steps_done, self.steps)
            v.tensor_scalar(ss, ss, scale, eps, ALU.mult, ALU.add).then_inc(self.steps_done, 1)
        self.steps += 1

        @self.block.scalar
        def _(s):
            s.wait_ge(self.steps_done, self.steps)
            s.activation(ss, ss, ACT.Sqrt).then_inc(self.steps_done, 1)
        self.steps += 1

        @self.block.vector
        def _(v):
            v.wait_ge(self.steps_done, self.steps)
            v.reciprocal(ss, ss).then_inc(self.steps_done, 1)
        self.steps += 1

    def rmsnorm(self, xs, outs, gain, n=D, squared=None):
        ss = self.small[:, 0:len(xs)]

        @self.block.scalar
        def _(s):
            s.wait_ge(self.steps_done, self.steps)
            for j, (x, out) in enumerate(zip(xs, squared or outs)):
                last = s.activation(out, x, ACT.Square, accum_out=ss[:, j:j + 1])
            last.then_inc(self.steps_done, 1)
        self.steps += 1
        self.rstd(ss, 1.0 / n, EPS)

        @self.block.vector
        def _(v):
            v.wait_ge(self.steps_done, self.steps)
            for j, (x, out) in enumerate(zip(xs, outs)):
                last = v.scalar_tensor_tensor(out, x, ss[:, j:j + 1], gain, ALU.mult, ALU.mult)
            last.then_inc(self.steps_done, 1)
        self.steps += 1

    def log1p(self, e, out, z, z2):

        @self.block.vector
        def _(v):
            v.wait_ge(self.steps_done, self.steps)
            v.tensor_scalar(z, e, 2.0, None, ALU.add).then_inc(self.steps_done, 1)
        self.steps += 1

        @self.block.vector
        def _(v):
            v.wait_ge(self.steps_done, self.steps)
            v.reciprocal(z, z).then_inc(self.steps_done, 1)
        self.steps += 1

        @self.block.vector
        def _(v):
            v.wait_ge(self.steps_done, self.steps)
            v.tensor_tensor(z, z, e, ALU.mult).then_inc(self.steps_done, 1)
        self.steps += 1

        @self.block.vector
        def _(v):
            v.wait_ge(self.steps_done, self.steps)
            v.tensor_tensor(z2, z, z, ALU.mult).then_inc(self.steps_done, 1)
        self.steps += 1

        @self.block.vector
        def _(v):
            v.wait_ge(self.steps_done, self.steps)
            v.tensor_scalar(out, z2, 1.0 / 17, None, ALU.mult).then_inc(self.steps_done, 1)
        self.steps += 1
        for odd in (15, 13, 11, 9, 7, 5, 3):

            @self.block.vector
            def _(v):
                v.wait_ge(self.steps_done, self.steps)
                v.scalar_tensor_tensor(out, out, 1.0 / odd, z2, ALU.add, ALU.mult).then_inc(self.steps_done, 1)
            self.steps += 1

        @self.block.vector
        def _(v):
            v.wait_ge(self.steps_done, self.steps)
            v.scalar_tensor_tensor(out, out, 1.0, z, ALU.add, ALU.mult).then_inc(self.steps_done, 1)
        self.steps += 1

        @self.block.vector
        def _(v):
            v.wait_ge(self.steps_done, self.steps)
            v.tensor_scalar(out, out, 2.0, None, ALU.mult).then_inc(self.steps_done, 1)
        self.steps += 1

    def softplus(self, x, out, t1, t2, t3):

        @self.block.scalar
        def _(s):
            s.wait_ge(self.steps_done, self.steps)
            s.activation(t1, x, ACT.Abs).then_inc(self.steps_done, 1)
        self.steps += 1

        @self.block.scalar
        def _(s):
            s.wait_ge(self.steps_done, self.steps)
            s.activation(t2, t1, ACT.Exp, scale=-1.0).then_inc(self.steps_done, 1)
        self.steps += 1
        self.log1p(t2, out, t1, t3)

        @self.block.vector
        def _(v):
            v.wait_ge(self.steps_done, self.steps)
            v.scalar_tensor_tensor(out, x, 0.0, out, ALU.max, ALU.add).then_inc(self.steps_done, 1)
        self.steps += 1


def cols(buf, offset, *dims):
    n = int(np.prod(dims))
    flat = buf[:, offset:offset + n]
    if len(dims) == 1:
        return flat
    names = "abcd"[:len(dims)]
    sizes = {names[i]: dims[i] for i in range(1, len(dims))}
    return flat.rearrange(f"p ({' '.join(names)}) -> p {' '.join(names)}", **sizes)


def column_chunks(w, first, width=BANK):
    w_v = w.rearrange("(k p) n -> p k n", p=P)
    return lambda i: w_v[:, :, bass.ds(i * width + first, width)]


def column_units(w, first):
    w_v = w.rearrange("(k p) n -> p k n", p=P)
    return lambda i, u: w_v[:, :, bass.ds(i * BANK + (first + u * P), P)]


def split_narrow(c):
    c.split_input(c.x_t[:, :, 0:SEQ], c.x_t_split[:, :, SEQ:2 * SEQ], c.x_t_split[:, :, 0:SEQ])


def split_wide(c, tokens):
    c.split_input(c.x_t[:, :, 0:tokens], c.work_split[:, :, 0:tokens], c.x_t_split[:, :, 0:tokens])


def rows_stage(split):
    return split[:, 0:4, :].rearrange("p (s h) t -> p s h t", s=2)


def make_constants(c):
    c.ident = c.sb("identity", [P, P])
    c.ones = c.sb("ones", [P, P])
    c.upto = c.sb("mask_row_upto_column", [P, P])
    c.onward = c.sb("mask_row_from_column_on", [P, P])
    c.after = c.sb("mask_row_after_column", [P, NT, SEQ])
    c.future = c.sb("minus_big_where_key_after_query", [P, NT, SEQ])

    @c.block.gpsimd
    def _(g):
        g.wait_ge(c.steps_done, c.steps)
        g.memset(c.ident[:, :], 0.0)
        g.memset(c.ones[:, :], 1.0)
        g.memset(c.upto[:, :], 1.0)
        g.memset(c.onward[:, :], 1.0)
        g.memset(c.after[:, :, :], 1.0)
        g.memset(c.future[:, :, :], 0.0).then_inc(c.steps_done, 1)
    c.steps += 1

    @c.block.gpsimd
    def _(g):
        g.wait_ge(c.steps_done, c.steps)
        g.affine_select(out=c.ident[:, :], in_=c.ident[:, :], compare_op=ALU.not_equal, fill=1.0, base=0,
                        pattern=[[-1, P]], channel_multiplier=1)
        g.affine_select(out=c.upto[:, :], in_=c.upto[:, :], compare_op=ALU.is_ge, fill=0.0, base=0,
                        pattern=[[1, P]], channel_multiplier=-1)
        g.affine_select(out=c.onward[:, :], in_=c.onward[:, :], compare_op=ALU.is_ge, fill=0.0, base=0,
                        pattern=[[-1, P]], channel_multiplier=1)
        g.affine_select(out=c.after[:, :, :], in_=c.after[:, :, :], compare_op=ALU.is_gt, fill=0.0, base=0,
                        pattern=[[P, NT], [-1, SEQ]], channel_multiplier=1)
        g.affine_select(out=c.future[:, :, :], in_=c.future[:, :, :], compare_op=ALU.is_ge, fill=-1e30,
                        base=0, pattern=[[P, NT], [-1, SEQ]], channel_multiplier=1).then_inc(c.steps_done, 1)
    c.steps += 1


def copy_halves(c, dst):
    def scalar(i, half, s):
        last = None
        for n in dst.scalar:
            last = s.activation(dst.place(i, n), dst.bank(half * 4 + n), ACT.Copy)
        return last

    def vector(i, half, v):
        last = None
        for n in dst.vector:
            last = v.tensor_copy(dst.place(i, n), dst.bank(half * 4 + n))
        return last
    return scalar, vector


class Copies:

    def __init__(self, c, place, banks, width=BANK):
        self.place = place
        self.scalar = [n for n in range(banks) if n % 2 == 0]
        self.vector = [n for n in range(banks) if n % 2 == 1]
        self.bank = lambda b: c.ps[:, b, 0:width]


def token_copies(c, dst, tiles, width=BANK):
    return copy_halves(c, Copies(c, lambda i, n: dst[:, tiles[n], bass.ds(i * width, width)], len(tiles), width))


def swiglu(c, w_gu, w_down, out):
    dff = w_down.shape[0]
    k_hidden = dff // P
    hidden = cols(c.z, 0, k_hidden, SEQ)
    act = cols(c.work, 0, 2, 2 * SEQ)
    w_v = w_gu.rearrange("(k p) n -> p k n", p=P)

    def source(i, u):
        return w_v[:, :, bass.ds(i * (2 * P) + (u // 2 * dff + u % 2 * P), P)]

    def scalar(i, half, s):
        return s.activation(act[:, half, :], c.ps[:, half * 4, :], ACT.Silu)

    def vector(i, half, v):
        dst = hidden[:, bass.ds(i * 2, 2), :]
        return v.tensor_tensor(dst, act[:, half, :].rearrange("p (j t) -> p j t", t=SEQ),
                               c.ps[:, half * 4 + 1, :].rearrange("p (j t) -> p j t", t=SEQ), ALU.mult)
    c.gemm_feature_major(SEQ, dff // (2 * P), source, scalar, vector, after_scalar=True)
    c.gemm_rows(hidden, k_hidden, range(NT), w_down, rows_stage(c.x_t_split))
    c.take_rows(out, NT)


def add_normed(c, h, y, gain, scale):
    squared = [c.x_t[:, 2 * t:2 * t + 2, :].rearrange("p k n -> p (k n)") for t in range(NT)]
    c.rmsnorm([y[:, t, :] for t in range(NT)], [y[:, t, :] for t in range(NT)], gain, squared=squared)

    @c.block.vector
    def _(v):
        v.wait_ge(c.steps_done, c.steps)
        for t in range(NT):
            last = v.scalar_tensor_tensor(h[:, t, :], y[:, t, :], scale, h[:, t, :], ALU.mult, ALU.add)
        last.then_inc(c.steps_done, 1)
    c.steps += 1


def mlstm(c, qk_t, v_tok, o_tok, gates, out, gain):
    heads, dv = 4, 256
    scale = float(P) ** -0.5
    w = c.work
    r = cols(w, 2048, heads, NT, SEQ)
    di = cols(w, 4096, heads, NT, P)
    ld = cols(w, 5120, heads, SEQ)
    dm = cols(w, 6144, heads, SEQ)
    s_t = cols(w, 7168, heads, NT, P)
    sm = c.small
    lf, t1, t2, t3 = (cols(sm, 16 + 8 * n, NT, heads) for n in range(4))
    negf = cols(sm, 48, NT, heads)
    mx, den, em, rs = (cols(sm, 56 + 4 * n, heads) for n in range(4))
    stats = cols(sm, 72, heads, 6)
    mv = cols(sm, 96, heads, 2)

    @c.block.vector
    def _(v):
        v.wait_ge(c.steps_done, c.steps)
        v.tensor_scalar(negf, gates[:, :, 4:8], -1.0, None, ALU.mult).then_inc(c.steps_done, 1)
    c.steps += 1
    c.softplus(negf, lf, t1, t2, t3)

    @c.block.vector
    def _(v):
        v.wait_ge(c.steps_done, c.steps)
        v.tensor_scalar(lf, lf, -1.0, None, ALU.mult).then_inc(c.steps_done, 1)
    @c.block.scalar
    def _(s):
        s.wait_ge(c.steps_done, c.steps)
        s.activation(o_tok, o_tok, ACT.Sigmoid).then_inc(c.steps_done, 1)
    c.steps += 2

    @c.block.vector
    def _(v):
        v.wait_ge(c.steps_done, c.steps)
        for h in range(heads):
            for j in range(NT):
                v.tensor_scalar(r[:, h, j, :], c.after[:, j, :], lf[:, j, h:h + 1], None, ALU.mult)
                last = v.tensor_scalar(di[:, h, j, :], c.ident[:, :], gates[:, j, h:h + 1], None, ALU.mult)
        last.then_inc(c.steps_done, 1)
    c.steps += 1
    for t in range(NT):
        n = (t + 1) * P

        def bank(first, h, cut=n):
            return c.ps[:, first + h // 2, h % 2 * SEQ:h % 2 * SEQ + cut]

        def four(first, cut=n):
            return c.ps[:, first:first + 2, :].rearrange("p b (h s) -> p (b h) s", s=SEQ)[:, :, 0:cut]

        @c.block.tensor
        def _(pe):
            pe.wait_ge(c.steps_done, c.steps)
            for h in range(heads):
                for j in range(t + 1):
                    pe.matmul(bank(0, h), c.upto[:, :] if j == t else c.ones[:, :], r[:, h, j, 0:n],
                              start=(j == 0), stop=False)
                for j in range(t + 1):
                    pe.matmul(bank(0, h)[:, j * P:(j + 1) * P], c.ones[:, :], di[:, h, j, :],
                              start=False, stop=(j == t))
            for h in range(heads):
                last = pe.matmul(bank(2, h), qk_t[:, h, t * P:(t + 1) * P], qk_t[:, heads + h, 0:n],
                                 start=True, stop=True)
            last.then_inc(c.steps_done, 1)
        c.steps += 1

        @c.block.vector
        def _(v):
            v.wait_ge(c.steps_done, c.steps)
            v.tensor_tensor(
ld[:, :, 0:n], four(0), c.future[:, t:t + 1, 0:n].broadcast_to([P, heads, n]), ALU.add).then_inc(c.steps_done, 1)
        c.steps += 1

        @c.block.vector
        def _(v):
            v.wait_ge(c.steps_done, c.steps)
            v.reduce_max(mx, ld[:, :, 0:n], AX).then_inc(c.steps_done, 1)
        c.steps += 1

        @c.block.vector
        def _(v):
            v.wait_ge(c.steps_done, c.steps)
            v.tensor_scalar(mx, mx, -1.0, None, ALU.mult).then_inc(c.steps_done, 1)
        c.steps += 1

        @c.block.scalar
        def _(s):
            s.wait_ge(c.steps_done, c.steps)
            for h in range(heads):
                s.activation(dm[:, h, 0:n], ld[:, h, 0:n], ACT.Exp, bias=mx[:, h:h + 1])
            s.activation(em, mx, ACT.Exp).then_inc(c.steps_done, 1)
        c.steps += 1

        @c.block.vector
        def _(v):
            v.wait_ge(c.steps_done, c.steps)
            for h in range(heads):
                last = v.scalar_tensor_tensor(ld[:, h, 0:n], bank(2, h), scale, dm[:, h, 0:n],
                                              ALU.mult, ALU.mult, accum_out=den[:, h:h + 1])
            last.then_inc(c.steps_done, 1)
        c.steps += 1

        @c.block.scalar
        def _(s):
            s.wait_ge(c.steps_done, c.steps)
            s.activation(den, den, ACT.Abs).then_inc(c.steps_done, 1)
        c.steps += 1

        @c.block.vector
        def _(v):
            v.wait_ge(c.steps_done, c.steps)
            v.tensor_tensor(den, den, em, ALU.max).then_inc(c.steps_done, 1)
        c.steps += 1

        @c.block.vector
        def _(v):
            v.wait_ge(c.steps_done, c.steps)
            v.reciprocal(den, den).then_inc(c.steps_done, 1)
        c.steps += 1
        c.transposes([([ld[:, h, j * P:(j + 1) * P] for j in range(t + 1)], s_t[:, h, 0:t + 1, :])
                      for h in range(heads)])

        @c.block.tensor
        def _(pe):
            pe.wait_ge(c.steps_done, c.steps)
            for h in range(heads):
                for j in range(t + 1):
                    last = pe.matmul(bank(4, h, dv), s_t[:, h, j, :], v_tok[:, j, h * dv:(h + 1) * dv],
                                     start=(j == 0), stop=(j == t))
            last.then_inc(c.steps_done, 1)
        c.steps += 1
        y = out[:, t, :].rearrange("p (h d) -> p h d", d=dv)
        heads_layernorm(c, lambda h: bank(4, h, dv), [den[:, h:h + 1] for h in range(heads)],
                        [y[:, h, :] for h in range(heads)], stats, mv, rs)

        @c.block.vector
        def _(v):
            v.wait_ge(c.steps_done, c.steps)
            v.tensor_tensor(out[:, t, :], out[:, t, :], gain, ALU.mult).then_inc(c.steps_done, 1)
        c.steps += 1

        @c.block.vector
        def _(v):
            v.wait_ge(c.steps_done, c.steps)
            v.tensor_tensor(out[:, t, :], out[:, t, :], o_tok[:, t, :], ALU.mult).then_inc(c.steps_done, 1)
        c.steps += 1


def heads_layernorm(c, src, scales, dsts, stats, mv, rs, eps=EPS):
    n = len(dsts)
    if scales is not None:

        @c.block.vector
        def _(v):
            v.wait_ge(c.steps_done, c.steps)
            for h in range(n):
                last = v.tensor_scalar(dsts[h], src(h), scales[h], None, ALU.mult)
            last.then_inc(c.steps_done, 1)
        c.steps += 1
        src = lambda h: dsts[h]

    @c.block.vector
    def _(v):
        v.wait_ge(c.steps_done, c.steps)
        for h in range(n):
            last = v.bn_stats(stats[:, h, :], src(h))
        last.then_inc(c.steps_done, 1)
    c.steps += 1

    @c.block.vector
    def _(v):
        v.wait_ge(c.steps_done, c.steps)
        for h in range(n):
            last = v.bn_aggr(mv[:, h, :], stats[:, h, :])
        last.then_inc(c.steps_done, 1)
    c.steps += 1

    @c.block.vector
    def _(v):
        v.wait_ge(c.steps_done, c.steps)
        v.tensor_scalar(rs, mv[:, :, 1], eps, None, ALU.add).then_inc(c.steps_done, 1)
    c.steps += 1

    @c.block.scalar
    def _(s):
        s.wait_ge(c.steps_done, c.steps)
        s.activation(rs, rs, ACT.Sqrt).then_inc(c.steps_done, 1)
    c.steps += 1

    @c.block.vector
    def _(v):
        v.wait_ge(c.steps_done, c.steps)
        v.reciprocal(rs, rs).then_inc(c.steps_done, 1)
    c.steps += 1

    @c.block.vector
    def _(v):
        v.wait_ge(c.steps_done, c.steps)
        for h in range(n):
            last = v.tensor_scalar(dsts[h], src(h), mv[:, h, 0:1], rs[:, h:h + 1], ALU.subtract, ALU.mult)
        last.then_inc(c.steps_done, 1)
    c.steps += 1


def spatial_gating(c, us, out, w_t, bias, gain, shift):
    groups, dg = 4, 256
    u, v_tok = us[:, :, 0:D], us[:, :, D:2 * D]
    sm = c.small
    stats = cols(sm, 72, NT * groups, 6)
    mv = cols(sm, 120, NT * groups, 2)
    rs = cols(sm, 136, NT * groups)

    @c.block.scalar
    def _(s):
        s.wait_ge(c.steps_done, c.steps)
        s.activation(us, us, ACT.Gelu_apprx_tanh).then_inc(c.steps_done, 1)
    @c.block.gpsimd
    def _(g):
        g.wait_ge(c.steps_done, c.steps)
        g.affine_select(out=w_t, in_=w_t, compare_op=ALU.is_ge, fill=0.0, base=0,
                        pattern=[[0, groups], [1, P]], channel_multiplier=-1).then_inc(c.steps_done, 1)
    c.steps += 2
    pieces = [v_tok[:, t, g * dg:(g + 1) * dg] for t in range(NT) for g in range(groups)]
    heads_layernorm(c, lambda h: pieces[h], None, pieces, stats, mv, rs)

    @c.block.vector
    def _(v):
        v.wait_ge(c.steps_done, c.steps)
        v.tensor_tensor(v_tok, v_tok, gain.unsqueeze(1).broadcast_to([P, NT, D]), ALU.mult).then_inc(c.steps_done, 1)
    c.steps += 1

    @c.block.vector
    def _(v):
        v.wait_ge(c.steps_done, c.steps)
        v.tensor_tensor(v_tok, v_tok, shift.unsqueeze(1).broadcast_to([P, NT, D]), ALU.add).then_inc(c.steps_done, 1)
    c.steps += 1

    @c.block.tensor
    def _(pe):
        pe.wait_ge(c.steps_done, c.steps)
        for t in range(NT):
            for g in range(groups):
                last = pe.matmul(c.ps[:, t * 2 + g // 2, g % 2 * dg:(g % 2 + 1) * dg], w_t[:, g, :],
                                 v_tok[:, t, g * dg:(g + 1) * dg], start=True, stop=True)
        last.then_inc(c.steps_done, 1)
    c.steps += 1

    @c.block.vector
    def _(v):
        v.wait_ge(c.steps_done, c.steps)
        for t in range(NT):
            for g in range(groups):
                ch = slice(g * dg, (g + 1) * dg)
                last = v.scalar_tensor_tensor(out[:, t, ch], c.ps[:, t * 2 + g // 2, g % 2 * dg:(g % 2 + 1) * dg],
                                              bias[:, g:g + 1], u[:, t, ch], ALU.add, ALU.mult)
        last.then_inc(c.steps_done, 1)
    c.steps += 1


def memory_attention(c, q_t, k_t, v_tok, out):
    heads, dh = 4, 256
    scale = float(dh) ** -0.5
    p = cols(c.work, 0, heads, SEQ)
    p_t = cols(c.work, 1024, heads, NT, P)
    mx, total = cols(c.small, 56, heads), cols(c.small, 60, heads)
    for t in range(NT):
        def bank(first, h):
            return c.ps[:, first + h // 2, h % 2 * SEQ:(h % 2 + 1) * SEQ]

        @c.block.tensor
        def _(pe):
            pe.wait_ge(c.steps_done, c.steps)
            for h in range(heads):
                for j in range(2):
                    last = pe.matmul(bank(0, h), q_t[:, 2 * h + j, t * P:(t + 1) * P], k_t[:, 2 * h + j, :],
                                     start=(j == 0), stop=(j == 1))
            last.then_inc(c.steps_done, 1)
        c.steps += 1

        @c.block.vector
        def _(v):
            v.wait_ge(c.steps_done, c.steps)
            v.reduce_max(
mx, c.ps[:, 0:2, :].rearrange("p b (h s) -> p (b h) s", s=SEQ), AX).then_inc(c.steps_done, 1)
        c.steps += 1

        @c.block.vector
        def _(v):
            v.wait_ge(c.steps_done, c.steps)
            v.tensor_scalar(mx, mx, -scale, None, ALU.mult).then_inc(c.steps_done, 1)
        c.steps += 1

        @c.block.scalar
        def _(s):
            s.wait_ge(c.steps_done, c.steps)
            for h in range(heads):
                last = s.activation(p[:, h, :], bank(0, h), ACT.Exp, bias=mx[:, h:h + 1], scale=scale,
                                    accum_out=total[:, h:h + 1])
            last.then_inc(c.steps_done, 1)
        c.steps += 1

        @c.block.vector
        def _(v):
            v.wait_ge(c.steps_done, c.steps)
            v.reciprocal(total, total).then_inc(c.steps_done, 1)
        c.steps += 1
        c.transposes([([p[:, h, j * P:(j + 1) * P] for j in range(NT)], p_t[:, h, :, :]) for h in range(heads)])

        @c.block.tensor
        def _(pe):
            pe.wait_ge(c.steps_done, c.steps)
            for h in range(heads):
                for j in range(NT):
                    last = pe.matmul(bank(4, h), p_t[:, h, j, :], v_tok[:, j, h * dh:(h + 1) * dh],
                                     start=(j == 0), stop=(j == NT - 1))
            last.then_inc(c.steps_done, 1)
        c.steps += 1

        @c.block.vector
        def _(v):
            v.wait_ge(c.steps_done, c.steps)
            for h in range(heads):
                last = v.tensor_scalar(out[:, t, h * dh:(h + 1) * dh], bank(4, h), total[:, h:h + 1], None,
                                       ALU.mult)
            last.then_inc(c.steps_done, 1)
        c.steps += 1


def first_block(c, a):
    h, x_t = c.h, c.x_t
    h_tiles = [h[:, t, :] for t in range(NT)]
    y = cols(c.work, 9728, NT, D)
    y_tiles = [y[:, t, :] for t in range(NT)]
    gain = [c.par[:, n * D:(n + 1) * D] for n in range(4)]
    z = c.z

    for layer in range(DEPTH):
        g = a["norm_g"][layer]

        def feed_forward(which, n_in, n_out):
            c.load(gain[0], g[n_in, :].partition_broadcast(P))
            c.load(gain[1], g[n_out, :].partition_broadcast(P))
            c.loaded()
            c.rmsnorm(h_tiles, y_tiles, gain[0])
            c.to_feature_major(lambda t, k: y[:, t, k * P:(k + 1) * P], x_t, NT)
            split_narrow(c)
            swiglu(c, a["w_ffn_gu"][layer, which], a["w_ffn_down"][layer, which], y)
            add_normed(c, h, y, gain[1], 0.5)

        feed_forward(0, 0, 1)

        vo = cols(z, 0, NT, 2 * D)
        us = cols(z, 4096, NT, 2 * D)
        xq_t = cols(z, 8192, KD, SEQ)
        gates = cols(z, 10240, NT, 3 * D)
        qk_pad = cols(z, 16384, KD, 3 + SEQ)
        w_in = a["w_in"][layer]
        i_f = cols(c.small, 0, NT, 8)
        b_if = cols(c.small, 160, 8)
        conv_w = cols(c.small, 168, KD, 4)
        conv_b = cols(c.small, 200, KD)
        c.load(gain[0], g[2, :].partition_broadcast(P))
        c.load(gain[1], a["mlstm_norm_g"][layer, :].partition_broadcast(P))
        c.load(gain[2], a["sgu_ln_g"][layer, :].partition_broadcast(P))
        c.load(gain[3], a["sgu_ln_b"][layer, :].partition_broadcast(P))
        c.load(b_if[:, 0:4], a["b_i"][layer, :].partition_broadcast(P))
        c.load(b_if[:, 4:8], a["b_f"][layer, :].partition_broadcast(P))
        c.load(conv_w, a["conv_w"][layer])
        c.load(conv_b, a["conv_b"][layer])
        c.loaded()
        c.rmsnorm(h_tiles, y_tiles, gain[0])
        c.to_feature_major(lambda t, k: y[:, t, k * P:(k + 1) * P], x_t, NT)
        split_narrow(c)

        @c.block.vector
        def _(v):
            v.wait_ge(c.steps_done, c.steps)
            v.memset(qk_pad[:, :, 0:3], 0.0).then_inc(c.steps_done, 1)
        c.steps += 1

        def feature_copies(dst, first=0):
            def place(i, n):
                return dst[:, bass.ds(i * 4 + 2 * n, 2), first:first + SEQ]
            cp = Copies(c, place, 2)
            cp.bank = lambda b: c.ps[:, b, :].rearrange("p (j t) -> p j t", t=SEQ)
            return copy_halves(c, cp)
        c.gemm_feature_major(SEQ, 2, column_units(w_in, 0), *feature_copies(qk_pad, 3))
        c.gemm_token_major(range(NT), 4, column_chunks(w_in, D), BANK, *token_copies(c, vo, range(NT)))
        c.gemm_token_major(range(NT), 1, column_chunks(w_in, 3 * D, 8), 8,
                           *token_copies(c, i_f, range(NT), 8))
        c.gemm_token_major(range(NT), 4, column_chunks(w_in, 3 * D + 8), BANK,
                           *token_copies(c, us, range(NT)))
        c.gemm_feature_major(SEQ, 2, column_units(w_in, 5 * D + 8), *feature_copies(xq_t))
        c.gemm_token_major(range(NT), 6, column_chunks(w_in, 6 * D + 8), BANK,
                           *token_copies(c, gates, range(NT)))

        qk_t = cols(c.work, 0, KD, SEQ)
        for tap in range(4):

            @c.block.vector
            def _(v):
                v.wait_ge(c.steps_done, c.steps)
                for k in range(KD):
                    src, weight = qk_pad[:, k, tap:tap + SEQ], conv_w[:, k, tap:tap + 1]
                    if tap == 0:
                        last = v.tensor_scalar(qk_t[:, k, :], src, weight, None, ALU.mult)
                    else:
                        last = v.scalar_tensor_tensor(qk_t[:, k, :], src, weight, qk_t[:, k, :],
                                                      ALU.mult, ALU.add)
                last.then_inc(c.steps_done, 1)
            c.steps += 1

        @c.block.scalar
        def _(s):
            s.wait_ge(c.steps_done, c.steps)
            for k in range(KD):
                last = s.activation(qk_t[:, k, :], qk_t[:, k, :], ACT.Silu, bias=conv_b[:, k:k + 1])
            last.then_inc(c.steps_done, 1)
        @c.block.vector
        def _(v):
            v.wait_ge(c.steps_done, c.steps)
            v.tensor_tensor(
i_f, i_f, b_if.unsqueeze(1).broadcast_to([P, NT, 8]), ALU.add).then_inc(c.steps_done, 1)
        c.steps += 2

        @c.block.scalar
        def _(s):
            s.wait_ge(c.steps_done, c.steps)
            s.activation(gates, gates, ACT.Sigmoid).then_inc(c.steps_done, 1)
        c.steps += 1
        v_tok, o_tok = vo[:, :, 0:D], vo[:, :, D:2 * D]
        mlstm(c, qk_t, v_tok, o_tok, i_f, y, gain[1])
        merged = cols(c.work, 5632, NT, D)
        branch = cols(c.work, 7680, NT, D)

        def merge(which):
            c.to_feature_major(lambda t, k: y[:, t, k * P:(k + 1) * P], x_t, NT)
            split_narrow(c)
            dst = merged if which == 0 else branch
            c.gemm_token_major(range(NT), 2, column_chunks(a["w_branch"][layer, which], 0), BANK,
                               *token_copies(c, dst, range(NT)))

            @c.block.vector
            def _(v):
                v.wait_ge(c.steps_done, c.steps)
                v.tensor_tensor(dst, dst, gates[:, :, which * D:(which + 1) * D], ALU.mult).then_inc(c.steps_done, 1)
            c.steps += 1
            if which:

                @c.block.vector
                def _(v):
                    v.wait_ge(c.steps_done, c.steps)
                    v.tensor_tensor(merged, merged, branch, ALU.add).then_inc(c.steps_done, 1)
                c.steps += 1
        merge(0)

        w_t, bias = cols(c.work, 0, 4, P), cols(c.small, 144, 4)
        c.load(w_t, a["sgu_w_s"][layer])
        c.load(bias, a["sgu_b_s"][layer])
        c.load(gain[0], g[6, :].partition_broadcast(P))
        c.load(gain[1], g[3, :].partition_broadcast(P))
        c.loaded()
        spatial_gating(c, us, y, w_t, bias, gain[2], gain[3])
        merge(1)

        mem = cols(z, 0, NT, D)
        k_t = cols(z, 2048, KD, SEQ)
        v_mem = cols(z, 4096, NT, D)
        c.load(mem, a["mem"].rearrange("o (t p) d -> p (o t) d", p=P))
        c.loaded()
        mem_tiles = [mem[:, t, :] for t in range(NT)]
        c.rmsnorm(mem_tiles, y_tiles, gain[0])
        c.to_feature_major(lambda t, k: y[:, t, k * P:(k + 1) * P], x_t, NT)
        split_narrow(c)
        w_mkv = a["w_mkv"][layer]
        c.gemm_feature_major(SEQ, 2, column_units(w_mkv, 0), *feature_copies(k_t))
        c.gemm_token_major(range(NT), 2, column_chunks(w_mkv, D), BANK, *token_copies(c, v_mem, range(NT)))
        memory_attention(c, xq_t, k_t, v_mem, y)
        merge(2)
        c.to_feature_major(lambda t, k: merged[:, t, k * P:(k + 1) * P], x_t, NT)
        split_narrow(c)
        c.gemm_token_major(range(NT), 2, column_chunks(a["w_out"][layer], 0), BANK,
                           *token_copies(c, y, range(NT)))
        add_normed(c, h, y, gain[1], 1.0)
        feed_forward(1, 4, 5)


HEADS, HD = 8, 64
RW = HEADS * HD
HYB = 3328
Q_AT = 1792
SSD_G, SSD_HEADS, SSD_P = 8, 32, 64
D_IN = 2 * D
ROWS = 2 * NT
WORK = 11776
LEVELS = 7

LAYOUTS = {
    "conv_w": lambda w: w.reshape(DEPTH, 4, KD, P).transpose(0, 3, 2, 1),
    "conv_b": lambda b: b.reshape(DEPTH, KD, P).transpose(0, 2, 1),
    "sgu_w_s": lambda w: w.transpose(0, 3, 1, 2),
    "sgu_b_s": lambda b: b.transpose(0, 2, 1),
    "c_2": lambda v: v.reshape(KD, P).T,
    "c_ctx_2": lambda v: v.reshape(KD, P).T,
    "ssd_conv_w_2": lambda w: w.reshape(5, 32, P).transpose(2, 1, 0),
    "ssd_conv_b_2": lambda b: b.reshape(32, P).T,
    "rwkv_r_k_2": lambda v: v.reshape(1, RW),
}


def shape_constants():
    j, t = np.arange(P)[:, None], np.arange(P)[None, :]
    shift = 0.5 * (abs(j - t) == 1)
    from_next = 0.5 * ((j == 0) & (t == P - 1))
    from_before = 0.5 * ((j == P - 1) & (t == 0))
    mid = P // 2
    sum_forward = 1.0 * (j <= t) - 1.0 * (j < mid)
    sum_backward = 1.0 * (j >= t) - 1.0 * (j >= mid)
    strictly_before = 1.0 * (j < t)
    halves = 1.0 * ((t == 0) & (j < mid)) + 1.0 * ((t == 1) & (j >= mid))
    merges = [1.0 * ((j >> (n + 1) == t >> (n + 1)) & (j >> n != t >> n)) for n in range(LEVELS)]
    tok = np.arange(SEQ)
    inv = np.float32(10000.0) ** (-np.arange(0, 32, 2, dtype=np.float32) / np.float32(32))
    row = (tok // 64).astype(np.float32)[:, None] * inv
    col = (tok % 64).astype(np.float32)[:, None] * inv
    cos = np.concatenate([np.cos(row), np.cos(row), np.cos(col), np.cos(col)], 1)
    sin = np.concatenate([-np.sin(row), np.sin(row), -np.sin(col), np.sin(col)], 1)
    rope = np.stack([cos, sin], 1).reshape(NT, P, 2, HD).transpose(1, 0, 2, 3)
    return {
        "shifts": np.stack([shift, from_next, from_before], 1).astype(np.float32),
        "sums": np.stack([sum_forward, sum_backward, strictly_before, halves], 1).astype(np.float32),
        "sums_before": np.stack([sum_forward - (j == t), sum_backward - (j == t)], 1).astype(np.float32),
        "merges": np.stack(merges, 1).astype(np.float32),
        "rope": rope.astype(np.float32),
    }


def modulation(c, a, layer, first, count, dst, tiles):
    spread = c.x_t[:, :, 0:SEQ]
    cond = cols(c.small, 0, 2, KD)
    c.load(cond[:, 0, :], a["c_2"])
    c.load(cond[:, 1, :], a["c_ctx_2"])
    c.loaded()

    @c.block.scalar
    def _(s):
        s.wait_ge(c.steps_done, c.steps)
        s.activation(cond, cond, ACT.Silu).then_inc(c.steps_done, 1)
    c.steps += 1

    @c.block.vector
    def _(v):
        v.wait_ge(c.steps_done, c.steps)
        for n in range(2):
            last = v.tensor_copy(spread[:, :, n * P:(n + 1) * P], cond[:, n, :].unsqueeze(2).broadcast_to([P, KD, P]))
        last.then_inc(c.steps_done, 1)
    c.steps += 1
    split_narrow(c)
    c.gemm_token_major(tiles, count, column_chunks(a["ada_w_2"][layer], first), BANK,
                       *token_copies(c, dst, tiles))


def tiles_of(x, n=NT):
    return [x[:, t, :] for t in range(n)]


def modulated_norm(c, x, out, gain, shift, scale):

    @c.block.vector
    def _(v):
        v.wait_ge(c.steps_done, c.steps)
        v.scalar_tensor_tensor(scale, scale, 1.0, gain, ALU.add, ALU.mult).then_inc(c.steps_done, 1)
    c.steps += 1
    c.rmsnorm(x, out, scale)

    @c.block.vector
    def _(v):
        v.wait_ge(c.steps_done, c.steps)
        for o in out:
            last = v.tensor_tensor(o, o, shift, ALU.add)
        last.then_inc(c.steps_done, 1)
    c.steps += 1


def heads_of(x, n=HEADS):
    if len(x.shape) == 2:
        return x.rearrange("p (h d) -> p h d", h=n)
    return x.rearrange("p t (h d) -> p t h d", h=n)


def rwkv(c, a, rows):
    ps, small, w, x_t = c.ps, c.small, c.work, cols_of(c.x_t)
    kk = cols(c.z, ROWS * HYB, ROWS, RW)
    y_all = cols(c.z, ROWS * HYB + 2048, ROWS, RW)
    low_t = cols(c.z, ROWS * HYB + 4096, ROWS, P)
    up = [cols(x_t, 3456, RW), cols(c.z, ROWS * HYB + 4608, RW)]
    merges = cols(x_t, 2560, LEVELS, P)
    state = cols(x_t, 1536, 2, HEADS, HD)[0:HD]
    inv_t = cols(x_t, 0, HEADS, P)
    u = cols(x_t, 1024, RW)
    sums_before = c.after[:, 1, :].rearrange("p (a t) -> p a t", t=P)
    sums = c.future[:, :, :].rearrange("p a (b t) -> p (a b) t", t=P)
    w0 = [c.par[:, n * RW:(n + 1) * RW] for n in range(2)]
    a0 = [c.par[:, (2 + n) * RW:(3 + n) * RW] for n in range(2)]
    k_k, k_a, r_k, g_up = (c.par[:, n * RW:(n + 1) * RW] for n in range(4, 8))

    n_mix = Q_AT
    quarter = n_mix // 4
    delta = cols(w, 0, ROWS, n_mix)
    mu = cols(w, ROWS * n_mix, n_mix)
    shifts = cols(w, ROWS * n_mix + n_mix, 3, P)
    c.load(mu, a["rwkv_mu_2"][0, :].partition_broadcast(P))
    c.load(shifts, a["shifts"])
    c.load(merges, a["merges"])
    c.load(sums, a["sums"])
    c.load(sums_before, a["sums_before"])
    for d in range(2):
        c.load(w0[d], a["rwkv_w0_2"][0, d, :].partition_broadcast(P))
        c.load(a0[d], a["rwkv_a0_2"][0, d, :].partition_broadcast(P))
        c.load(up[d][0:HD, :], a["rwkv_w_up_2"][0, d])
        c.load(up[d][HD:P, :], a["rwkv_a_up_2"][0, d])
    c.load(k_k, a["rwkv_k_k_2"][0, :].partition_broadcast(P))
    c.load(k_a, a["rwkv_k_a_2"][0, :].partition_broadcast(P))
    c.load(r_k, a["rwkv_r_k_2"][0, :].partition_broadcast(P))
    c.load(g_up, a["rwkv_g_up_2"][0])
    c.loaded()
    mixed = rows[:, :, 0:n_mix]
    for seq in range(2):

        @c.block.tensor
        def _(pe):
            pe.wait_ge(c.steps_done, c.steps)
            for t in range(NT):
                tile, other = seq * NT + t, seq * NT + 1 - t
                for q in range(4):
                    part = slice(q * quarter, (q + 1) * quarter)
                    out = ps[:, t * 4 + q, 0:quarter]
                    pe.matmul(out, shifts[:, 0, :], rows[:, tile, part], start=True, stop=False)
                    last = pe.matmul(out, shifts[:, 1 + t, :], rows[:, other, part], start=False, stop=True)
            last.then_inc(c.steps_done, 1)
        c.steps += 1

        @c.block.vector
        def _(v):
            v.wait_ge(c.steps_done, c.steps)
            for t in range(NT):
                tile = seq * NT + t
                out = delta[:, tile, :].rearrange("p (q n) -> p q n", q=4)
                last = v.tensor_tensor(out, ps[:, t * 4:t * 4 + 4, 0:quarter],
                                       rows[:, tile, 0:n_mix].rearrange("p (q n) -> p q n", q=4), ALU.subtract)
            last.then_inc(c.steps_done, 1)
        c.steps += 1

    @c.block.vector
    def _(v):
        v.wait_ge(c.steps_done, c.steps)
        v.tensor_tensor(delta, delta, mu.unsqueeze(1).broadcast_to([P, ROWS, n_mix]), ALU.mult).then_inc(c.steps_done, 1)
    c.steps += 1

    @c.block.vector
    def _(v):
        v.wait_ge(c.steps_done, c.steps)
        v.tensor_tensor(mixed, mixed, delta, ALU.add).then_inc(c.steps_done, 1)
    c.steps += 1
    r, k, v_tok = (rows[:, :, n * RW:(n + 1) * RW] for n in range(3))
    low = rows[:, :, 3 * RW:3 * RW + P]
    gd = rows[:, :, 3 * RW + P:3 * RW + 2 * P]

    square = cols(w, 0, ROWS, RW)
    ss = cols(small, 0, ROWS, HEADS)

    @c.block.vector
    def _(v):
        v.wait_ge(c.steps_done, c.steps)
        v.tensor_tensor(kk, k, k_k.unsqueeze(1).broadcast_to([P, ROWS, RW]), ALU.mult).then_inc(c.steps_done, 1)
    @c.block.scalar
    def _(s):
        s.wait_ge(c.steps_done, c.steps)
        s.activation(low[:, :, 0:HD], low[:, :, 0:HD], ACT.Tanh).then_inc(c.steps_done, 1)
    c.steps += 2

    @c.block.vector
    def _(v):
        v.wait_ge(c.steps_done, c.steps)
        v.tensor_tensor(square, kk, kk, ALU.mult).then_inc(c.steps_done, 1)
    c.steps += 1

    @c.block.vector
    def _(v):
        v.wait_ge(c.steps_done, c.steps)
        v.reduce_sum(ss, heads_of(square), AX).then_inc(c.steps_done, 1)
    c.steps += 1
    c.rstd(ss, 1.0, 1e-12)

    @c.block.vector
    def _(v):
        v.wait_ge(c.steps_done, c.steps)
        v.tensor_tensor(heads_of(kk), heads_of(kk),
                        ss.unsqueeze(3).broadcast_to([P, ROWS, HEADS, HD]), ALU.mult).then_inc(c.steps_done, 1)
    c.steps += 1
    c.transposes([([low[:, t, :] for t in range(ROWS)], low_t)])

    half_heads = HEADS // 2
    half_width = half_heads * HD
    bonus = cols(small, 32, 2, ROWS, HEADS)
    lower = cols(w, 6144, HEADS, P)
    alpha, beta, kappa, rho = (cols(w, n * RW, RW) for n in range(4))
    alpha_t, beta_t, kappa_t, rho_t = (cols(w, 2048 + n * D, HEADS, P)[0:HD] for n in range(4))
    minus_gv = cols(w, 11264, RW)
    level = cols(w, 2048, HEADS, P)
    half = cols(w, 3072, HEADS, P)
    minus_w = cols(w, 4096, HEADS, P)[0:HD]

    def over_heads(mask):
        return mask.unsqueeze(1).broadcast_to([P, half_heads, P])

    class Group:

        def __init__(self, q):
            self.q, self.chain = q, c.chains[q]
            self.heads = slice(half_heads * q, half_heads * (q + 1))
            self.columns = slice(half_width * q, half_width * (q + 1))
            place = 7168 + 2048 * q
            self.g1_t, self.g2_t, self.g3_t, self.inv = (cols(w, place + 512 * n, half_heads, P) for n in range(4))
            self.e_in, self.e_out, self.e_ex, self.lw, self.aa, self.kmod, self.t1 = (
                cols(w, place + half_width * n, half_width) for n in range(7))
            self.ends = cols(small, 96 + 8 * q, half_heads, 2)[0:HD]
            self.alpha, self.beta, self.kappa, self.rho, self.minus_gv, self.u = (
                x[:, self.columns] for x in (alpha, beta, kappa, rho, minus_gv, u))
            self.alpha_t, self.beta_t, self.kappa_t, self.rho_t, self.level, self.half, self.minus_w = (
                x[:, self.heads, :] for x in (alpha_t, beta_t, kappa_t, rho_t, level, half, minus_w))
            self.lower, self.inv_t = lower[:, self.heads, :], inv_t[:, self.heads, :]

        def bank(self, n, width=BANK, parts=P):
            return ps[0:parts, 4 * self.q + n, 0:width]

        def heads_of_bank(self, n, width=P, parts=P):
            return self.bank(n, half_heads * width, parts).rearrange("p (h t) -> p h t", t=width)

        def by_head(self, n, lhs, rhs, pe, width=P, parts=P, start=True):
            for h in range(half_heads):
                last = pe.matmul(self.heads_of_bank(n, width, parts)[:, h, :], lhs(h), rhs(h), start=start,
                                 stop=True, skip_group_check=not start)
            return last

    def head(x, h):
        return x[:, h * HD:(h + 1) * HD]

    groups = [Group(q) for q in range(2)]

    def flat(x):
        return x.rearrange("p h t -> p (h t)")

    def chunk(d, tile, first_of_scan, first_of_tile):
        strict, strict_t, incl_t = ((c.after[:, 0, 0:P], sums[:, 2, :], c.upto[:, :]) if d == 0 else
                                    (sums[:, 2, :], c.after[:, 0, 0:P], c.onward[:, :]))
        for g in groups:
            ch = g.chain

            @ch.block.tensor
            def _(pe):
                pe.wait_ge(ch.steps_done, ch.steps)
                pe.matmul(g.bank(0, half_width), low_t[0:HD, tile, :], up[d][0:HD, g.columns], start=True, stop=True)
                pe.matmul(g.bank(1, half_width), low_t[HD:P, tile, :], up[d][HD:P, g.columns],
                          start=True, stop=True).then_inc(ch.steps_done, 1)
            ch.steps += 1
        for g in groups:
            ch = g.chain

            @ch.block.vector
            def _(v):
                v.wait_ge(ch.steps_done, ch.steps)
                v.tensor_tensor(g.lw, g.bank(0, half_width), w0[d][:, g.columns], ALU.add)
                v.tensor_tensor(g.aa, g.bank(1, half_width), a0[d][:, g.columns], ALU.add).then_inc(ch.steps_done, 1)
            ch.steps += 1
        for g in groups:
            ch = g.chain


            @ch.block.scalar
            def _(s):
                s.wait_ge(ch.steps_done, ch.steps)
                s.activation(g.lw, g.lw, ACT.Sigmoid)
                s.activation(g.aa, g.aa, ACT.Sigmoid).then_inc(ch.steps_done, 1)
            ch.steps += 1
        for g in groups:
            ch = g.chain

            @ch.block.vector
            def _(v):
                v.wait_ge(ch.steps_done, ch.steps)
                v.tensor_scalar(g.lw, g.lw, -math.exp(-0.5), None, ALU.mult)
                v.tensor_tensor(g.beta, kk[:, tile, g.columns], g.aa, ALU.mult)
                v.scalar_tensor_tensor(g.t1, g.aa, -1.0, k_a[:, g.columns], ALU.add, ALU.mult).then_inc(ch.steps_done, 1)
            ch.steps += 1
        for g in groups:
            ch = g.chain

            @ch.block.tensor
            def _(pe):
                pe.wait_ge(ch.steps_done, ch.steps)
                pe.matmul(g.bank(0, half_width), sums[:, d, :], g.lw, start=True, stop=True)
                pe.matmul(g.bank(2, half_width), sums_before[:, d, :], g.lw, start=True, stop=True)
                for h in range(half_heads):
                    last = pe.matmul(g.bank(3, 8, HD)[:, 2 * h:2 * h + 2], head(g.lw, h), sums[:, 3, 0:2],
                                     start=True, stop=True)
                last.then_inc(ch.steps_done, 1)
            @ch.block.vector
            def _(v):
                v.wait_ge(ch.steps_done, ch.steps)
                v.scalar_tensor_tensor(
g.kmod, g.t1, 1.0, k[:, tile, g.columns], ALU.add, ALU.mult).then_inc(ch.steps_done, 1)
            ch.steps += 2
        for g in groups:
            ch = g.chain

            @ch.block.scalar
            def _(s):
                s.wait_ge(ch.steps_done, ch.steps)
                s.activation(g.e_in, g.bank(0, half_width), ACT.Exp)
                s.activation(g.e_out, g.bank(0, half_width), ACT.Exp, scale=-1.0)
                s.activation(g.e_ex, g.bank(2, half_width), ACT.Exp)
                s.activation(g.ends, g.heads_of_bank(3, 2, HD), ACT.Exp).then_inc(ch.steps_done, 1)
            @ch.block.vector
            def _(v):
                v.wait_ge(ch.steps_done, ch.steps)
                v.tensor_tensor(g.t1, g.kmod, r_k[:, g.columns], ALU.mult).then_inc(ch.steps_done, 1)
            ch.steps += 2
        for g in groups:
            ch = g.chain

            @ch.block.vector
            def _(v):
                v.wait_ge(ch.steps_done, ch.steps)
                v.tensor_tensor(g.alpha, kk[:, tile, g.columns], g.e_ex, ALU.mult)
                v.tensor_tensor(g.beta, g.beta, g.e_out, ALU.mult)
                v.tensor_tensor(g.kappa, g.kmod, g.e_out, ALU.mult)
                v.tensor_tensor(g.rho, r[:, tile, g.columns], g.e_in, ALU.mult)
                v.tensor_tensor(g.t1, g.t1, r[:, tile, g.columns], ALU.mult).then_inc(ch.steps_done, 1)
            ch.steps += 1
        for g in groups:
            ch = g.chain

            @ch.block.tensor
            def _(pe):
                pe.wait_ge(ch.steps_done, ch.steps)
                for n, src in enumerate((g.alpha, g.beta, g.kappa, g.rho)):
                    for h in range(half_heads):
                        last = pe.transpose(g.heads_of_bank(n, P, HD)[:, h, :], head(src, h), c.ident[:, :])
                last.then_inc(ch.steps_done, 1)
            @ch.block.vector
            def _(v):
                v.wait_ge(ch.steps_done, ch.steps)
                v.reduce_sum(
bonus[:, d, tile, g.heads], heads_of(g.t1, half_heads), AX).then_inc(ch.steps_done, 1)
            ch.steps += 2
        for g in groups:
            ch = g.chain

            @ch.block.scalar
            def _(s):
                s.wait_ge(ch.steps_done, ch.steps)
                s.activation(g.alpha_t, g.heads_of_bank(0, P, HD), ACT.Copy)
                s.activation(g.kappa_t, g.heads_of_bank(2, P, HD), ACT.Copy).then_inc(ch.steps_done, 1)
            @ch.block.vector
            def _(v):
                v.wait_ge(ch.steps_done, ch.steps)
                v.tensor_copy(g.beta_t, g.heads_of_bank(1, P, HD))
                v.tensor_copy(g.rho_t, g.heads_of_bank(3, P, HD)).then_inc(ch.steps_done, 1)
            ch.steps += 2
        for g in groups:
            ch = g.chain

            @ch.block.tensor
            def _(pe):
                pe.wait_ge(ch.steps_done, ch.steps)
                g.by_head(0, lambda h: g.alpha_t[:, h, :], lambda h: g.beta_t[:, h, :], pe).then_inc(ch.steps_done, 1)
            ch.steps += 1
        for g in groups:
            ch = g.chain

            @ch.block.tensor
            def _(pe):
                pe.wait_ge(ch.steps_done, ch.steps)
                g.by_head(1, lambda h: g.kappa_t[:, h, :], lambda h: g.alpha_t[:, h, :], pe)
                g.by_head(2, lambda h: g.beta_t[:, h, :], lambda h: g.rho_t[:, h, :], pe)
                g.by_head(3, lambda h: g.kappa_t[:, h, :], lambda h: g.rho_t[:, h, :], pe).then_inc(ch.steps_done, 1)
            @ch.block.vector
            def _(v):
                v.wait_ge(ch.steps_done, ch.steps)
                v.tensor_tensor(
g.lower, g.heads_of_bank(0), over_heads(strict), ALU.mult).then_inc(ch.steps_done, 1)
            ch.steps += 2

        for g in groups:
            ch = g.chain

            @ch.block.vector
            def _(v):
                v.wait_ge(ch.steps_done, ch.steps)
                v.tensor_tensor(g.level, g.lower, over_heads(merges[:, 0, :]), ALU.mult)
                v.tensor_tensor(g.g1_t, g.heads_of_bank(1), over_heads(strict_t), ALU.mult).then_inc(ch.steps_done, 1)
            ch.steps += 1
        for g in groups:
            ch = g.chain

            @ch.block.tensor
            def _(pe):
                pe.wait_ge(ch.steps_done, ch.steps)
                g.by_head(0, lambda h: g.level[:, h, :], lambda h: c.ident[:, :], pe)
                g.by_head(1, lambda h: g.g1_t[:, h, :], lambda h: head(v_tok[:, tile, g.columns], h), pe,
                          width=HD).then_inc(ch.steps_done, 1)
            @ch.block.vector
            def _(v):
                v.wait_ge(ch.steps_done, ch.steps)
                v.tensor_tensor(
g.g2_t, g.heads_of_bank(2), over_heads(incl_t), ALU.mult).then_inc(ch.steps_done, 1)
            ch.steps += 2
        for g in groups:
            ch = g.chain

            @ch.block.vector
            def _(v):
                v.wait_ge(ch.steps_done, ch.steps)
                v.tensor_tensor(g.inv, over_heads(c.ident[:, :]), g.level, ALU.subtract)
                v.tensor_tensor(g.inv_t, over_heads(c.ident[:, :]), g.heads_of_bank(0), ALU.subtract).then_inc(ch.steps_done, 1)
            @ch.block.scalar
            def _(s):
                s.wait_ge(ch.steps_done, ch.steps)
                s.mul(g.minus_gv, g.bank(1, half_width), -1.0).then_inc(ch.steps_done, 1)
            ch.steps += 2
        for g in groups:
            ch = g.chain


            @ch.block.tensor
            def _(pe):
                pe.wait_ge(ch.steps_done, ch.steps)
                pe.matmul(g.bank(1), c.ident[:, :], flat(g.inv), start=True, stop=True)
                pe.matmul(g.bank(2), c.ident[:, :], flat(g.inv_t), start=True, stop=True).then_inc(ch.steps_done, 1)
            @ch.block.vector
            def _(v):
                v.wait_ge(ch.steps_done, ch.steps)
                v.tensor_tensor(g.level, g.lower, over_heads(merges[:, 1, :]), ALU.mult)
                v.tensor_tensor(g.g3_t, g.heads_of_bank(3), over_heads(incl_t), ALU.mult).then_inc(ch.steps_done, 1)
            ch.steps += 2
        for n in range(1, LEVELS):
            for g in groups:
                ch = g.chain

                @ch.block.tensor
                def _(pe):
                    pe.wait_ge(ch.steps_done, ch.steps)
                    g.by_head(0, lambda h: g.level[:, h, :], lambda h: g.inv_t[:, h, :], pe).then_inc(ch.steps_done, 1)
                ch.steps += 1
            for g in groups:
                ch = g.chain

                @ch.block.scalar
                def _(s):
                    s.wait_ge(ch.steps_done, ch.steps)
                    s.mul(flat(g.half), g.bank(0), -1.0).then_inc(ch.steps_done, 1)
                ch.steps += 1
            if n < LEVELS - 1:
                for g in groups:
                    ch = g.chain

                    @ch.block.tensor
                    def _(pe):
                        pe.wait_ge(ch.steps_done, ch.steps)
                        g.by_head(2, lambda h: g.inv[:, h, :], lambda h: g.half[:, h, :], pe, start=False)
                        g.by_head(1, lambda h: g.half[:, h, :], lambda h: g.inv[:, h, :], pe, start=False).then_inc(ch.steps_done, 1)
                    @ch.block.vector
                    def _(v):
                        v.wait_ge(ch.steps_done, ch.steps)
                        v.tensor_tensor(
g.level, g.lower, over_heads(merges[:, n + 1, :]), ALU.mult).then_inc(ch.steps_done, 1)
                    ch.steps += 2
                for g in groups:
                    ch = g.chain

                    @ch.block.scalar
                    def _(s):
                        s.wait_ge(ch.steps_done, ch.steps)
                        s.activation(flat(g.inv_t), g.bank(2), ACT.Copy).then_inc(ch.steps_done, 1)
                    @ch.block.vector
                    def _(v):
                        v.wait_ge(ch.steps_done, ch.steps)
                        v.tensor_copy(flat(g.inv), g.bank(1)).then_inc(ch.steps_done, 1)
                    ch.steps += 2
            else:
                for g in groups:
                    ch = g.chain

                    @ch.block.tensor
                    def _(pe):
                        pe.wait_ge(ch.steps_done, ch.steps)
                        g.by_head(2, lambda h: g.inv[:, h, :], lambda h: g.half[:, h, :], pe,
                                  start=False).then_inc(ch.steps_done, 1)
                    ch.steps += 1
                for g in groups:
                    ch = g.chain

                    @ch.block.scalar
                    def _(s):
                        s.wait_ge(ch.steps_done, ch.steps)
                        s.activation(flat(g.inv_t), g.bank(2), ACT.Copy).then_inc(ch.steps_done, 1)
                    ch.steps += 1

        for g in groups:
            ch = g.chain
            before, starts = state[:, d, g.heads, :], g.ends[:, :, d:d + 1]
            if first_of_scan:

                @ch.block.tensor
                def _(pe):
                    pe.wait_ge(ch.steps_done, ch.steps)
                    g.by_head(0, lambda h: head(g.alpha, h), lambda h: g.inv_t[:, h, :], pe,
                              parts=HD).then_inc(ch.steps_done, 1)
                ch.steps += 1
            else:

                @ch.block.tensor
                def _(pe):
                    pe.wait_ge(ch.steps_done, ch.steps)
                    g.by_head(0, lambda h: head(g.alpha, h), lambda h: g.inv_t[:, h, :], pe,
                              parts=HD).then_inc(ch.steps_done, 1)
                @ch.block.vector
                def _(v):
                    v.wait_ge(ch.steps_done, ch.steps)
                    v.tensor_tensor(before, before,
                                    starts.broadcast_to([HD, half_heads, HD]), ALU.mult).then_inc(ch.steps_done, 1)
                ch.steps += 2
        for g in groups:
            ch = g.chain

            @ch.block.scalar
            def _(s):
                s.wait_ge(ch.steps_done, ch.steps)
                s.mul(g.minus_w, g.heads_of_bank(0, P, HD), -1.0).then_inc(ch.steps_done, 1)
            ch.steps += 1
        for g in groups:
            ch = g.chain
            before = state[:, d, g.heads, :]

            @ch.block.tensor
            def _(pe):
                pe.wait_ge(ch.steps_done, ch.steps)
                for h in range(half_heads):
                    out = head(g.bank(3), h)
                    last = pe.matmul(out, g.inv_t[:, h, :], head(g.minus_gv, h), start=True, stop=first_of_scan)
                    if not first_of_scan:
                        last = pe.matmul(out, g.minus_w[:, h, :], before[:, h, :], start=False, stop=True)
                last.then_inc(ch.steps_done, 1)
            ch.steps += 1
        for g in groups:
            ch = g.chain

            @ch.block.scalar
            def _(s):
                s.wait_ge(ch.steps_done, ch.steps)
                s.activation(g.u, g.bank(3, half_width), ACT.Copy).then_inc(ch.steps_done, 1)
            ch.steps += 1
        for g in groups:
            ch = g.chain
            before = state[:, d, g.heads, :]

            @ch.block.tensor
            def _(pe):
                pe.wait_ge(ch.steps_done, ch.steps)
                values = v_tok[:, tile, g.columns]
                for h in range(half_heads):
                    out = head(g.bank(0), h)
                    if not first_of_scan:
                        pe.matmul(out, g.rho_t[:, h, :], before[:, h, :], start=True, stop=False)
                    pe.matmul(out, g.g2_t[:, h, :], head(g.u, h), start=first_of_scan, stop=False)
                    pe.matmul(out, g.g3_t[:, h, :], head(values, h), start=False, stop=True)
                for h in range(half_heads):
                    out = head(g.bank(1, BANK, HD), h)
                    pe.matmul(out, head(g.beta, h), head(g.u, h), start=True, stop=False)
                    last = pe.matmul(out, head(g.kappa, h), head(values, h), start=False, stop=True)
                last.then_inc(ch.steps_done, 1)
            ch.steps += 1
        for g in groups:
            ch = g.chain
            before, ending = state[:, d, g.heads, :], g.ends[:, :, 1 - d:2 - d]
            gained = g.heads_of_bank(1, HD, HD)
            y_g = y_all[:, tile, g.columns]

            @ch.block.vector
            def _(v):
                v.wait_ge(ch.steps_done, ch.steps)
                if first_of_tile:
                    v.tensor_copy(y_g, g.bank(0, half_width))
                else:
                    v.tensor_tensor(y_g, y_g, g.bank(0, half_width), ALU.add)
                if first_of_scan:
                    v.tensor_tensor(before, gained, ending.broadcast_to([HD, half_heads, HD]), ALU.mult).then_inc(ch.steps_done, 1)
                    return
                v.tensor_tensor(before, before, gained, ALU.add).then_inc(ch.steps_done, 1)
            ch.steps += 1
            if not first_of_scan:

                @ch.block.vector
                def _(v):
                    v.wait_ge(ch.steps_done, ch.steps)
                    v.tensor_tensor(before, before, ending.broadcast_to([HD, half_heads, HD]),
                                    ALU.mult).then_inc(ch.steps_done, 1)
                ch.steps += 1

    c.begin_chains()
    for d, order in enumerate(((2, 3, 0, 1), (3, 2, 1, 0))):
        for n, tile in enumerate(order):
            chunk(d, tile, n == 0, d == 0)
    c.end_chains()

    ln_w, ln_b = k_k, k_a
    c.load(ln_w, a["rwkv_ln_w_2"][0, :].partition_broadcast(P))
    c.load(ln_b, a["rwkv_ln_b_2"][0, :].partition_broadcast(P))
    c.loaded()
    y_h = heads_of(y_all)
    gd_t = cols(w, 2048, ROWS, P)

    def over_width(x):
        return x.unsqueeze(3).broadcast_to([P, ROWS, HEADS, HD])

    def over_rows(x):
        return x.unsqueeze(1).broadcast_to([P, ROWS, RW])

    @c.block.vector
    def _(v):
        v.wait_ge(c.steps_done, c.steps)
        v.reduce_sum(ss, y_h, AX).then_inc(c.steps_done, 1)
    @c.block.scalar
    def _(s):
        s.wait_ge(c.steps_done, c.steps)
        s.activation(gd, gd, ACT.Sigmoid).then_inc(c.steps_done, 1)
    c.steps += 2

    @c.block.vector
    def _(v):
        v.wait_ge(c.steps_done, c.steps)
        v.tensor_scalar(ss, ss, 1.0 / HD, None, ALU.mult).then_inc(c.steps_done, 1)
    c.steps += 1

    @c.block.vector
    def _(v):
        v.wait_ge(c.steps_done, c.steps)
        v.tensor_tensor(y_h, y_h, over_width(ss), ALU.subtract).then_inc(c.steps_done, 1)
    c.steps += 1

    @c.block.vector
    def _(v):
        v.wait_ge(c.steps_done, c.steps)
        v.tensor_tensor(square, y_all, y_all, ALU.mult).then_inc(c.steps_done, 1)
    c.steps += 1

    @c.block.vector
    def _(v):
        v.wait_ge(c.steps_done, c.steps)
        v.reduce_sum(ss, heads_of(square), AX).then_inc(c.steps_done, 1)
    c.steps += 1
    c.rstd(ss, 1.0 / HD, 64e-5)
    c.transposes([([gd[:, t, :] for t in range(ROWS)], gd_t)])

    @c.block.tensor
    def _(pe):
        pe.wait_ge(c.steps_done, c.steps)
        for t in range(ROWS):
            last = pe.matmul(ps[:, t, :], gd_t[:, t, :], g_up, start=True, stop=True)
        last.then_inc(c.steps_done, 1)
    @c.block.vector
    def _(v):
        v.wait_ge(c.steps_done, c.steps)
        v.tensor_tensor(y_h, y_h, over_width(ss), ALU.mult).then_inc(c.steps_done, 1)
    c.steps += 2

    @c.block.vector
    def _(v):
        v.wait_ge(c.steps_done, c.steps)
        v.tensor_tensor(y_all, y_all, over_rows(ln_w), ALU.mult).then_inc(c.steps_done, 1)
    c.steps += 1

    @c.block.vector
    def _(v):
        v.wait_ge(c.steps_done, c.steps)
        v.tensor_tensor(bonus[:, 0], bonus[:, 0], bonus[:, 1], ALU.add).then_inc(c.steps_done, 1)
    c.steps += 1

    @c.block.vector
    def _(v):
        v.wait_ge(c.steps_done, c.steps)
        v.tensor_scalar(bonus[:, 0], bonus[:, 0], 0.5, None, ALU.mult).then_inc(c.steps_done, 1)
    c.steps += 1

    @c.block.vector
    def _(v):
        v.wait_ge(c.steps_done, c.steps)
        v.tensor_tensor(y_all, y_all, over_rows(ln_b), ALU.add).then_inc(c.steps_done, 1)
    c.steps += 1

    @c.block.vector
    def _(v):
        v.wait_ge(c.steps_done, c.steps)
        v.tensor_tensor(heads_of(square), heads_of(v_tok), over_width(bonus[:, 0]), ALU.mult).then_inc(c.steps_done, 1)
    c.steps += 1

    @c.block.vector
    def _(v):
        v.wait_ge(c.steps_done, c.steps)
        v.tensor_tensor(y_all, y_all, square, ALU.add).then_inc(c.steps_done, 1)
    c.steps += 1

    @c.block.vector
    def _(v):
        v.wait_ge(c.steps_done, c.steps)
        v.tensor_tensor(y_all, y_all, ps[:, 0:ROWS, :], ALU.mult).then_inc(c.steps_done, 1)
    c.steps += 1
    return y_all


def cols_of(buf):
    return buf[:, :, :].rearrange("p a b -> p (a b)")


def differential_attention(c, a, rows):
    lam_init = 0.8 - 0.6 * math.exp(-0.3 * 0)
    scale = HD ** -0.5
    ps, small, w, x_t = c.ps, c.small, c.work, cols_of(c.x_t)
    q, k, v_tok = (rows[:, :, Q_AT + n * RW:Q_AT + (n + 1) * RW] for n in range(3))
    qr_t, qp_t, qc_t, kr_t, kc_t = (cols(w, n * 2048, HEADS, SEQ)[0:HD] for n in range(5))
    q_rot, k_rot, swapped = cols(x_t, 0, NT, RW), cols(x_t, 1024, NT, RW), cols(x_t, 2048, NT, RW)
    rope = cols(x_t, 3072, NT, 2, HD)
    lq = cols(small, 256, 4, HD)
    sub_g = cols(c.par, 0, P)
    for n, name in enumerate(("diff_lq1_2", "diff_lk1_2", "diff_lq2_2", "diff_lk2_2")):
        c.load(lq[:, n, :], a[name][0, :].partition_broadcast(P))
    c.load(rope, a["rope"])
    c.load(sub_g, a["diff_subln_g_2"][0, :].partition_broadcast(P))
    c.loaded()
    lam2 = cols(small, 0, 2)
    lam = cols(small, 2, 1)

    @c.block.vector
    def _(v):
        v.wait_ge(c.steps_done, c.steps)
        v.tensor_tensor(lq[:, 0:4:2, :], lq[:, 0:4:2, :], lq[:, 1:4:2, :], ALU.mult).then_inc(c.steps_done, 1)
    c.steps += 1

    @c.block.vector
    def _(v):
        v.wait_ge(c.steps_done, c.steps)
        v.reduce_sum(lam2, lq[:, 0:4:2, :], AX).then_inc(c.steps_done, 1)
    c.steps += 1

    @c.block.scalar
    def _(s):
        s.wait_ge(c.steps_done, c.steps)
        s.activation(lam2, lam2, ACT.Exp).then_inc(c.steps_done, 1)
    c.steps += 1

    @c.block.vector
    def _(v):
        v.wait_ge(c.steps_done, c.steps)
        v.tensor_tensor(lam, lam2[:, 0:1], lam2[:, 1:2], ALU.subtract).then_inc(c.steps_done, 1)
    c.steps += 1

    @c.block.vector
    def _(v):
        v.wait_ge(c.steps_done, c.steps)
        v.tensor_scalar(lam, lam, -1.0, -lam_init, ALU.mult, ALU.add).then_inc(c.steps_done, 1)
    c.steps += 1

    for src, dst in ((q, q_rot), (k, k_rot)):
        for t in range(NT):
            x = src[:, t, :].rearrange("p (b s i) -> p b s i", s=2, i=16)
            sw = swapped[:, t, :].rearrange("p (b s i) -> p b s i", s=2, i=16)
            cos = rope[:, t, 0:1, :].broadcast_to([P, HEADS, HD])
            sin = rope[:, t, 1:2, :].broadcast_to([P, HEADS, HD])
            x_h, d_h, s_h = heads_of(src[:, t, :]), heads_of(dst[:, t, :]), heads_of(swapped[:, t, :])

            @c.block.vector
            def _(v):
                v.wait_ge(c.steps_done, c.steps)
                v.tensor_copy(sw[:, :, 0, :], x[:, :, 1, :])
                v.tensor_copy(sw[:, :, 1, :], x[:, :, 0, :])
                v.tensor_tensor(d_h, x_h, cos, ALU.mult).then_inc(c.steps_done, 1)
            c.steps += 1

            @c.block.vector
            def _(v):
                v.wait_ge(c.steps_done, c.steps)
                v.tensor_tensor(s_h, s_h, sin, ALU.mult).then_inc(c.steps_done, 1)
            c.steps += 1

            @c.block.vector
            def _(v):
                v.wait_ge(c.steps_done, c.steps)
                v.tensor_tensor(dst[:, t, :], dst[:, t, :], swapped[:, t, :], ALU.add).then_inc(c.steps_done, 1)
            c.steps += 1

    c.transposes([([src(t)[:, (b + j) * HD:(b + j + 1) * HD] for j in range(4)],
                   dst[:, b:b + 4, t * P:(t + 1) * P])
                  for src, dst in ((lambda t: q_rot[:, t, :], qr_t), (lambda t: q[:, t, :], qp_t),
                                   (lambda t: q[:, NT + t, :], qc_t), (lambda t: k_rot[:, t, :], kr_t),
                                   (lambda t: k[:, NT + t, :], kc_t))
                  for t in range(NT) for b in (0, 4)])

    p_all = cols(x_t, 0, HEADS, 2 * SEQ)
    heads = HEADS // 2
    p_t = cols(c.z, ROWS * HYB, heads, ROWS, P)
    mx, total = cols(small, 8, HEADS), cols(small, 16, HEADS)
    mx2, total2 = mx, total
    for tile in range(ROWS):
        main = tile < NT
        tokens = slice(tile % NT * P, (tile % NT + 1) * P)
        keys = ROWS if main else NT
        n = keys * P
        first = 0 if main else NT

        @c.block.tensor
        def _(pe):
            pe.wait_ge(c.steps_done, c.steps)
            for b in range(HEADS):
                if main:
                    pe.matmul(ps[:, b, 0:SEQ], qr_t[:, b, tokens], kr_t[:, b, :], start=True, stop=True)
                    last = pe.matmul(ps[:, b, SEQ:2 * SEQ], qp_t[:, b, tokens], kc_t[:, b, :],
                                     start=True, stop=True)
                else:
                    last = pe.matmul(ps[:, b, 0:SEQ], qc_t[:, b, tokens], kc_t[:, b, :], start=True, stop=True)
            last.then_inc(c.steps_done, 1)
        c.steps += 1

        @c.block.vector
        def _(v):
            v.wait_ge(c.steps_done, c.steps)
            v.reduce_max(mx, ps[:, :, 0:n], AX).then_inc(c.steps_done, 1)
        c.steps += 1

        @c.block.vector
        def _(v):
            v.wait_ge(c.steps_done, c.steps)
            v.tensor_scalar(mx, mx, -scale, None, ALU.mult).then_inc(c.steps_done, 1)
        c.steps += 1

        @c.block.scalar
        def _(s):
            s.wait_ge(c.steps_done, c.steps)
            for b in range(HEADS):
                last = s.activation(p_all[:, b, 0:n], ps[:, b, 0:n], ACT.Exp, bias=mx[:, b:b + 1], scale=scale,
                                    accum_out=total[:, b:b + 1])
            last.then_inc(c.steps_done, 1)
        c.steps += 1

        @c.block.vector
        def _(v):
            v.wait_ge(c.steps_done, c.steps)
            v.reciprocal(total, total).then_inc(c.steps_done, 1)
        c.steps += 1
        pairs = total.rearrange("p (h m) -> p h m", m=2)

        @c.block.vector
        def _(v):
            v.wait_ge(c.steps_done, c.steps)
            v.tensor_scalar(pairs[:, :, 1], pairs[:, :, 1], lam, None, ALU.mult).then_inc(c.steps_done, 1)
        c.steps += 1

        @c.block.vector
        def _(v):
            v.wait_ge(c.steps_done, c.steps)
            for h in range(heads):
                last = v.tensor_scalar(p_all[:, 2 * h, 0:n], p_all[:, 2 * h, 0:n], total[:, 2 * h:2 * h + 1],
                                       None, ALU.mult)
            last.then_inc(c.steps_done, 1)
        c.steps += 1

        @c.block.vector
        def _(v):
            v.wait_ge(c.steps_done, c.steps)
            for h in range(heads):
                last = v.scalar_tensor_tensor(p_all[:, 2 * h, 0:n], p_all[:, 2 * h + 1, 0:n],
                                              total[:, 2 * h + 1:2 * h + 2], p_all[:, 2 * h, 0:n],
                                              ALU.mult, ALU.add)
            last.then_inc(c.steps_done, 1)
        c.steps += 1
        c.transposes([([p_all[:, 2 * h, j * P:(j + 1) * P] for j in range(keys)], p_t[:, h, 0:keys, :])
                      for h in range(heads)])

        @c.block.tensor
        def _(pe):
            pe.wait_ge(c.steps_done, c.steps)
            for h in range(heads):
                for j in range(keys):
                    last = pe.matmul(ps[:, 4, h * P:(h + 1) * P], p_t[:, h, j, :],
                                     v_tok[:, first + j, h * P:(h + 1) * P], start=(j == 0), stop=(j == keys - 1))
            last.then_inc(c.steps_done, 1)
        c.steps += 1

        @c.block.vector
        def _(v):
            v.wait_ge(c.steps_done, c.steps)
            v.tensor_copy(q[:, tile, :], ps[:, 4, :]).then_inc(c.steps_done, 1)
        c.steps += 1

    square = cols(w, 0, ROWS, RW)
    ss = cols(small, 32, ROWS, heads)
    q_h = heads_of(q, heads)

    @c.block.vector
    def _(v):
        v.wait_ge(c.steps_done, c.steps)
        v.tensor_tensor(square, q, q, ALU.mult).then_inc(c.steps_done, 1)
    c.steps += 1

    @c.block.vector
    def _(v):
        v.wait_ge(c.steps_done, c.steps)
        v.reduce_sum(ss, heads_of(square, heads), AX).then_inc(c.steps_done, 1)
    c.steps += 1
    c.rstd(ss, 1.0 / P, EPS)

    @c.block.vector
    def _(v):
        v.wait_ge(c.steps_done, c.steps)
        v.tensor_scalar(ss, ss, 1.0 - lam_init, None, ALU.mult).then_inc(c.steps_done, 1)
    c.steps += 1

    @c.block.vector
    def _(v):
        v.wait_ge(c.steps_done, c.steps)
        v.tensor_tensor(q_h, q_h, ss.unsqueeze(3).broadcast_to([P, ROWS, heads, P]), ALU.mult).then_inc(c.steps_done, 1)
    c.steps += 1
    for t in range(ROWS):

        @c.block.vector
        def _(v):
            v.wait_ge(c.steps_done, c.steps)
            v.tensor_tensor(q_h[:, t], q_h[:, t], sub_g.unsqueeze(1).broadcast_to([P, heads, P]),
                            ALU.mult).then_inc(c.steps_done, 1)
        c.steps += 1
    return q


def hybrid_mixer(c, a, out):
    rows = cols(c.z, 0, ROWS, HYB)
    c.gemm_token_major(range(ROWS), 6, column_chunks(a["hy_w_in_2"][0], 0), BANK,
                       *token_copies(c, rows, range(ROWS)))
    n = HYB - 6 * BANK
    c.gemm_token_major(range(ROWS), 1, column_chunks(a["hy_w_in_2"][0], 6 * BANK, n), n,
                       *token_copies(c, rows[:, :, 6 * BANK:], range(ROWS), n))
    y = rwkv(c, a, rows)
    o = differential_attention(c, a, rows)
    c.to_feature_major(lambda t, k: y[:, t, k * P:(k + 1) * P] if k < 4 else o[:, t, (k - 4) * P:(k - 3) * P],
                       c.x_t, ROWS)
    split_wide(c, ROWS * P)
    c.gemm_token_major(range(ROWS), 2, column_chunks(a["hy_w_out_2"][0], 0), BANK,
                       *token_copies(c, out, range(ROWS)))


def ssd_mixer(c, a, out):
    ps, small, w = c.ps, c.small, c.work
    x_t = c.x_t
    xs = cols(c.z, 0, ROWS, D_IN)
    b_tok = cols(c.z, 8192, ROWS, D)
    b_t = cols(c.z, 12288, SSD_G, SEQ)
    c_t = cols(c.z, 14336, SSD_G, SEQ)
    z = cols(w, 0, NT, D_IN)
    pad = cols(w, 0, 4, 2, SEQ + 4)
    conv = cols(w, 2080, 4, 2, SEQ)
    w_in = a["ssd_w_in_2"][0]
    taps = cols(c.par, 0, 32, 5)
    conv_b = cols(c.par, 160, 32)
    dt_bias = cols(c.par, 192, 2, SSD_HEADS)
    decay_rate = cols(c.par, 256, 2, SSD_HEADS)
    d_skip = cols(c.par, 320, SSD_HEADS)
    dt_raw = cols(small, 0, ROWS, SSD_HEADS)
    c.load(taps, a["ssd_conv_w_2"])
    c.load(conv_b, a["ssd_conv_b_2"])
    for d in range(2):
        c.load(dt_bias[:, d, :], a["ssd_dt_bias_2"][0, d, :].partition_broadcast(P))
        c.load(decay_rate[:, d, :], a["ssd_a_log_2"][0, d, :].partition_broadcast(P))
    c.load(d_skip, a["ssd_d_2"][0, :].partition_broadcast(P))
    c.loaded()

    @c.block.vector
    def _(v):
        v.wait_ge(c.steps_done, c.steps)
        v.memset(pad, 0.0).then_inc(c.steps_done, 1)
    c.steps += 1
    for i in range(8):
        seqs = 2 if i < 6 else 1
        tokens = seqs * SEQ
        per_bank = BANK // tokens

        def place(_, n):
            return pad[:, n * per_bank:(n + 1) * per_bank, 0:seqs, 2:2 + SEQ]
        cp = Copies(c, place, 4 // per_bank)
        cp.bank = lambda b: ps[:, b, :].rearrange("p (g s t) -> p g s t", g=per_bank, s=seqs)
        c.gemm_feature_major(tokens, 1, column_units(w_in, D_IN + i * BANK), *copy_halves(c, cp))
        for tap in range(5):

            @c.block.vector
            def _(v):
                v.wait_ge(c.steps_done, c.steps)
                for g in range(4):
                    src, weight = pad[:, g, 0:seqs, tap:tap + SEQ], taps[:, i * 4 + g, tap:tap + 1]
                    dst = conv[:, g, 0:seqs, :]
                    if tap == 0:
                        last = v.tensor_scalar(dst, src, weight, None, ALU.mult)
                    else:
                        last = v.scalar_tensor_tensor(dst, src, weight, dst, ALU.mult, ALU.add)
                last.then_inc(c.steps_done, 1)
            c.steps += 1

        @c.block.scalar
        def _(s):
            s.wait_ge(c.steps_done, c.steps)
            for g in range(4):
                ch = i * 4 + g
                dst = conv[:, g, 0:seqs, :] if i < 6 else c_t[:, (i - 6) * 4 + g, :].unsqueeze(1)
                last = s.activation(dst, conv[:, g, 0:seqs, :], ACT.Silu, bias=conv_b[:, ch:ch + 1])
            last.then_inc(c.steps_done, 1)
        c.steps += 1
        if i in (4, 5):

            @c.block.vector
            def _(v):
                v.wait_ge(c.steps_done, c.steps)
                v.tensor_copy(b_t[:, (i - 4) * 4:(i - 3) * 4, :], conv[:, :, 0, :]).then_inc(c.steps_done, 1)
            c.steps += 1
        if i < 6:
            dst, at = (xs, i * BANK) if i < 4 else (b_tok, (i - 4) * BANK)
            c.transposes([([conv[:, g, t // NT, t % NT * P:(t % NT + 1) * P] for g in range(4)],
                           dst[:, t, at:at + BANK].rearrange("p (g n) -> p g n", g=4)) for t in range(ROWS)])
    c.gemm_token_major(range(ROWS), 1, column_chunks(w_in, 6144, SSD_HEADS), SSD_HEADS,
                       *token_copies(c, dt_raw, range(ROWS), SSD_HEADS))
    c.gemm_token_major(range(NT), 4, column_chunks(w_in, 0), BANK, *token_copies(c, z, range(NT)))
    y = cols(w, 4096, NT, D_IN)
    state = cols(w, 8192, SSD_HEADS, SSD_P)
    cb = cols(w, 10240, SSD_G, P)
    free = cols_of(c.x_t)
    xdt, xw = cols(free, 0, SSD_HEADS, SSD_P), cols(free, 2048, SSD_HEADS, SSD_P)
    seg_l = cols(c.par, 1024, 8, P)
    seg_e = cols(c.par, 2048, 8, P)
    dt = cols(small, 128, ROWS, SSD_HEADS)
    dta = cols(small, 256, ROWS, SSD_HEADS)
    ex = cols(small, 384, 3, SSD_HEADS)
    before = cols_of(c.future)[:, 2 * P:3 * P]
    t1, t2, t3 = (cols(c.par, 3072 + n * P, ROWS, SSD_HEADS) for n in range(3))
    raw = cols(c.par, 3072 + 3 * P, ROWS, SSD_HEADS)

    def over_width(x):
        return x.unsqueeze(2).broadcast_to([P, SSD_HEADS, SSD_P])

    def as_heads(x):
        return x.rearrange("p (h d) -> p h d", d=SSD_P)

    def four_banks(first):
        return ps[:, first:first + 4, :].rearrange("p b (h d) -> p (b h) d", d=SSD_P)

    @c.block.scalar
    def _(s):
        s.wait_ge(c.steps_done, c.steps)
        s.activation(z, z, ACT.Silu).then_inc(c.steps_done, 1)
    c.steps += 1

    @c.block.scalar
    def _(s):
        s.wait_ge(c.steps_done, c.steps)
        s.activation(decay_rate, decay_rate, ACT.Exp).then_inc(c.steps_done, 1)
    c.steps += 1

    @c.block.vector
    def _(v):
        v.wait_ge(c.steps_done, c.steps)
        v.tensor_scalar(decay_rate, decay_rate, -1.0, None, ALU.mult).then_inc(c.steps_done, 1)
    c.steps += 1

    @c.block.vector
    def _(v):
        v.wait_ge(c.steps_done, c.steps)
        for t in range(NT):
            last = v.tensor_tensor(as_heads(y[:, t, :]), as_heads(xs[:, t, :]), over_width(d_skip), ALU.mult)
        last.then_inc(c.steps_done, 1)
    c.steps += 1

    for d, order in enumerate(((2, 3, 0, 1), (3, 2, 1, 0))):
        after, incl = (c.after[:, 0, 0:P], c.upto[:, :]) if d == 0 else (before, c.onward[:, :])

        @c.block.vector
        def _(v):
            v.wait_ge(c.steps_done, c.steps)
            v.tensor_tensor(
raw, dt_raw, dt_bias[:, d:d + 1, :].broadcast_to([P, ROWS, SSD_HEADS]), ALU.add).then_inc(c.steps_done, 1)
        c.steps += 1
        c.softplus(raw, dt, t1, t2, t3)

        @c.block.vector
        def _(v):
            v.wait_ge(c.steps_done, c.steps)
            v.tensor_tensor(
dta, dt, decay_rate[:, d:d + 1, :].broadcast_to([P, ROWS, SSD_HEADS]), ALU.mult).then_inc(c.steps_done, 1)
        c.steps += 1
        for n, tile in enumerate(order):
            x_h = as_heads(xs[:, tile, :])

            @c.block.tensor
            def _(pe):
                pe.wait_ge(c.steps_done, c.steps)
                pe.matmul(ps[:, 0, 0:SSD_HEADS], after, dta[:, tile, :], start=True, stop=True)
                pe.matmul(ps[:, 0, SSD_HEADS:2 * SSD_HEADS], incl, dta[:, tile, :], start=True, stop=True)
                pe.matmul(ps[:, 0, 2 * SSD_HEADS:3 * SSD_HEADS], c.ones[:, :], dta[:, tile, :],
                          start=True, stop=True).then_inc(c.steps_done, 1)
            @c.block.vector
            def _(v):
                v.wait_ge(c.steps_done, c.steps)
                v.tensor_tensor(xdt, x_h, over_width(dt[:, tile, :]), ALU.mult).then_inc(c.steps_done, 1)
            c.steps += 2

            @c.block.scalar
            def _(s):
                s.wait_ge(c.steps_done, c.steps)
                s.activation(
ex, ps[:, 0, 0:3 * SSD_HEADS].rearrange("p (k h) -> p k h", k=3), ACT.Exp).then_inc(c.steps_done, 1)
            c.steps += 1

            @c.block.vector
            def _(v):
                v.wait_ge(c.steps_done, c.steps)
                v.tensor_tensor(xw, xdt, over_width(ex[:, 0, :]), ALU.mult).then_inc(c.steps_done, 1)
            c.steps += 1
            if tile < NT:
                y_h = as_heads(y[:, tile, :])
                tokens = slice(tile * P, (tile + 1) * P)

                @c.block.tensor
                def _(pe):
                    pe.wait_ge(c.steps_done, c.steps)
                    for g in range(SSD_G):
                        pe.matmul(ps[:, 4 + g // 4, g % 4 * P:(g % 4 + 1) * P], b_t[:, g, tokens],
                                  c_t[:, g, tokens], start=True, stop=True)
                    for g in range(SSD_G):
                        last = pe.matmul(ps[:, g // 2, g % 2 * SEQ:(g % 2 + 1) * SEQ], c_t[:, g, tokens],
                                         state[:, g * 4:(g + 1) * 4, :].rearrange("p h d -> p (h d)"),
                                         start=True, stop=True)
                    last.then_inc(c.steps_done, 1)
                c.steps += 1

                @c.block.vector
                def _(v):
                    v.wait_ge(c.steps_done, c.steps)
                    v.tensor_tensor(
cb, ps[:, 4:6, :].rearrange("p b (g l) -> p (b g) l", l=P),
incl.unsqueeze(1).broadcast_to([P, SSD_G, P]), ALU.mult).then_inc(c.steps_done, 1)
                c.steps += 1
                off = cols(c.par, 1024, SSD_HEADS, SSD_P)

                @c.block.vector
                def _(v):
                    v.wait_ge(c.steps_done, c.steps)
                    v.tensor_tensor(off, four_banks(0), over_width(ex[:, 1, :]), ALU.mult).then_inc(c.steps_done, 1)
                c.steps += 1

                @c.block.vector
                def _(v):
                    v.wait_ge(c.steps_done, c.steps)
                    v.tensor_tensor(y_h, y_h, off, ALU.add).then_inc(c.steps_done, 1)
                c.steps += 1
                for part in range(4):
                    heads = slice(part * 8, part * 8 + 8)

                    @c.block.vector
                    def _(v):
                        v.wait_ge(c.steps_done, c.steps)
                        v.tensor_tensor(
    seg_l, after.unsqueeze(1).broadcast_to([P, 8, P]),
    dta[:, tile, heads].unsqueeze(2).broadcast_to([P, 8, P]), ALU.mult).then_inc(c.steps_done, 1)
                    c.steps += 1

                    @c.block.tensor
                    def _(pe):
                        pe.wait_ge(c.steps_done, c.steps)
                        for h in range(8):
                            last = pe.matmul(ps[:, 4 + h // 4, h % 4 * P:(h % 4 + 1) * P], seg_l[:, h, :], incl,
                                             start=True, stop=True)
                        last.then_inc(c.steps_done, 1)
                    c.steps += 1

                    @c.block.scalar
                    def _(s):
                        s.wait_ge(c.steps_done, c.steps)
                        s.activation(
    seg_e, ps[:, 4:6, :].rearrange("p b (h l) -> p (b h) l", l=P), ACT.Exp).then_inc(c.steps_done, 1)
                    c.steps += 1

                    @c.block.vector
                    def _(v):
                        v.wait_ge(c.steps_done, c.steps)
                        v.tensor_tensor(
    seg_e.rearrange("p (g h) l -> p g h l", g=2), seg_e.rearrange("p (g h) l -> p g h l", g=2),
    cb[:, 2 * part:2 * part + 2, :].unsqueeze(2).broadcast_to([P, 2, 4, P]), ALU.mult).then_inc(c.steps_done, 1)
                    c.steps += 1

                    @c.block.tensor
                    def _(pe):
                        pe.wait_ge(c.steps_done, c.steps)
                        for h in range(8):
                            last = pe.matmul(ps[:, part, h * SSD_P:(h + 1) * SSD_P], seg_e[:, h, :],
                                             xdt[:, part * 8 + h, :], start=True, stop=True)
                        last.then_inc(c.steps_done, 1)
                    c.steps += 1

                @c.block.vector
                def _(v):
                    v.wait_ge(c.steps_done, c.steps)
                    v.tensor_tensor(y_h, y_h, four_banks(0), ALU.add).then_inc(c.steps_done, 1)
                c.steps += 1
            if n < len(order) - 1:

                @c.block.tensor
                def _(pe):
                    pe.wait_ge(c.steps_done, c.steps)
                    for g in range(SSD_G):
                        last = pe.matmul(ps[:, g // 2, g % 2 * SEQ:(g % 2 + 1) * SEQ],
                                         b_tok[:, tile, g * P:(g + 1) * P],
                                         xw[:, g * 4:(g + 1) * 4, :].rearrange("p h d -> p (h d)"),
                                         start=True, stop=True)
                    last.then_inc(c.steps_done, 1)
                c.steps += 1
                if n == 0:

                    @c.block.vector
                    def _(v):
                        v.wait_ge(c.steps_done, c.steps)
                        v.tensor_copy(state, four_banks(0)).then_inc(c.steps_done, 1)
                    c.steps += 1
                else:

                    @c.block.vector
                    def _(v):
                        v.wait_ge(c.steps_done, c.steps)
                        v.tensor_tensor(state, state, over_width(ex[:, 2, :]), ALU.mult).then_inc(c.steps_done, 1)
                    c.steps += 1

                    @c.block.vector
                    def _(v):
                        v.wait_ge(c.steps_done, c.steps)
                        v.tensor_tensor(state, state, four_banks(0), ALU.add).then_inc(c.steps_done, 1)
                    c.steps += 1

    gain = cols(c.par, 1024, D_IN)
    c.load(gain, a["ssd_norm_g_2"][0, :].partition_broadcast(P))
    c.loaded()
    ss = cols(small, 0, NT, SSD_G)
    square = cols(free, 0, NT, D_IN)
    y_g = y.rearrange("p t (g d) -> p t g d", g=SSD_G)

    @c.block.vector
    def _(v):
        v.wait_ge(c.steps_done, c.steps)
        v.tensor_tensor(y, y, z, ALU.mult).then_inc(c.steps_done, 1)
    c.steps += 1

    @c.block.vector
    def _(v):
        v.wait_ge(c.steps_done, c.steps)
        v.tensor_tensor(square, y, y, ALU.mult).then_inc(c.steps_done, 1)
    c.steps += 1

    @c.block.vector
    def _(v):
        v.wait_ge(c.steps_done, c.steps)
        v.reduce_sum(ss, square.rearrange("p t (g d) -> p t g d", g=SSD_G), AX).then_inc(c.steps_done, 1)
    c.steps += 1
    c.rstd(ss, 1.0 / 256, EPS)

    @c.block.vector
    def _(v):
        v.wait_ge(c.steps_done, c.steps)
        v.tensor_tensor(y_g, y_g, ss.unsqueeze(3).broadcast_to([P, NT, SSD_G, 256]), ALU.mult).then_inc(c.steps_done, 1)
    c.steps += 1

    @c.block.vector
    def _(v):
        v.wait_ge(c.steps_done, c.steps)
        v.tensor_tensor(y, y, gain.unsqueeze(1).broadcast_to([P, NT, D_IN]), ALU.mult).then_inc(c.steps_done, 1)
    c.steps += 1
    wide = cols(free, 0, D_IN // P, SEQ)
    c.to_feature_major(lambda t, k: y[:, t, k * P:(k + 1) * P], wide, NT, kd=D_IN // P)
    c.gemm_rows(wide, D_IN // P, range(NT), a["ssd_w_out_2"][0], rows_stage(c.work_split))
    c.take_rows(out, NT)


def second_block(c, a):
    y4 = cols(c.work, 7680, ROWS, D)
    gain = [c.par[:, n * D:(n + 1) * D] for n in range(4)]
    for layer in range(DEPTH):
        last_layer = layer == DEPTH - 1
        mods = cols(c.z, 0, 2, 2 * D)
        modulation(c, a, layer, 0, 4, mods, range(2))
        c.load(c.par[:, 0:2 * D], a["ada_b_2"][layer, 0:2 * D].partition_broadcast(P))
        c.load(gain[2], a["norm1_g_2"][layer, :].partition_broadcast(P))
        c.loaded()

        @c.block.vector
        def _(v):
            v.wait_ge(c.steps_done, c.steps)
            v.tensor_tensor(mods, mods, c.par[:, 0:2 * D].unsqueeze(1).broadcast_to(
[P, 2, 2 * D]), ALU.add).then_inc(c.steps_done, 1)
        c.steps += 1
        for n, x in enumerate((c.h, c.hc)):
            modulated_norm(c, tiles_of(x), tiles_of(y4[:, NT * n:NT * n + NT, :]), gain[2],
                           mods[:, n, 0:D], mods[:, n, D:2 * D])
        c.to_feature_major(lambda t, k: y4[:, t, k * P:(k + 1) * P], c.x_t, ROWS)
        split_wide(c, ROWS * P)
        if layer % 2 == 0:
            mixed = cols(c.work, 0, ROWS, D)
            hybrid_mixer(c, a, mixed)
        else:
            mixed = cols(c.work, 0, NT, D)
            ssd_mixer(c, a, mixed)

        seqs = 1 if last_layer else 2
        mods = cols(c.z, 0, 2, 3 * D)
        mod5 = cols(c.z, 16384, 2, D)
        modulation(c, a, layer, 2 * D, 6, mods, range(seqs))
        modulation(c, a, layer, 5 * D, 2, mod5, range(seqs))
        c.load(c.par[:, :], a["ada_b_2"][layer, 2 * D:6 * D].partition_broadcast(P))
        norm2 = cols(c.z, 8192, D)
        c.load(norm2, a["norm2_g_2"][layer, :].partition_broadcast(P))
        c.loaded()

        @c.block.vector
        def _(v):
            v.wait_ge(c.steps_done, c.steps)
            v.tensor_tensor(mods[:, 0:seqs], mods[:, 0:seqs],
                            c.par[:, 0:3 * D].unsqueeze(1).broadcast_to([P, seqs, 3 * D]), ALU.add)
            v.tensor_tensor(mod5[:, 0:seqs], mod5[:, 0:seqs],
                            gain[3].unsqueeze(1).broadcast_to([P, seqs, D]), ALU.add).then_inc(c.steps_done, 1)
        c.steps += 1
        streams = (c.h, c.hc)[:seqs]

        def add_scaled(out, by):

            @c.block.vector
            def _(v):
                v.wait_ge(c.steps_done, c.steps)
                for n in range(seqs):
                    o = out[:, NT * n:NT * n + NT, :]
                    last = v.tensor_tensor(o, o, by(n).unsqueeze(1).broadcast_to([P, NT, D]), ALU.mult)
                last.then_inc(c.steps_done, 1)
            c.steps += 1

            @c.block.vector
            def _(v):
                v.wait_ge(c.steps_done, c.steps)
                for n, x in enumerate(streams):
                    last = v.tensor_tensor(x[:, :, :], x[:, :, :], out[:, NT * n:NT * n + NT, :], ALU.add)
                last.then_inc(c.steps_done, 1)
            c.steps += 1
        add_scaled(mixed, lambda n: mods[:, n, 0:D])
        for n, x in enumerate(streams):
            modulated_norm(c, tiles_of(x), tiles_of(y4[:, NT * n:NT * n + NT, :]), norm2,
                           mods[:, n, D:2 * D], mods[:, n, 2 * D:3 * D])
        tiles = seqs * NT
        tokens = tiles * P
        c.to_feature_major(lambda t, k: y4[:, t, k * P:(k + 1) * P], c.x_t, tiles)
        split_wide(c, tokens)

        k_hidden = 4 * KD
        hidden = cols(c.z, 0, k_hidden, tokens)
        banks = 4 * tokens // BANK

        def relu(i, half, s):
            src = c.ps[:, half * 4:half * 4 + banks, :].rearrange("p b n -> p (b n)")
            return s.activation(hidden[:, bass.ds(i * 4, 4), :].rearrange("p k n -> p (k n)"), src, ACT.Relu)

        def squared(i, half, v):
            part = hidden[:, bass.ds(i * 4, 4), :].rearrange("p k n -> p (k n)")
            return v.tensor_tensor(part, part, part, ALU.mult)
        c.gemm_feature_major(tokens, 8, column_units(a["mlp_w1_2"][layer], 0), relu, squared,
                             after_scalar=True)
        c.gemm_rows(hidden, k_hidden, range(tiles), a["mlp_w2_2"][layer], rows_stage(c.x_t_split))
        out = cols(c.work, 0, tiles, D)
        c.take_rows(out, tiles)
        add_scaled(out, lambda n: mod5[:, n, :])
    final_gain = c.par[:, 0:D]
    c.load(final_gain, a["norm_f_g_2"].partition_broadcast(P))
    c.loaded()
    result = cols(c.work, 0, NT, D)
    c.rmsnorm(tiles_of(c.h), tiles_of(result), final_gain)
    c.result = result


def program(nc, a, out):
    ctx = ExitStack()
    with ctx:
        block = ctx.enter_context(nc.Block())
        c = Core(nc, block, ctx)
        c.z = c.sb("wide", [P, 18560])
        c.h = c.sb("residual", [P, NT, D])
        c.hc = c.sb("context_residual", [P, NT, D])
        x_t_at = nc.sbuf_base
        c.x_t = c.sb("input_feature_major", [P, KD, 2 * SEQ])
        c.x_t_split = nc.alloc_sbuf_tensor_at("input_split", [P, KD, 2 * SEQ], F32R, offset=x_t_at)
        c.par = c.sb("parameters", [P, 4 * D])
        c.small = c.sb("small", [P, 512])
        work_at = nc.sbuf_base
        c.work = c.sb("work", [P, WORK])
        c.work_split = nc.alloc_sbuf_tensor_at("work_split", [P, KD, 2 * SEQ], F32R,
                                               offset=work_at + 4 * (WORK - 2 * KD * SEQ))
        c.result_stored = ctx.enter_context(nc.semaphore("result_stored"))
        c.prime()
        c.load(c.h[:, :, :], a["x"].rearrange("o (t p) d -> p (o t) d", p=P))
        c.load(c.hc[:, :, :], a["ctx_2"].rearrange("o (t p) d -> p (o t) d", p=P))
        c.loaded()
        make_constants(c)
        first_block(c, a)
        second_block(c, a)
        last = c.steps

        @block.sync
        def _(sp):
            sp.wait_ge(c.steps_done, last)
            sp.dma_start(out.rearrange("o (t p) d -> p (o t) d", p=P), c.result).then_inc(c.result_stored, 16)
            sp.wait_ge(c.result_stored, 16)


def kernel(**inputs):
    import numpy as _np
    import concourse.bacc as _bacc
    from concourse import mybir as _mybir
    from concourse.bass_utils import run_bass_kernel_spmd as _run

    laid = {name: _np.asarray(value) for name, value in inputs.items()}
    for name, order in LAYOUTS.items():
        laid[name] = order(laid[name])
    laid.update(shape_constants())
    nc = _bacc.Bacc("TRN2", target_bir_lowering=False, num_devices=1)
    arrays, a = {}, {}
    for name, value in laid.items():
        value = _np.ascontiguousarray(value)
        arrays[f"in_{name}"] = value
        a[name] = nc.dram_tensor(f"in_{name}", value.shape, _mybir.dt.from_np(value.dtype),
                                 kind="ExternalInput").ap()
    out = nc.dram_tensor("out_0", (1, SEQ, D), _mybir.dt.float32, kind="ExternalOutput").ap()
    program(nc, a, out)
    r = _run(nc, [arrays], core_ids=[0])
    return r.results[0]["out_0"]
```

```python
import math
from contextlib import ExitStack

import concourse.bass as bass
import numpy as np
from concourse import mybir

F32 = mybir.dt.float32
F32R = mybir.dt.float32r
ALU = mybir.AluOpType
ACT = mybir.ActivationFunctionType
AX = mybir.AxisListType.X

P = 128
D = 1024
KD = D // P
SEQ = 256
NT = SEQ // P
DEPTH = 2
EPS = 1e-6
BANK = 512
UNITS = 4
UNIT = KD * BANK // UNITS


class Chain:

    def __init__(self, c, name):
        self.block, self.nc = c.block, c.nc
        self.steps_done = c.ctx.enter_context(c.nc.semaphore(name))
        self.steps = 0


class Core:

    def __init__(self, nc, block, ctx):
        self.nc, self.block, self.ctx = nc, block, ctx
        self.steps_done = ctx.enter_context(nc.semaphore("steps_done"))
        self.steps = 0
        self.raw_arrived = [ctx.enter_context(nc.semaphore(f"raw_weights_arrived_{u}")) for u in range(UNITS)]
        self.hi_made = ctx.enter_context(nc.semaphore("weights_hi_made"))
        self.lo_made = ctx.enter_context(nc.semaphore("weights_lo_made"))
        self.pads_filled = ctx.enter_context(nc.semaphore("convolution_pads_filled"))
        self.taps_done = ctx.enter_context(nc.semaphore("convolution_taps_done"))
        self.input_transposed = ctx.enter_context(nc.semaphore("input_transposed"))
        self.input_hi_made = ctx.enter_context(nc.semaphore("input_hi_made"))
        self.multiplied = ctx.enter_context(nc.semaphore("units_multiplied"))
        self.taken_by_scalar = ctx.enter_context(nc.semaphore("products_taken_by_scalar"))
        self.taken_by_vector = ctx.enter_context(nc.semaphore("products_taken_by_vector"))
        self.params_arrived = ctx.enter_context(nc.semaphore("params_arrived"))
        self.chunks = 0
        self.taken = 2
        self.params = 0
        self.units_ahead = 0
        self.left_to_empty = None
        self.next_half = 0
        self.inputs_transposed = 0
        self.inputs_split = 0
        self.raw = self.sb("raw_weights", [P, UNITS, UNIT])
        self.w_hi = self.sb("weights_hi", [P, 2, UNIT], F32R)
        self.w_lo = self.sb("weights_lo", [P, 2, UNIT], F32R)
        self.ps = ctx.enter_context(nc.psum_tensor("banks", [P, 8, BANK], F32))
        self.chains = [Chain(self, f"chain_{q}_steps_done") for q in range(2)]

    def sb(self, name, shape, dtype=F32):
        return self.ctx.enter_context(self.nc.sbuf_tensor(name, shape, dtype))

    def begin_chains(self):
        n = self.steps

        @self.block.tensor
        def _(pe):
            pe.wait_ge(self.steps_done, n)

        @self.block.vector
        def _(v):
            v.wait_ge(self.steps_done, n)

        @self.block.scalar
        def _(s):
            s.wait_ge(self.steps_done, n)

    def end_chains(self):
        for chain in self.chains:
            n = chain.steps

            @self.block.tensor
            def _(pe):
                pe.wait_ge(chain.steps_done, n)

            @self.block.vector
            def _(v):
                v.wait_ge(chain.steps_done, n)

            @self.block.scalar
            def _(s):
                s.wait_ge(chain.steps_done, n)

            @self.block.gpsimd
            def _(g):
                g.wait_ge(chain.steps_done, n)

    def load(self, dst, src):
        at = self.steps

        @self.block.gpsimd
        def _(pool):
            pool.wait_ge(self.steps_done, at)
            pool.dma_start(dst, src).then_inc(self.params_arrived, 16)
        self.params += 1

    def loaded(self):
        n = 16 * self.params

        @self.block.tensor
        def _(pe):
            pe.wait_ge(self.params_arrived, n)

        @self.block.vector
        def _(v):
            v.wait_ge(self.params_arrived, n)

        @self.block.scalar
        def _(s):
            s.wait_ge(self.params_arrived, n)

        @self.block.gpsimd
        def _(g):
            g.wait_ge(self.params_arrived, n)

    def prime(self):
        @self.block.tensor
        def _(pe):
            pe.sem_inc(self.multiplied, 2)

        @self.block.scalar
        def _(s):
            s.sem_inc(self.taken_by_scalar, 2)

        @self.block.vector
        def _(v):
            v.sem_inc(self.taken_by_vector, 2)
            v.sem_inc(self.lo_made, UNITS)

    def split_input(self, x, hi, lo):
        at, made = self.steps, self.inputs_split
        pieces = [slice(k, k + KD // 4) for k in range(0, KD, KD // 4)]

        @self.block.scalar
        def _(s):
            s.wait_ge(self.steps_done, at)
            for piece in pieces:
                s.activation(hi[:, piece, :], x[:, piece, :], ACT.Copy).then_inc(self.input_hi_made, 1)

        @self.block.vector
        def _(v):
            v.wait_ge(self.steps_done, at)
            for n, piece in enumerate(pieces):
                v.wait_ge(self.input_hi_made, made + n + 1)
                last = v.tensor_tensor(lo[:, piece, :], x[:, piece, :], hi[:, piece, :].bitcast(F32), ALU.subtract)
            last.then_inc(self.steps_done, 1)
        self.inputs_split += len(pieces)
        self.steps += 1
        self.x_hi, self.x_lo = hi, lo

    def split_first_weights(self):
        c0, m0 = self.chunks, self.chunks * UNITS

        @self.block.scalar
        def _(s):
            for u in range(2):
                self.hi_unit(s, u, c0, m0)

        @self.block.vector
        def _(v):
            for u in range(2):
                self.lo_unit(v, u, m0)
        self.units_ahead = 2

    def unit(self, buf, shape):
        return buf[:, 0:int(np.prod(shape))].rearrange("p (k n) -> p k n", n=shape[-1])

    def load_units(self, sp, source, shape, chunk, unit):
        for u in range(UNITS):
            sp.wait_ge(self.lo_made, unit + u + 1)
            sp.dma_start(self.unit(self.raw[:, u, :], shape), source(u)).then_inc(self.raw_arrived[u], 16)

    def hi_unit(self, s, u, chunk, unit, x=None):
        s.wait_ge(self.raw_arrived[u], chunk * 16 + 16)
        s.wait_ge(self.multiplied, unit + u + 1)
        last = s.activation(self.w_hi[:, u % 2, :], self.raw[:, u, :], ACT.Copy)
        if x is not None:
            last = s.activation(self.stage_hi(u, x), x, ACT.Copy)
        last.then_inc(self.hi_made, 1)

    def lo_unit(self, v, u, unit, x=None):
        v.wait_ge(self.hi_made, unit + u + 1)
        last = v.tensor_tensor(self.w_lo[:, u % 2, :], self.raw[:, u, :], self.w_hi[:, u % 2, :].bitcast(F32),
                               ALU.subtract)
        if x is not None:
            last = v.tensor_tensor(self.stage_lo(u, x), x, self.stage_hi(u, x).bitcast(F32), ALU.subtract)
        last.then_inc(self.lo_made, 1)

    def stage_hi(self, u, x):
        return self.staged[:, u % 2, 0:1, 0:x.shape[-1]]

    def stage_lo(self, u, x):
        return self.staged[:, u % 2, 1:2, 0:x.shape[-1]]

    def three_products(self, pe, out, left_hi, left_lo, right_hi, right_lo, start, stop):
        pe.matmul(out, left_hi, right_hi, start=start, stop=False)
        pe.matmul(out, left_hi, right_lo, start=False, stop=False)
        return pe.matmul(out, left_lo, right_hi, start=False, stop=stop)

    def gemm(self, count, source, shape, product, take_scalar, take_vector, after_scalar=False,
             finish=None, more=False):
        nc, at, g0 = self.nc, self.steps, self.taken
        ahead, left, h0 = self.units_ahead, self.left_to_empty, self.next_half
        c0, m0 = self.chunks, self.chunks * UNITS
        pairs = (count - 1) // 2 if count >= 5 and not finish else 0

        def empty_by_scalar(s, chunk, half):
            s.wait_ge(self.multiplied, chunk * UNITS + (m0 + 2 + UNITS))
            last = take_scalar(chunk, (half + h0) % 2, s)
            if last is None:
                s.sem_inc(self.taken_by_scalar, 1)
            else:
                last.then_inc(self.taken_by_scalar, 1)

        def empty_by_vector(v, chunk, half):
            v.wait_ge(self.multiplied, chunk * UNITS + (m0 + 2 + UNITS))
            if after_scalar:
                v.wait_ge(self.taken_by_scalar, chunk + (g0 + 1))
            last = take_vector(chunk, (half + h0) % 2, v)
            if last is None:
                v.sem_inc(self.taken_by_vector, 1)
            else:
                last.then_inc(self.taken_by_vector, 1)

        def empty_last(s):
            empty_by_scalar(s, count - 1, (count - 1) % 2)

        def empty_last_too(v):
            empty_by_vector(v, count - 1, (count - 1) % 2)

        @self.block.sync
        def _(sp):
            if count > 1:
                with sp.Fori(0, count) as i:
                    self.load_units(sp, lambda u: source(i, u), shape, i + c0, i * UNITS + m0)
            else:
                self.load_units(sp, lambda u: source(0, u), shape, c0, m0)

        @self.block.tensor
        def _(pe):
            pe.wait_ge(self.steps_done, at)

            def multiply(chunk, half):
                pe.wait_ge(self.taken_by_scalar, chunk + (g0 - 1))
                pe.wait_ge(self.taken_by_vector, chunk + (g0 - 1))
                for u in range(UNITS):
                    pe.wait_ge(self.lo_made, chunk * UNITS + (m0 + u + 1 + UNITS))
                    product((half + h0) % 2 * 4, u, self.unit(self.w_hi[:, u % 2, :], shape),
                            self.unit(self.w_lo[:, u % 2, :], shape), nc.tensor).then_inc(self.multiplied, 1)
            multiply(0, 0)
            if pairs:
                with pe.Fori(0, pairs) as i:
                    multiply(i * 2 + 1, 1)
                    multiply(i * 2 + 2, 0)
            for chunk in range(1 + 2 * pairs, count):
                multiply(chunk, chunk % 2)

        @self.block.scalar
        def _(s):
            s.wait_ge(self.steps_done, at)

            def split_and_empty(chunk, half):
                for u in range(UNITS):
                    if u == UNITS // 2:
                        empty_by_scalar(s, chunk - 1, 1 - half)
                    self.hi_unit(s, u, chunk + c0, chunk * UNITS + m0)
            for u in range(ahead, UNITS):
                if left and u == UNITS // 2:
                    left[0](s)
                self.hi_unit(s, u, c0, m0)
            if pairs:
                with s.Fori(0, pairs) as i:
                    split_and_empty(i * 2 + 1, 1)
                    split_and_empty(i * 2 + 2, 0)
            for chunk in range(1 + 2 * pairs, count):
                split_and_empty(chunk, chunk % 2)
            if not more:
                empty_last(s)

        @self.block.vector
        def _(v):
            v.wait_ge(self.steps_done, at)

            def split_and_empty(chunk, half):
                for u in range(UNITS):
                    if u == UNITS // 2:
                        empty_by_vector(v, chunk - 1, 1 - half)
                    self.lo_unit(v, u, chunk * UNITS + m0)
                if finish:
                    finish(chunk - 1, v)
            for u in range(ahead, UNITS):
                if left and u == UNITS // 2:
                    left[1](v)
                self.lo_unit(v, u, m0)
            if pairs:
                with v.Fori(0, pairs) as i:
                    split_and_empty(i * 2 + 1, 1)
                    split_and_empty(i * 2 + 2, 0)
            for chunk in range(1 + 2 * pairs, count):
                split_and_empty(chunk, chunk % 2)
            if not more:
                empty_last_too(v)
                if finish:
                    finish(count - 1, v)
        self.chunks += count
        self.taken += count
        self.units_ahead = 0
        self.left_to_empty = (empty_last, empty_last_too) if more else None
        self.next_half = (h0 + count) % 2 if more else 0
        n = self.taken
        if more:
            return

        @self.block.tensor
        def _(pe):
            pe.wait_ge(self.taken_by_scalar, n)
            pe.wait_ge(self.taken_by_vector, n)

        @self.block.scalar
        def _(s):
            s.wait_ge(self.taken_by_scalar, n)
            s.wait_ge(self.taken_by_vector, n)

        @self.block.vector
        def _(v):
            v.wait_ge(self.taken_by_scalar, n)
            v.wait_ge(self.taken_by_vector, n)

        @self.block.gpsimd
        def _(g):
            g.wait_ge(self.taken_by_scalar, n)
            g.wait_ge(self.taken_by_vector, n)

    def gemm_token_major(self, tiles, count, source, width, take_scalar, take_vector, after_scalar=False,
                         more=False):
        per_unit = KD // UNITS

        def product(banks, u, hi, lo, pe):
            for n, t in enumerate(tiles):
                for j in range(per_unit):
                    k, tokens = u * per_unit + j, slice(t * P, (t + 1) * P)
                    last = self.three_products(pe, self.ps[:, banks + n, 0:width], self.x_hi[:, k, tokens],
                                               self.x_lo[:, k, tokens], hi[:, j, :], lo[:, j, :],
                                               k == 0, k == KD - 1)
            return last
        self.gemm(count, lambda i, u: source(i)[:, u * per_unit:(u + 1) * per_unit, :], (per_unit, width), product,
                  take_scalar, take_vector, after_scalar, more=more)

    def gemm_feature_major(self, tokens, count, source, take_scalar, take_vector, after_scalar=False,
                           finish=None, more=False):
        def product(banks, u, hi, lo, pe):
            at = u * tokens
            out = self.ps[:, banks + at // BANK, at % BANK:at % BANK + tokens]
            for k in range(KD):
                last = self.three_products(pe, out, hi[:, k, :], lo[:, k, :], self.x_hi[:, k, 0:tokens],
                                           self.x_lo[:, k, 0:tokens], k == 0, k == KD - 1)
            return last
        self.gemm(count, source, (KD, P), product, take_scalar, take_vector, after_scalar, finish, more)

    def gemm_rows(self, x, k_chunks, tiles, w_rows, staged):
        nc, at = self.nc, self.steps
        self.staged = staged
        w_v = w_rows.rearrange("(k p) n -> p k n", p=P)
        full = k_chunks // UNITS
        tail = k_chunks % UNITS
        middle = full - 2 + bool(tail)
        c0, m0 = self.chunks, self.chunks * UNITS

        def piece(k):
            return x[:, bass.ds(k, 1), :]

        @self.block.sync
        def _(sp):
            with sp.Fori(0, full) as i:
                self.load_units(sp, lambda u: w_v[:, bass.ds(i * UNITS + u, 1), :], (1, D), i + c0,
                                i * UNITS + m0)
            if tail:
                self.load_units(sp, lambda u: w_v[:, full * UNITS + u // 2:full * UNITS + u // 2 + 1,
                                                  u % 2 * BANK:(u % 2 + 1) * BANK], (1, BANK), full + c0,
                                full * UNITS + m0)

        @self.block.tensor
        def _(pe):
            pe.wait_ge(self.steps_done, at)

            def multiply(chunk, first, last_chunk, halves):
                for u in range(UNITS):
                    pe.wait_ge(self.lo_made, chunk * UNITS + (m0 + u + 1 + UNITS))
                    for n, t in enumerate(tiles):
                        tokens = slice(t * P, (t + 1) * P)
                        for half in (range(2) if halves else (u % 2,)):
                            columns = slice(half * BANK, (half + 1) * BANK) if halves else slice(0, BANK)
                            last = self.three_products(
                                nc.tensor, self.ps[:, 2 * n + half, :], self.staged[:, u % 2, 0, tokens],
                                self.staged[:, u % 2, 1, tokens], self.w_hi[:, u % 2, columns],
                                self.w_lo[:, u % 2, columns], first and u == 0,
                                last_chunk and (u == UNITS - 1 or (not halves and u >= 2)))
                    last.then_inc(self.multiplied, 1)
            multiply(0, True, False, True)
            with pe.Fori(0, middle) as i:
                multiply(i + 1, False, False, True)
            multiply(middle + 1, False, True, not tail)

        @self.block.scalar
        def _(s):
            s.wait_ge(self.steps_done, at)
            with s.Fori(0, full) as i:
                for u in range(UNITS):
                    self.hi_unit(s, u, i + c0, i * UNITS + m0, piece(i * UNITS + u))
            if tail:
                for u in range(UNITS):
                    self.hi_unit(s, u, full + c0, full * UNITS + m0, piece(full * UNITS + u // 2))

        @self.block.vector
        def _(v):
            v.wait_ge(self.steps_done, at)
            with v.Fori(0, full) as i:
                for u in range(UNITS):
                    self.lo_unit(v, u, i * UNITS + m0, piece(i * UNITS + u))
            if tail:
                for u in range(UNITS):
                    self.lo_unit(v, u, full * UNITS + m0, piece(full * UNITS + u // 2))
        self.chunks += full + bool(tail)
        n = self.chunks * UNITS + 2

        @self.block.scalar
        def _(s):
            s.wait_ge(self.multiplied, n)

        @self.block.vector
        def _(v):
            v.wait_ge(self.multiplied, n)

    def take_rows(self, out, tiles):
        ps = self.ps

        @self.block.scalar
        def _(s):
            s.wait_ge(self.steps_done, self.steps)
            for t in range(tiles):
                last = s.activation(out[:, t, 0:BANK], ps[:, 2 * t, :], ACT.Copy)
            last.then_inc(self.steps_done, 1)
        @self.block.vector
        def _(v):
            v.wait_ge(self.steps_done, self.steps)
            for t in range(tiles):
                last = v.tensor_copy(out[:, t, BANK:D], ps[:, 2 * t + 1, :])
            last.then_inc(self.steps_done, 1)
        self.steps += 2

    def transposes(self, quads):
        ident, ps = self.ident, self.ps
        batches = [quads[n:n + 4] for n in range(0, len(quads), 4)]

        def banks_of(n, which):
            for b, (srcs, dst) in enumerate(batches[n]):
                if b % 2 == which:
                    m = srcs[0].shape[-1]
                    yield ps[0:m, n % 2 * 4 + b, 0:len(srcs) * P].rearrange("p (j t) -> p j t", t=P), dst

        for n in range(len(batches) + 1):
            at = self.steps
            if n < len(batches):
                @self.block.tensor
                def _(pe):
                    pe.wait_ge(self.steps_done, at)
                    for b, (srcs, _) in enumerate(batches[n]):
                        for j, src in enumerate(srcs):
                            out = ps[0:src.shape[-1], n % 2 * 4 + b, j * P:(j + 1) * P]
                            last = pe.transpose(out, src, ident[:, :])
                    last.then_inc(self.steps_done, 1)
                self.steps += 1
            if n:
                @self.block.scalar
                def _(s):
                    s.wait_ge(self.steps_done, at)
                    for src, dst in banks_of(n - 1, 0):
                        last = s.activation(dst, src, ACT.Copy)
                    last.then_inc(self.steps_done, 1)
                self.steps += 1
            if n and len(batches[n - 1]) > 1:
                @self.block.vector
                def _(v):
                    v.wait_ge(self.steps_done, at)
                    for src, dst in banks_of(n - 1, 1):
                        last = v.tensor_copy(dst, src)
                    last.then_inc(self.steps_done, 1)
                self.steps += 1

    def to_feature_major(self, x, dst, tiles, kd):
        self.transposes([([x(t, k + j) for j in range(4)], dst[:, k:k + 4, t * P:(t + 1) * P])
                         for t in range(tiles) for k in range(0, kd, 4)])

    def input_from(self, x, hi, lo, tiles):
        self.split_first_weights()
        at, t0, made, ident = self.steps, self.inputs_transposed, self.inputs_split, self.ident
        quads = [(t, k) for t in range(tiles) for k in range(0, KD, 4)]

        def place(buf, t, k):
            return buf[:, k:k + 4, t * P:(t + 1) * P]

        def bank(n):
            return self.ps[:, n, :].rearrange("p (j t) -> p j t", t=P)

        @self.block.tensor
        def _(pe):
            pe.wait_ge(self.steps_done, at)
            for n, (t, k) in enumerate(quads):
                for j in range(4):
                    last = pe.transpose(bank(n)[:, j, :], x(t, k + j), ident[:, :])
                last.then_inc(self.input_transposed, 1)

        @self.block.scalar
        def _(s):
            s.wait_ge(self.steps_done, at)
            for n, (t, k) in enumerate(quads):
                s.wait_ge(self.input_transposed, t0 + n + 1)
                s.activation(place(hi, t, k), bank(n), ACT.Copy).then_inc(self.input_hi_made, 1)

        @self.block.vector
        def _(v):
            v.wait_ge(self.steps_done, at)
            for n, (t, k) in enumerate(quads):
                v.wait_ge(self.input_hi_made, made + n + 1)
                last = v.tensor_tensor(place(lo, t, k), bank(n), place(hi, t, k).bitcast(F32), ALU.subtract)
            last.then_inc(self.steps_done, 1)
        self.inputs_transposed += len(quads)
        self.inputs_split += len(quads)
        self.steps += 1
        self.x_hi, self.x_lo = hi, lo

    def rstd(self, ss, scale, eps):

        @self.block.vector
        def _(v):
            v.wait_ge(self.steps_done, self.steps)
            v.tensor_scalar(ss, ss, scale, eps, ALU.mult, ALU.add).then_inc(self.steps_done, 1)
        self.steps += 1

        @self.block.scalar
        def _(s):
            s.wait_ge(self.steps_done, self.steps)
            s.activation(ss, ss, ACT.Sqrt).then_inc(self.steps_done, 1)
        self.steps += 1

        @self.block.vector
        def _(v):
            v.wait_ge(self.steps_done, self.steps)
            v.reciprocal(ss, ss).then_inc(self.steps_done, 1)
        self.steps += 1

    def rmsnorm(self, xs, outs, gain, n=D, squared=None):
        ss = self.small[:, 0:len(xs)]

        @self.block.scalar
        def _(s):
            s.wait_ge(self.steps_done, self.steps)
            for j, (x, out) in enumerate(zip(xs, squared or outs)):
                last = s.activation(out, x, ACT.Square, accum_out=ss[:, j:j + 1])
            last.then_inc(self.steps_done, 1)
        self.steps += 1
        self.rstd(ss, 1.0 / n, EPS)

        @self.block.vector
        def _(v):
            v.wait_ge(self.steps_done, self.steps)
            for j, (x, out) in enumerate(zip(xs, outs)):
                last = v.scalar_tensor_tensor(out, x, ss[:, j:j + 1], gain, ALU.mult, ALU.mult)
            last.then_inc(self.steps_done, 1)
        self.steps += 1

    def log1p(self, e, out, z, z2):

        @self.block.vector
        def _(v):
            v.wait_ge(self.steps_done, self.steps)
            v.tensor_scalar(z, e, 2.0, None, ALU.add).then_inc(self.steps_done, 1)
        self.steps += 1

        @self.block.vector
        def _(v):
            v.wait_ge(self.steps_done, self.steps)
            v.reciprocal(z, z).then_inc(self.steps_done, 1)
        self.steps += 1

        @self.block.vector
        def _(v):
            v.wait_ge(self.steps_done, self.steps)
            v.tensor_tensor(z, z, e, ALU.mult).then_inc(self.steps_done, 1)
        self.steps += 1

        @self.block.vector
        def _(v):
            v.wait_ge(self.steps_done, self.steps)
            v.tensor_tensor(z2, z, z, ALU.mult).then_inc(self.steps_done, 1)
        self.steps += 1

        @self.block.vector
        def _(v):
            v.wait_ge(self.steps_done, self.steps)
            v.tensor_scalar(out, z2, 1.0 / 17, None, ALU.mult).then_inc(self.steps_done, 1)
        self.steps += 1
        for odd in (15, 13, 11, 9, 7, 5, 3):

            @self.block.vector
            def _(v):
                v.wait_ge(self.steps_done, self.steps)
                v.scalar_tensor_tensor(out, out, 1.0 / odd, z2, ALU.add, ALU.mult).then_inc(self.steps_done, 1)
            self.steps += 1

        @self.block.vector
        def _(v):
            v.wait_ge(self.steps_done, self.steps)
            v.scalar_tensor_tensor(out, out, 1.0, z, ALU.add, ALU.mult).then_inc(self.steps_done, 1)
        self.steps += 1

        @self.block.vector
        def _(v):
            v.wait_ge(self.steps_done, self.steps)
            v.tensor_scalar(out, out, 2.0, None, ALU.mult).then_inc(self.steps_done, 1)
        self.steps += 1

    def softplus(self, x, out, t1, t2, t3):

        @self.block.scalar
        def _(s):
            s.wait_ge(self.steps_done, self.steps)
            s.activation(t1, x, ACT.Abs).then_inc(self.steps_done, 1)
        self.steps += 1

        @self.block.scalar
        def _(s):
            s.wait_ge(self.steps_done, self.steps)
            s.activation(t2, t1, ACT.Exp, scale=-1.0).then_inc(self.steps_done, 1)
        self.steps += 1
        self.log1p(t2, out, t1, t3)

        @self.block.vector
        def _(v):
            v.wait_ge(self.steps_done, self.steps)
            v.scalar_tensor_tensor(out, x, 0.0, out, ALU.max, ALU.add).then_inc(self.steps_done, 1)
        self.steps += 1


def cols(buf, offset, *dims):
    n = int(np.prod(dims))
    flat = buf[:, offset:offset + n]
    if len(dims) == 1:
        return flat
    names = "abcd"[:len(dims)]
    sizes = {names[i]: dims[i] for i in range(1, len(dims))}
    return flat.rearrange(f"p ({' '.join(names)}) -> p {' '.join(names)}", **sizes)


def column_chunks(w, first, width=BANK):
    w_v = w.rearrange("(k p) n -> p k n", p=P)
    return lambda i: w_v[:, :, bass.ds(i * width + first, width)]


def column_units(w, first):
    w_v = w.rearrange("(k p) n -> p k n", p=P)
    return lambda i, u: w_v[:, :, bass.ds(i * BANK + (first + u * P), P)]


def split_narrow(c):
    c.split_input(c.x_t[:, :, 0:SEQ], *narrow(c))


def narrow(c):
    return c.x_t_split[:, :, SEQ:2 * SEQ], c.x_t_split[:, :, 0:SEQ]


def wide(c, tokens):
    return c.work_split[:, :, 0:tokens], c.x_t_split[:, :, 0:tokens]


def rows_stage(split):
    return split[:, 0:4, :].rearrange("p (s h) t -> p s h t", s=2)


def make_constants(c):
    c.ident = c.sb("identity", [P, P])
    c.ones = c.sb("ones", [P, P])
    c.upto = c.sb("mask_row_upto_column", [P, P])
    c.onward = c.sb("mask_row_from_column_on", [P, P])
    c.after = c.sb("mask_row_after_column", [P, NT, SEQ])
    c.future = c.sb("minus_big_where_key_after_query", [P, NT, SEQ])

    @c.block.gpsimd
    def _(g):
        g.wait_ge(c.steps_done, c.steps)
        g.memset(c.ident[:, :], 0.0)
        g.memset(c.ones[:, :], 1.0)
        g.memset(c.upto[:, :], 1.0)
        g.memset(c.onward[:, :], 1.0)
        g.memset(c.after[:, :, :], 1.0)
        g.memset(c.future[:, :, :], 0.0).then_inc(c.steps_done, 1)
    c.steps += 1

    @c.block.gpsimd
    def _(g):
        g.wait_ge(c.steps_done, c.steps)
        g.affine_select(out=c.ident[:, :], in_=c.ident[:, :], compare_op=ALU.not_equal, fill=1.0, base=0,
                        pattern=[[-1, P]], channel_multiplier=1)
        g.affine_select(out=c.upto[:, :], in_=c.upto[:, :], compare_op=ALU.is_ge, fill=0.0, base=0,
                        pattern=[[1, P]], channel_multiplier=-1)
        g.affine_select(out=c.onward[:, :], in_=c.onward[:, :], compare_op=ALU.is_ge, fill=0.0, base=0,
                        pattern=[[-1, P]], channel_multiplier=1)
        g.affine_select(out=c.after[:, :, :], in_=c.after[:, :, :], compare_op=ALU.is_gt, fill=0.0, base=0,
                        pattern=[[P, NT], [-1, SEQ]], channel_multiplier=1)
        g.affine_select(out=c.future[:, :, :], in_=c.future[:, :, :], compare_op=ALU.is_ge, fill=-1e30,
                        base=0, pattern=[[P, NT], [-1, SEQ]], channel_multiplier=1).then_inc(c.steps_done, 1)
    c.steps += 1


def copy_halves(c, dst):
    def scalar(i, half, s):
        last = None
        for n in dst.scalar:
            last = s.activation(dst.place(i, n), dst.bank(half * 4 + n), ACT.Copy)
        return last

    def vector(i, half, v):
        last = None
        for n in dst.vector:
            last = v.tensor_copy(dst.place(i, n), dst.bank(half * 4 + n))
        return last
    return scalar, vector


class Copies:

    def __init__(self, c, place, banks, width=BANK):
        self.place = place
        self.scalar = [n for n in range(banks) if n % 2 == 0]
        self.vector = [n for n in range(banks) if n % 2 == 1]
        self.bank = lambda b: c.ps[:, b, 0:width]


def token_copies(c, dst, tiles, width=BANK):
    return copy_halves(c, Copies(c, lambda i, n: dst[:, tiles[n], bass.ds(i * width, width)], len(tiles), width))


def swiglu(c, w_gu, w_down, out):
    dff = w_down.shape[0]
    k_hidden = dff // P
    hidden = cols(c.z, 0, k_hidden, SEQ)
    act = cols(c.work, 0, 2, 2 * SEQ)
    w_v = w_gu.rearrange("(k p) n -> p k n", p=P)

    def source(i, u):
        return w_v[:, :, bass.ds(i * (2 * P) + (u // 2 * dff + u % 2 * P), P)]

    def scalar(i, half, s):
        return s.activation(act[:, half, :], c.ps[:, half * 4, :], ACT.Silu)

    def vector(i, half, v):
        dst = hidden[:, bass.ds(i * 2, 2), :]
        return v.tensor_tensor(dst, act[:, half, :].rearrange("p (j t) -> p j t", t=SEQ),
                               c.ps[:, half * 4 + 1, :].rearrange("p (j t) -> p j t", t=SEQ), ALU.mult)
    c.gemm_feature_major(SEQ, dff // (2 * P), source, scalar, vector, after_scalar=True)
    c.gemm_rows(hidden, k_hidden, range(NT), w_down, rows_stage(c.x_t_split))
    c.take_rows(out, NT)


def add_normed(c, h, y, gain, scale):
    squared = [c.x_t[:, 2 * t:2 * t + 2, :].rearrange("p k n -> p (k n)") for t in range(NT)]
    c.rmsnorm([y[:, t, :] for t in range(NT)], [y[:, t, :] for t in range(NT)], gain, squared=squared)

    @c.block.vector
    def _(v):
        v.wait_ge(c.steps_done, c.steps)
        for t in range(NT):
            last = v.scalar_tensor_tensor(h[:, t, :], y[:, t, :], scale, h[:, t, :], ALU.mult, ALU.add)
        last.then_inc(c.steps_done, 1)
    c.steps += 1


def mlstm(c, qk_t, v_tok, o_tok, gates, out, gain):
    heads, dv = 4, 256
    scale = float(P) ** -0.5
    w = c.work
    r = cols(w, 2048, heads, NT, SEQ)
    di = cols(w, 4096, heads, NT, P)
    ld = cols(w, 5120, heads, SEQ)
    dm = cols(w, 6144, heads, SEQ)
    s_t = cols(w, 7168, heads, NT, P)
    sm = c.small
    lf, t1, t2, t3 = (cols(sm, 16 + 8 * n, NT, heads) for n in range(4))
    negf = cols(sm, 48, NT, heads)
    mx, den, em, rs = (cols(sm, 56 + 4 * n, heads) for n in range(4))
    stats = cols(sm, 72, heads, 6)
    mv = cols(sm, 96, heads, 2)

    @c.block.vector
    def _(v):
        v.wait_ge(c.steps_done, c.steps)
        v.tensor_scalar(negf, gates[:, :, 4:8], -1.0, None, ALU.mult).then_inc(c.steps_done, 1)
    c.steps += 1
    c.softplus(negf, lf, t1, t2, t3)

    @c.block.vector
    def _(v):
        v.wait_ge(c.steps_done, c.steps)
        v.tensor_scalar(lf, lf, -1.0, None, ALU.mult).then_inc(c.steps_done, 1)
    @c.block.scalar
    def _(s):
        s.wait_ge(c.steps_done, c.steps)
        s.activation(o_tok, o_tok, ACT.Sigmoid).then_inc(c.steps_done, 1)
    c.steps += 2

    @c.block.vector
    def _(v):
        v.wait_ge(c.steps_done, c.steps)
        for h in range(heads):
            for j in range(NT):
                v.tensor_scalar(r[:, h, j, :], c.after[:, j, :], lf[:, j, h:h + 1], None, ALU.mult)
                last = v.tensor_scalar(di[:, h, j, :], c.ident[:, :], gates[:, j, h:h + 1], None, ALU.mult)
        last.then_inc(c.steps_done, 1)
    c.steps += 1
    for t in range(NT):
        n = (t + 1) * P

        def bank(first, h, cut=n):
            return c.ps[:, first + h // 2, h % 2 * SEQ:h % 2 * SEQ + cut]

        def four(first, cut=n):
            return c.ps[:, first:first + 2, :].rearrange("p b (h s) -> p (b h) s", s=SEQ)[:, :, 0:cut]

        @c.block.tensor
        def _(pe):
            pe.wait_ge(c.steps_done, c.steps)
            for h in range(heads):
                for j in range(t + 1):
                    pe.matmul(bank(0, h), c.upto[:, :] if j == t else c.ones[:, :], r[:, h, j, 0:n],
                              start=(j == 0), stop=False)
                for j in range(t + 1):
                    pe.matmul(bank(0, h)[:, j * P:(j + 1) * P], c.ones[:, :], di[:, h, j, :],
                              start=False, stop=(j == t))
            for h in range(heads):
                last = pe.matmul(bank(2, h), qk_t[:, h, t * P:(t + 1) * P], qk_t[:, heads + h, 0:n],
                                 start=True, stop=True)
            last.then_inc(c.steps_done, 1)
        c.steps += 1

        @c.block.vector
        def _(v):
            v.wait_ge(c.steps_done, c.steps)
            v.tensor_tensor(
ld[:, :, 0:n], four(0), c.future[:, t:t + 1, 0:n].broadcast_to([P, heads, n]), ALU.add).then_inc(c.steps_done, 1)
        c.steps += 1

        @c.block.vector
        def _(v):
            v.wait_ge(c.steps_done, c.steps)
            v.reduce_max(mx, ld[:, :, 0:n], AX).then_inc(c.steps_done, 1)
        c.steps += 1

        @c.block.vector
        def _(v):
            v.wait_ge(c.steps_done, c.steps)
            v.tensor_scalar(mx, mx, -1.0, None, ALU.mult).then_inc(c.steps_done, 1)
        c.steps += 1

        @c.block.scalar
        def _(s):
            s.wait_ge(c.steps_done, c.steps)
            for h in range(heads):
                s.activation(dm[:, h, 0:n], ld[:, h, 0:n], ACT.Exp, bias=mx[:, h:h + 1])
            s.activation(em, mx, ACT.Exp).then_inc(c.steps_done, 1)
        c.steps += 1

        @c.block.vector
        def _(v):
            v.wait_ge(c.steps_done, c.steps)
            for h in range(heads):
                last = v.scalar_tensor_tensor(ld[:, h, 0:n], bank(2, h), scale, dm[:, h, 0:n],
                                              ALU.mult, ALU.mult, accum_out=den[:, h:h + 1])
            last.then_inc(c.steps_done, 1)
        c.steps += 1

        @c.block.scalar
        def _(s):
            s.wait_ge(c.steps_done, c.steps)
            s.activation(den, den, ACT.Abs).then_inc(c.steps_done, 1)
        c.steps += 1

        @c.block.vector
        def _(v):
            v.wait_ge(c.steps_done, c.steps)
            v.tensor_tensor(den, den, em, ALU.max).then_inc(c.steps_done, 1)
        c.steps += 1

        @c.block.vector
        def _(v):
            v.wait_ge(c.steps_done, c.steps)
            v.reciprocal(den, den).then_inc(c.steps_done, 1)
        c.steps += 1
        c.transposes([([ld[:, h, j * P:(j + 1) * P] for j in range(t + 1)], s_t[:, h, 0:t + 1, :])
                      for h in range(heads)])

        @c.block.tensor
        def _(pe):
            pe.wait_ge(c.steps_done, c.steps)
            for h in range(heads):
                for j in range(t + 1):
                    last = pe.matmul(bank(4, h, dv), s_t[:, h, j, :], v_tok[:, j, h * dv:(h + 1) * dv],
                                     start=(j == 0), stop=(j == t))
            last.then_inc(c.steps_done, 1)
        c.steps += 1
        y = out[:, t, :].rearrange("p (h d) -> p h d", d=dv)
        heads_layernorm(c, lambda h: bank(4, h, dv), [den[:, h:h + 1] for h in range(heads)],
                        [y[:, h, :] for h in range(heads)], stats, mv, rs)

        @c.block.vector
        def _(v):
            v.wait_ge(c.steps_done, c.steps)
            v.tensor_tensor(out[:, t, :], out[:, t, :], gain, ALU.mult).then_inc(c.steps_done, 1)
        c.steps += 1

        @c.block.vector
        def _(v):
            v.wait_ge(c.steps_done, c.steps)
            v.tensor_tensor(out[:, t, :], out[:, t, :], o_tok[:, t, :], ALU.mult).then_inc(c.steps_done, 1)
        c.steps += 1


def heads_layernorm(c, src, scales, dsts, stats, mv, rs, eps=EPS):
    n = len(dsts)
    if scales is not None:

        @c.block.vector
        def _(v):
            v.wait_ge(c.steps_done, c.steps)
            for h in range(n):
                last = v.tensor_scalar(dsts[h], src(h), scales[h], None, ALU.mult)
            last.then_inc(c.steps_done, 1)
        c.steps += 1
        src = lambda h: dsts[h]

    @c.block.vector
    def _(v):
        v.wait_ge(c.steps_done, c.steps)
        for h in range(n):
            last = v.bn_stats(stats[:, h, :], src(h))
        last.then_inc(c.steps_done, 1)
    c.steps += 1

    @c.block.vector
    def _(v):
        v.wait_ge(c.steps_done, c.steps)
        for h in range(n):
            last = v.bn_aggr(mv[:, h, :], stats[:, h, :])
        last.then_inc(c.steps_done, 1)
    c.steps += 1

    @c.block.vector
    def _(v):
        v.wait_ge(c.steps_done, c.steps)
        v.tensor_scalar(rs, mv[:, :, 1], eps, None, ALU.add).then_inc(c.steps_done, 1)
    c.steps += 1

    @c.block.scalar
    def _(s):
        s.wait_ge(c.steps_done, c.steps)
        s.activation(rs, rs, ACT.Sqrt).then_inc(c.steps_done, 1)
    c.steps += 1

    @c.block.vector
    def _(v):
        v.wait_ge(c.steps_done, c.steps)
        v.reciprocal(rs, rs).then_inc(c.steps_done, 1)
    c.steps += 1

    @c.block.vector
    def _(v):
        v.wait_ge(c.steps_done, c.steps)
        for h in range(n):
            last = v.tensor_scalar(dsts[h], src(h), mv[:, h, 0:1], rs[:, h:h + 1], ALU.subtract, ALU.mult)
        last.then_inc(c.steps_done, 1)
    c.steps += 1


def spatial_gating(c, us, out, w_t, bias, gain, shift):
    groups, dg = 4, 256
    u, v_tok = us[:, :, 0:D], us[:, :, D:2 * D]
    sm = c.small
    stats = cols(sm, 72, NT * groups, 6)
    mv = cols(sm, 120, NT * groups, 2)
    rs = cols(sm, 136, NT * groups)

    @c.block.scalar
    def _(s):
        s.wait_ge(c.steps_done, c.steps)
        s.activation(us, us, ACT.Gelu_apprx_tanh).then_inc(c.steps_done, 1)
    @c.block.gpsimd
    def _(g):
        g.wait_ge(c.steps_done, c.steps)
        g.affine_select(out=w_t, in_=w_t, compare_op=ALU.is_ge, fill=0.0, base=0,
                        pattern=[[0, groups], [1, P]], channel_multiplier=-1).then_inc(c.steps_done, 1)
    c.steps += 2
    pieces = [v_tok[:, t, g * dg:(g + 1) * dg] for t in range(NT) for g in range(groups)]
    heads_layernorm(c, lambda h: pieces[h], None, pieces, stats, mv, rs)

    @c.block.vector
    def _(v):
        v.wait_ge(c.steps_done, c.steps)
        v.tensor_tensor(v_tok, v_tok, gain.unsqueeze(1).broadcast_to([P, NT, D]), ALU.mult).then_inc(c.steps_done, 1)
    c.steps += 1

    @c.block.vector
    def _(v):
        v.wait_ge(c.steps_done, c.steps)
        v.tensor_tensor(v_tok, v_tok, shift.unsqueeze(1).broadcast_to([P, NT, D]), ALU.add).then_inc(c.steps_done, 1)
    c.steps += 1

    @c.block.tensor
    def _(pe):
        pe.wait_ge(c.steps_done, c.steps)
        for t in range(NT):
            for g in range(groups):
                last = pe.matmul(c.ps[:, t * 2 + g // 2, g % 2 * dg:(g % 2 + 1) * dg], w_t[:, g, :],
                                 v_tok[:, t, g * dg:(g + 1) * dg], start=True, stop=True)
        last.then_inc(c.steps_done, 1)
    c.steps += 1

    @c.block.vector
    def _(v):
        v.wait_ge(c.steps_done, c.steps)
        for t in range(NT):
            for g in range(groups):
                ch = slice(g * dg, (g + 1) * dg)
                last = v.scalar_tensor_tensor(out[:, t, ch], c.ps[:, t * 2 + g // 2, g % 2 * dg:(g % 2 + 1) * dg],
                                              bias[:, g:g + 1], u[:, t, ch], ALU.add, ALU.mult)
        last.then_inc(c.steps_done, 1)
    c.steps += 1


def memory_attention(c, q_t, k_t, v_tok, out):
    heads, dh = 4, 256
    scale = float(dh) ** -0.5
    p = cols(c.work, 0, heads, SEQ)
    p_t = cols(c.work, 1024, heads, NT, P)
    mx, total = cols(c.small, 56, heads), cols(c.small, 60, heads)
    for t in range(NT):
        def bank(first, h):
            return c.ps[:, first + h // 2, h % 2 * SEQ:(h % 2 + 1) * SEQ]

        @c.block.tensor
        def _(pe):
            pe.wait_ge(c.steps_done, c.steps)
            for h in range(heads):
                for j in range(2):
                    last = pe.matmul(bank(0, h), q_t[:, 2 * h + j, t * P:(t + 1) * P], k_t[:, 2 * h + j, :],
                                     start=(j == 0), stop=(j == 1))
            last.then_inc(c.steps_done, 1)
        c.steps += 1

        @c.block.vector
        def _(v):
            v.wait_ge(c.steps_done, c.steps)
            v.reduce_max(
mx, c.ps[:, 0:2, :].rearrange("p b (h s) -> p (b h) s", s=SEQ), AX).then_inc(c.steps_done, 1)
        c.steps += 1

        @c.block.vector
        def _(v):
            v.wait_ge(c.steps_done, c.steps)
            v.tensor_scalar(mx, mx, -scale, None, ALU.mult).then_inc(c.steps_done, 1)
        c.steps += 1

        @c.block.scalar
        def _(s):
            s.wait_ge(c.steps_done, c.steps)
            for h in range(heads):
                last = s.activation(p[:, h, :], bank(0, h), ACT.Exp, bias=mx[:, h:h + 1], scale=scale,
                                    accum_out=total[:, h:h + 1])
            last.then_inc(c.steps_done, 1)
        c.steps += 1

        @c.block.vector
        def _(v):
            v.wait_ge(c.steps_done, c.steps)
            v.reciprocal(total, total).then_inc(c.steps_done, 1)
        c.steps += 1
        c.transposes([([p[:, h, j * P:(j + 1) * P] for j in range(NT)], p_t[:, h, :, :]) for h in range(heads)])

        @c.block.tensor
        def _(pe):
            pe.wait_ge(c.steps_done, c.steps)
            for h in range(heads):
                for j in range(NT):
                    last = pe.matmul(bank(4, h), p_t[:, h, j, :], v_tok[:, j, h * dh:(h + 1) * dh],
                                     start=(j == 0), stop=(j == NT - 1))
            last.then_inc(c.steps_done, 1)
        c.steps += 1

        @c.block.vector
        def _(v):
            v.wait_ge(c.steps_done, c.steps)
            for h in range(heads):
                last = v.tensor_scalar(out[:, t, h * dh:(h + 1) * dh], bank(4, h), total[:, h:h + 1], None,
                                       ALU.mult)
            last.then_inc(c.steps_done, 1)
        c.steps += 1


def first_block(c, a):
    h = c.h
    h_tiles = [h[:, t, :] for t in range(NT)]
    y = cols(c.work, 9728, NT, D)
    y_tiles = [y[:, t, :] for t in range(NT)]
    gain = [c.par[:, n * D:(n + 1) * D] for n in range(4)]
    z = c.z

    for layer in range(DEPTH):
        g = a["norm_g"][layer]

        def feed_forward(which, n_in, n_out):
            c.load(gain[0], g[n_in, :].partition_broadcast(P))
            c.load(gain[1], g[n_out, :].partition_broadcast(P))
            c.loaded()
            c.rmsnorm(h_tiles, y_tiles, gain[0])
            c.input_from(lambda t, k: y[:, t, k * P:(k + 1) * P], *narrow(c), NT)
            swiglu(c, a["w_ffn_gu"][layer, which], a["w_ffn_down"][layer, which], y)
            add_normed(c, h, y, gain[1], 0.5)

        feed_forward(0, 0, 1)

        vo = cols(z, 0, NT, 2 * D)
        us = cols(z, 4096, NT, 2 * D)
        xq_t = cols(z, 8192, KD, SEQ)
        gates = cols(z, 10240, NT, 3 * D)
        qk_pad = cols(z, 16384, KD, 3 + SEQ)
        w_in = a["w_in"][layer]
        i_f = cols(c.small, 0, NT, 8)
        b_if = cols(c.small, 160, 8)
        conv_w = cols(c.small, 168, KD, 4)
        conv_b = cols(c.small, 200, KD)
        c.load(gain[0], g[2, :].partition_broadcast(P))
        c.load(gain[1], a["mlstm_norm_g"][layer, :].partition_broadcast(P))
        c.load(gain[2], a["sgu_ln_g"][layer, :].partition_broadcast(P))
        c.load(gain[3], a["sgu_ln_b"][layer, :].partition_broadcast(P))
        c.load(b_if[:, 0:4], a["b_i"][layer, :].partition_broadcast(P))
        c.load(b_if[:, 4:8], a["b_f"][layer, :].partition_broadcast(P))
        c.load(conv_w, a["conv_w"][layer])
        c.load(conv_b, a["conv_b"][layer])
        c.loaded()
        c.rmsnorm(h_tiles, y_tiles, gain[0])
        c.input_from(lambda t, k: y[:, t, k * P:(k + 1) * P], *narrow(c), NT)

        @c.block.vector
        def _(v):
            v.wait_ge(c.steps_done, c.steps)
            v.memset(qk_pad[:, :, 0:3], 0.0).then_inc(c.steps_done, 1)
        c.steps += 1

        def feature_copies(dst, first=0):
            def place(i, n):
                return dst[:, bass.ds(i * 4 + 2 * n, 2), first:first + SEQ]
            cp = Copies(c, place, 2)
            cp.bank = lambda b: c.ps[:, b, :].rearrange("p (j t) -> p j t", t=SEQ)
            return copy_halves(c, cp)
        c.gemm_feature_major(SEQ, 2, column_units(w_in, 0), *feature_copies(qk_pad, 3), more=True)
        c.gemm_token_major(range(NT), 4, column_chunks(w_in, D), BANK, *token_copies(c, vo, range(NT)),
                           more=True)
        c.gemm_token_major(range(NT), 1, column_chunks(w_in, 3 * D, 8), 8,
                           *token_copies(c, i_f, range(NT), 8), more=True)
        c.gemm_token_major(range(NT), 4, column_chunks(w_in, 3 * D + 8), BANK,
                           *token_copies(c, us, range(NT)), more=True)
        c.gemm_feature_major(SEQ, 2, column_units(w_in, 5 * D + 8), *feature_copies(xq_t), more=True)
        c.gemm_token_major(range(NT), 6, column_chunks(w_in, 6 * D + 8), BANK,
                           *token_copies(c, gates, range(NT)))

        qk_t = cols(c.work, 0, KD, SEQ)
        for tap in range(4):
            part = gates[:, :, tap * (3 * D // 4):(tap + 1) * (3 * D // 4)]

            @c.block.vector
            def _(v):
                v.wait_ge(c.steps_done, c.steps)
                for k in range(KD):
                    src, weight = qk_pad[:, k, tap:tap + SEQ], conv_w[:, k, tap:tap + 1]
                    if tap == 0:
                        last = v.tensor_scalar(qk_t[:, k, :], src, weight, None, ALU.mult)
                    else:
                        last = v.scalar_tensor_tensor(qk_t[:, k, :], src, weight, qk_t[:, k, :],
                                                      ALU.mult, ALU.add)
                last.then_inc(c.steps_done, 1)
            @c.block.scalar
            def _(s):
                s.wait_ge(c.steps_done, c.steps)
                s.activation(part, part, ACT.Sigmoid).then_inc(c.steps_done, 1)
            c.steps += 2

        @c.block.scalar
        def _(s):
            s.wait_ge(c.steps_done, c.steps)
            for k in range(KD):
                last = s.activation(qk_t[:, k, :], qk_t[:, k, :], ACT.Silu, bias=conv_b[:, k:k + 1])
            last.then_inc(c.steps_done, 1)
        @c.block.vector
        def _(v):
            v.wait_ge(c.steps_done, c.steps)
            v.tensor_tensor(
i_f, i_f, b_if.unsqueeze(1).broadcast_to([P, NT, 8]), ALU.add).then_inc(c.steps_done, 1)
        c.steps += 2
        v_tok, o_tok = vo[:, :, 0:D], vo[:, :, D:2 * D]
        mlstm(c, qk_t, v_tok, o_tok, i_f, y, gain[1])
        merged = cols(c.work, 5632, NT, D)
        branch = cols(c.work, 7680, NT, D)

        def merge(which):
            c.input_from(lambda t, k: y[:, t, k * P:(k + 1) * P], *narrow(c), NT)
            dst = merged if which == 0 else branch
            c.gemm_token_major(range(NT), 2, column_chunks(a["w_branch"][layer, which], 0), BANK,
                               *token_copies(c, dst, range(NT)))

            @c.block.vector
            def _(v):
                v.wait_ge(c.steps_done, c.steps)
                v.tensor_tensor(dst, dst, gates[:, :, which * D:(which + 1) * D], ALU.mult).then_inc(c.steps_done, 1)
            c.steps += 1
            if which:

                @c.block.vector
                def _(v):
                    v.wait_ge(c.steps_done, c.steps)
                    v.tensor_tensor(merged, merged, branch, ALU.add).then_inc(c.steps_done, 1)
                c.steps += 1
        merge(0)

        w_t, bias = cols(c.work, 0, 4, P), cols(c.small, 144, 4)
        c.load(w_t, a["sgu_w_s"][layer])
        c.load(bias, a["sgu_b_s"][layer])
        c.load(gain[0], g[6, :].partition_broadcast(P))
        c.load(gain[1], g[3, :].partition_broadcast(P))
        c.loaded()
        spatial_gating(c, us, y, w_t, bias, gain[2], gain[3])
        merge(1)

        mem = cols(z, 0, NT, D)
        k_t = cols(z, 2048, KD, SEQ)
        v_mem = cols(z, 4096, NT, D)
        c.load(mem, a["mem"].rearrange("o (t p) d -> p (o t) d", p=P))
        c.loaded()
        mem_tiles = [mem[:, t, :] for t in range(NT)]
        c.rmsnorm(mem_tiles, y_tiles, gain[0])
        c.input_from(lambda t, k: y[:, t, k * P:(k + 1) * P], *narrow(c), NT)
        w_mkv = a["w_mkv"][layer]
        c.gemm_feature_major(SEQ, 2, column_units(w_mkv, 0), *feature_copies(k_t), more=True)
        c.gemm_token_major(range(NT), 2, column_chunks(w_mkv, D), BANK, *token_copies(c, v_mem, range(NT)))
        memory_attention(c, xq_t, k_t, v_mem, y)
        merge(2)
        c.input_from(lambda t, k: merged[:, t, k * P:(k + 1) * P], *narrow(c), NT)
        c.gemm_token_major(range(NT), 2, column_chunks(a["w_out"][layer], 0), BANK,
                           *token_copies(c, y, range(NT)))
        add_normed(c, h, y, gain[1], 1.0)
        feed_forward(1, 4, 5)


HEADS, HD = 8, 64
RW = HEADS * HD
HYB = 3328
Q_AT = 1792
SSD_G, SSD_HEADS, SSD_P = 8, 32, 64
D_IN = 2 * D
ROWS = 2 * NT
WORK = 11776
LEVELS = 7

LAYOUTS = {
    "conv_w": lambda w: w.reshape(DEPTH, 4, KD, P).transpose(0, 3, 2, 1),
    "conv_b": lambda b: b.reshape(DEPTH, KD, P).transpose(0, 2, 1),
    "sgu_w_s": lambda w: w.transpose(0, 3, 1, 2),
    "sgu_b_s": lambda b: b.transpose(0, 2, 1),
    "c_2": lambda v: v.reshape(KD, P).T,
    "c_ctx_2": lambda v: v.reshape(KD, P).T,
    "ssd_conv_w_2": lambda w: w.reshape(5, 32, P).transpose(2, 1, 0),
    "ssd_conv_b_2": lambda b: b.reshape(32, P).T,
    "rwkv_r_k_2": lambda v: v.reshape(1, RW),
}


def shape_constants():
    j, t = np.arange(P)[:, None], np.arange(P)[None, :]
    shift = 0.5 * (abs(j - t) == 1)
    from_next = 0.5 * ((j == 0) & (t == P - 1))
    from_before = 0.5 * ((j == P - 1) & (t == 0))
    mid = P // 2
    sum_forward = 1.0 * (j <= t) - 1.0 * (j < mid)
    sum_backward = 1.0 * (j >= t) - 1.0 * (j >= mid)
    strictly_before = 1.0 * (j < t)
    halves = 1.0 * ((t == 0) & (j < mid)) + 1.0 * ((t == 1) & (j >= mid))
    merges = [1.0 * ((j >> (n + 1) == t >> (n + 1)) & (j >> n != t >> n)) for n in range(LEVELS)]
    tok = np.arange(SEQ)
    inv = np.float32(10000.0) ** (-np.arange(0, 32, 2, dtype=np.float32) / np.float32(32))
    row = (tok // 64).astype(np.float32)[:, None] * inv
    col = (tok % 64).astype(np.float32)[:, None] * inv
    cos = np.concatenate([np.cos(row), np.cos(row), np.cos(col), np.cos(col)], 1)
    sin = np.concatenate([-np.sin(row), np.sin(row), -np.sin(col), np.sin(col)], 1)
    rope = np.stack([cos, sin], 1).reshape(NT, P, 2, HD).transpose(1, 0, 2, 3)
    return {
        "shifts": np.stack([shift, from_next, from_before], 1).astype(np.float32),
        "sums": np.stack([sum_forward, sum_backward, strictly_before, halves], 1).astype(np.float32),
        "sums_before": np.stack([sum_forward - (j == t), sum_backward - (j == t)], 1).astype(np.float32),
        "merges": np.stack(merges, 1).astype(np.float32),
        "rope": rope.astype(np.float32),
    }


def modulation(c, a, layer, parts, tiles):
    spread = c.x_t[:, :, 0:SEQ]
    cond = cols(c.small, 0, 2, KD)
    c.load(cond[:, 0, :], a["c_2"])
    c.load(cond[:, 1, :], a["c_ctx_2"])
    c.loaded()
    c.split_first_weights()

    @c.block.scalar
    def _(s):
        s.wait_ge(c.steps_done, c.steps)
        s.activation(cond, cond, ACT.Silu).then_inc(c.steps_done, 1)
    c.steps += 1

    @c.block.vector
    def _(v):
        v.wait_ge(c.steps_done, c.steps)
        for n in range(2):
            last = v.tensor_copy(spread[:, :, n * P:(n + 1) * P], cond[:, n, :].unsqueeze(2).broadcast_to([P, KD, P]))
        last.then_inc(c.steps_done, 1)
    c.steps += 1
    split_narrow(c)
    for first, count, dst in parts:
        c.gemm_token_major(tiles, count, column_chunks(a["ada_w_2"][layer], first), BANK,
                           *token_copies(c, dst, tiles), more=dst is not parts[-1][2])


def tiles_of(x, n=NT):
    return [x[:, t, :] for t in range(n)]


def modulated_norms(c, xs, out, gain, shifts, scales):
    tiles = [(seq, x, out[:, NT * seq + t, :]) for seq in range(len(xs)) for t, x in enumerate(xs[seq])]
    ss = c.small[:, 0:len(tiles)]

    @c.block.vector
    def _(v):
        v.wait_ge(c.steps_done, c.steps)
        for seq in range(len(xs)):
            last = v.scalar_tensor_tensor(scales[:, seq, :], scales[:, seq, :], 1.0, gain, ALU.add, ALU.mult)
        last.then_inc(c.steps_done, 1)
    @c.block.scalar
    def _(s):
        s.wait_ge(c.steps_done, c.steps)
        for j, (_, x, y) in enumerate(tiles):
            last = s.activation(y, x, ACT.Square, accum_out=ss[:, j:j + 1])
        last.then_inc(c.steps_done, 1)
    c.steps += 2
    c.rstd(ss, 1.0 / D, EPS)

    @c.block.vector
    def _(v):
        v.wait_ge(c.steps_done, c.steps)
        for j, (seq, x, y) in enumerate(tiles):
            last = v.scalar_tensor_tensor(y, x, ss[:, j:j + 1], scales[:, seq, :], ALU.mult, ALU.mult)
        last.then_inc(c.steps_done, 1)
    c.steps += 1

    @c.block.vector
    def _(v):
        v.wait_ge(c.steps_done, c.steps)
        for seq, _, y in tiles:
            last = v.tensor_tensor(y, y, shifts[:, seq, :], ALU.add)
        last.then_inc(c.steps_done, 1)
    c.steps += 1


def heads_of(x, n=HEADS):
    if len(x.shape) == 2:
        return x.rearrange("p (h d) -> p h d", h=n)
    return x.rearrange("p t (h d) -> p t h d", h=n)


def rwkv(c, a, rows):
    ps, small, w, x_t = c.ps, c.small, c.work, cols_of(c.x_t)
    kk = cols(c.z, ROWS * HYB, ROWS, RW)
    y_all = cols(c.z, ROWS * HYB + 2048, ROWS, RW)
    low_t = cols(c.z, ROWS * HYB + 4096, ROWS, P)
    up = [cols(x_t, 3456, RW), cols(c.z, ROWS * HYB + 4608, RW)]
    merges = cols(x_t, 2560, LEVELS, P)
    state = cols(x_t, 1536, 2, HEADS, HD)[0:HD]
    inv_t = cols(x_t, 0, HEADS, P)
    u = cols(x_t, 1024, RW)
    sums_before = c.after[:, 1, :].rearrange("p (a t) -> p a t", t=P)
    sums = c.future[:, :, :].rearrange("p a (b t) -> p (a b) t", t=P)
    w0 = [c.par[:, n * RW:(n + 1) * RW] for n in range(2)]
    a0 = [c.par[:, (2 + n) * RW:(3 + n) * RW] for n in range(2)]
    k_k, k_a, r_k, g_up = (c.par[:, n * RW:(n + 1) * RW] for n in range(4, 8))

    n_mix = Q_AT
    quarter = n_mix // 4
    delta = cols(w, 0, ROWS, n_mix)
    mu = cols(w, ROWS * n_mix, n_mix)
    shifts = cols(w, ROWS * n_mix + n_mix, 3, P)
    c.load(mu, a["rwkv_mu_2"][0, :].partition_broadcast(P))
    c.load(shifts, a["shifts"])
    c.load(merges, a["merges"])
    c.load(sums, a["sums"])
    c.load(sums_before, a["sums_before"])
    for d in range(2):
        c.load(w0[d], a["rwkv_w0_2"][0, d, :].partition_broadcast(P))
        c.load(a0[d], a["rwkv_a0_2"][0, d, :].partition_broadcast(P))
        c.load(up[d][0:HD, :], a["rwkv_w_up_2"][0, d])
        c.load(up[d][HD:P, :], a["rwkv_a_up_2"][0, d])
    c.load(k_k, a["rwkv_k_k_2"][0, :].partition_broadcast(P))
    c.load(k_a, a["rwkv_k_a_2"][0, :].partition_broadcast(P))
    c.load(r_k, a["rwkv_r_k_2"][0, :].partition_broadcast(P))
    c.load(g_up, a["rwkv_g_up_2"][0])
    c.loaded()
    mixed = rows[:, :, 0:n_mix]
    for seq in range(2):

        @c.block.tensor
        def _(pe):
            pe.wait_ge(c.steps_done, c.steps)
            for t in range(NT):
                tile, other = seq * NT + t, seq * NT + 1 - t
                for q in range(4):
                    part = slice(q * quarter, (q + 1) * quarter)
                    out = ps[:, t * 4 + q, 0:quarter]
                    pe.matmul(out, shifts[:, 0, :], rows[:, tile, part], start=True, stop=False)
                    last = pe.matmul(out, shifts[:, 1 + t, :], rows[:, other, part], start=False, stop=True)
            last.then_inc(c.steps_done, 1)
        c.steps += 1

        @c.block.vector
        def _(v):
            v.wait_ge(c.steps_done, c.steps)
            for t in range(NT):
                tile = seq * NT + t
                out = delta[:, tile, :].rearrange("p (q n) -> p q n", q=4)
                last = v.tensor_tensor(out, ps[:, t * 4:t * 4 + 4, 0:quarter],
                                       rows[:, tile, 0:n_mix].rearrange("p (q n) -> p q n", q=4), ALU.subtract)
            last.then_inc(c.steps_done, 1)
        c.steps += 1

    @c.block.vector
    def _(v):
        v.wait_ge(c.steps_done, c.steps)
        v.tensor_tensor(delta, delta, mu.unsqueeze(1).broadcast_to([P, ROWS, n_mix]), ALU.mult).then_inc(c.steps_done, 1)
    c.steps += 1

    @c.block.vector
    def _(v):
        v.wait_ge(c.steps_done, c.steps)
        v.tensor_tensor(mixed, mixed, delta, ALU.add).then_inc(c.steps_done, 1)
    c.steps += 1
    r, k, v_tok = (rows[:, :, n * RW:(n + 1) * RW] for n in range(3))
    low = rows[:, :, 3 * RW:3 * RW + P]
    gd = rows[:, :, 3 * RW + P:3 * RW + 2 * P]

    square = cols(w, 0, ROWS, RW)
    ss = cols(small, 0, ROWS, HEADS)

    @c.block.vector
    def _(v):
        v.wait_ge(c.steps_done, c.steps)
        v.tensor_tensor(kk, k, k_k.unsqueeze(1).broadcast_to([P, ROWS, RW]), ALU.mult).then_inc(c.steps_done, 1)
    @c.block.scalar
    def _(s):
        s.wait_ge(c.steps_done, c.steps)
        s.activation(low[:, :, 0:HD], low[:, :, 0:HD], ACT.Tanh).then_inc(c.steps_done, 1)
    c.steps += 2

    @c.block.vector
    def _(v):
        v.wait_ge(c.steps_done, c.steps)
        v.tensor_tensor(square, kk, kk, ALU.mult).then_inc(c.steps_done, 1)
    c.steps += 1

    @c.block.vector
    def _(v):
        v.wait_ge(c.steps_done, c.steps)
        v.reduce_sum(ss, heads_of(square), AX).then_inc(c.steps_done, 1)
    c.steps += 1
    c.rstd(ss, 1.0, 1e-12)

    @c.block.vector
    def _(v):
        v.wait_ge(c.steps_done, c.steps)
        v.tensor_tensor(heads_of(kk), heads_of(kk),
                        ss.unsqueeze(3).broadcast_to([P, ROWS, HEADS, HD]), ALU.mult).then_inc(c.steps_done, 1)
    c.steps += 1
    c.transposes([([low[:, t, :] for t in range(ROWS)], low_t)])

    half_heads = HEADS // 2
    half_width = half_heads * HD
    bonus = cols(small, 32, 2, ROWS, HEADS)
    lower = cols(w, 6144, HEADS, P)
    alpha, beta, kappa, rho = (cols(w, n * RW, RW) for n in range(4))
    alpha_t, beta_t, kappa_t, rho_t = (cols(w, 2048 + n * D, HEADS, P)[0:HD] for n in range(4))
    minus_gv = cols(w, 11264, RW)
    level = cols(w, 2048, HEADS, P)
    half = cols(w, 3072, HEADS, P)
    minus_w = cols(w, 4096, HEADS, P)[0:HD]

    def over_heads(mask):
        return mask.unsqueeze(1).broadcast_to([P, half_heads, P])

    class Group:

        def __init__(self, q):
            self.q, self.chain = q, c.chains[q]
            self.heads = slice(half_heads * q, half_heads * (q + 1))
            self.columns = slice(half_width * q, half_width * (q + 1))
            place = 7168 + 2048 * q
            self.g1_t, self.g2_t, self.g3_t, self.inv = (cols(w, place + 512 * n, half_heads, P) for n in range(4))
            self.e_in, self.e_out, self.e_ex, self.lw, self.aa, self.kmod, self.t1 = (
                cols(w, place + half_width * n, half_width) for n in range(7))
            self.ends = cols(small, 96 + 8 * q, half_heads, 2)[0:HD]
            self.alpha, self.beta, self.kappa, self.rho, self.minus_gv, self.u = (
                x[:, self.columns] for x in (alpha, beta, kappa, rho, minus_gv, u))
            self.alpha_t, self.beta_t, self.kappa_t, self.rho_t, self.level, self.half, self.minus_w = (
                x[:, self.heads, :] for x in (alpha_t, beta_t, kappa_t, rho_t, level, half, minus_w))
            self.lower, self.inv_t = lower[:, self.heads, :], inv_t[:, self.heads, :]

        def bank(self, n, width=BANK, parts=P):
            return ps[0:parts, 4 * self.q + n, 0:width]

        def heads_of_bank(self, n, width=P, parts=P):
            return self.bank(n, half_heads * width, parts).rearrange("p (h t) -> p h t", t=width)

        def by_head(self, n, lhs, rhs, pe, width=P, parts=P, start=True):
            for h in range(half_heads):
                last = pe.matmul(self.heads_of_bank(n, width, parts)[:, h, :], lhs(h), rhs(h), start=start,
                                 stop=True, skip_group_check=not start)
            return last

    def head(x, h):
        return x[:, h * HD:(h + 1) * HD]

    groups = [Group(q) for q in range(2)]

    def flat(x):
        return x.rearrange("p h t -> p (h t)")

    def chunk(d, tile, first_of_scan, first_of_tile):
        strict, strict_t, incl_t = ((c.after[:, 0, 0:P], sums[:, 2, :], c.upto[:, :]) if d == 0 else
                                    (sums[:, 2, :], c.after[:, 0, 0:P], c.onward[:, :]))
        for g in groups:
            ch = g.chain

            @ch.block.tensor
            def _(pe):
                pe.wait_ge(ch.steps_done, ch.steps)
                pe.matmul(g.bank(0, half_width), low_t[0:HD, tile, :], up[d][0:HD, g.columns], start=True, stop=True)
                pe.matmul(g.bank(1, half_width), low_t[HD:P, tile, :], up[d][HD:P, g.columns],
                          start=True, stop=True).then_inc(ch.steps_done, 1)
            ch.steps += 1
        for g in groups:
            ch = g.chain

            @ch.block.vector
            def _(v):
                v.wait_ge(ch.steps_done, ch.steps)
                v.tensor_tensor(g.lw, g.bank(0, half_width), w0[d][:, g.columns], ALU.add)
                v.tensor_tensor(g.aa, g.bank(1, half_width), a0[d][:, g.columns], ALU.add).then_inc(ch.steps_done, 1)
            ch.steps += 1
        for g in groups:
            ch = g.chain


            @ch.block.scalar
            def _(s):
                s.wait_ge(ch.steps_done, ch.steps)
                s.activation(g.lw, g.lw, ACT.Sigmoid)
                s.activation(g.aa, g.aa, ACT.Sigmoid).then_inc(ch.steps_done, 1)
            ch.steps += 1
        for g in groups:
            ch = g.chain

            @ch.block.vector
            def _(v):
                v.wait_ge(ch.steps_done, ch.steps)
                v.tensor_scalar(g.lw, g.lw, -math.exp(-0.5), None, ALU.mult)
                v.tensor_tensor(g.beta, kk[:, tile, g.columns], g.aa, ALU.mult)
                v.scalar_tensor_tensor(g.t1, g.aa, -1.0, k_a[:, g.columns], ALU.add, ALU.mult).then_inc(ch.steps_done, 1)
            ch.steps += 1
        for g in groups:
            ch = g.chain

            @ch.block.tensor
            def _(pe):
                pe.wait_ge(ch.steps_done, ch.steps)
                pe.matmul(g.bank(0, half_width), sums[:, d, :], g.lw, start=True, stop=True)
                pe.matmul(g.bank(2, half_width), sums_before[:, d, :], g.lw, start=True, stop=True)
                for h in range(half_heads):
                    last = pe.matmul(g.bank(3, 8, HD)[:, 2 * h:2 * h + 2], head(g.lw, h), sums[:, 3, 0:2],
                                     start=True, stop=True)
                last.then_inc(ch.steps_done, 1)
            @ch.block.vector
            def _(v):
                v.wait_ge(ch.steps_done, ch.steps)
                v.scalar_tensor_tensor(
g.kmod, g.t1, 1.0, k[:, tile, g.columns], ALU.add, ALU.mult).then_inc(ch.steps_done, 1)
            ch.steps += 2
        for g in groups:
            ch = g.chain

            @ch.block.scalar
            def _(s):
                s.wait_ge(ch.steps_done, ch.steps)
                s.activation(g.e_in, g.bank(0, half_width), ACT.Exp)
                s.activation(g.e_out, g.bank(0, half_width), ACT.Exp, scale=-1.0)
                s.activation(g.e_ex, g.bank(2, half_width), ACT.Exp)
                s.activation(g.ends, g.heads_of_bank(3, 2, HD), ACT.Exp).then_inc(ch.steps_done, 1)
            @ch.block.vector
            def _(v):
                v.wait_ge(ch.steps_done, ch.steps)
                v.tensor_tensor(g.t1, g.kmod, r_k[:, g.columns], ALU.mult).then_inc(ch.steps_done, 1)
            ch.steps += 2
        for g in groups:
            ch = g.chain

            @ch.block.vector
            def _(v):
                v.wait_ge(ch.steps_done, ch.steps)
                v.tensor_tensor(g.alpha, kk[:, tile, g.columns], g.e_ex, ALU.mult)
                v.tensor_tensor(g.beta, g.beta, g.e_out, ALU.mult)
                v.tensor_tensor(g.kappa, g.kmod, g.e_out, ALU.mult)
                v.tensor_tensor(g.rho, r[:, tile, g.columns], g.e_in, ALU.mult)
                v.tensor_tensor(g.t1, g.t1, r[:, tile, g.columns], ALU.mult).then_inc(ch.steps_done, 1)
            ch.steps += 1
        for g in groups:
            ch = g.chain

            @ch.block.tensor
            def _(pe):
                pe.wait_ge(ch.steps_done, ch.steps)
                for n, src in enumerate((g.alpha, g.beta, g.kappa, g.rho)):
                    for h in range(half_heads):
                        last = pe.transpose(g.heads_of_bank(n, P, HD)[:, h, :], head(src, h), c.ident[:, :])
                last.then_inc(ch.steps_done, 1)
            @ch.block.vector
            def _(v):
                v.wait_ge(ch.steps_done, ch.steps)
                v.reduce_sum(
bonus[:, d, tile, g.heads], heads_of(g.t1, half_heads), AX).then_inc(ch.steps_done, 1)
            ch.steps += 2
        for g in groups:
            ch = g.chain

            @ch.block.scalar
            def _(s):
                s.wait_ge(ch.steps_done, ch.steps)
                s.activation(g.alpha_t, g.heads_of_bank(0, P, HD), ACT.Copy)
                s.activation(g.kappa_t, g.heads_of_bank(2, P, HD), ACT.Copy).then_inc(ch.steps_done, 1)
            @ch.block.vector
            def _(v):
                v.wait_ge(ch.steps_done, ch.steps)
                v.tensor_copy(g.beta_t, g.heads_of_bank(1, P, HD))
                v.tensor_copy(g.rho_t, g.heads_of_bank(3, P, HD)).then_inc(ch.steps_done, 1)
            ch.steps += 2
        for g in groups:
            ch = g.chain

            @ch.block.tensor
            def _(pe):
                pe.wait_ge(ch.steps_done, ch.steps)
                g.by_head(0, lambda h: g.alpha_t[:, h, :], lambda h: g.beta_t[:, h, :], pe).then_inc(ch.steps_done, 1)
            ch.steps += 1
        for g in groups:
            ch = g.chain

            @ch.block.tensor
            def _(pe):
                pe.wait_ge(ch.steps_done, ch.steps)
                g.by_head(1, lambda h: g.kappa_t[:, h, :], lambda h: g.alpha_t[:, h, :], pe)
                g.by_head(2, lambda h: g.beta_t[:, h, :], lambda h: g.rho_t[:, h, :], pe)
                g.by_head(3, lambda h: g.kappa_t[:, h, :], lambda h: g.rho_t[:, h, :], pe).then_inc(ch.steps_done, 1)
            @ch.block.vector
            def _(v):
                v.wait_ge(ch.steps_done, ch.steps)
                v.tensor_tensor(
g.lower, g.heads_of_bank(0), over_heads(strict), ALU.mult).then_inc(ch.steps_done, 1)
            ch.steps += 2

        for g in groups:
            ch = g.chain

            @ch.block.vector
            def _(v):
                v.wait_ge(ch.steps_done, ch.steps)
                v.tensor_tensor(g.level, g.lower, over_heads(merges[:, 0, :]), ALU.mult)
                v.tensor_tensor(g.g1_t, g.heads_of_bank(1), over_heads(strict_t), ALU.mult).then_inc(ch.steps_done, 1)
            ch.steps += 1
        for g in groups:
            ch = g.chain

            @ch.block.tensor
            def _(pe):
                pe.wait_ge(ch.steps_done, ch.steps)
                g.by_head(0, lambda h: g.level[:, h, :], lambda h: c.ident[:, :], pe)
                g.by_head(1, lambda h: g.g1_t[:, h, :], lambda h: head(v_tok[:, tile, g.columns], h), pe,
                          width=HD).then_inc(ch.steps_done, 1)
            @ch.block.vector
            def _(v):
                v.wait_ge(ch.steps_done, ch.steps)
                v.tensor_tensor(
g.g2_t, g.heads_of_bank(2), over_heads(incl_t), ALU.mult).then_inc(ch.steps_done, 1)
            ch.steps += 2
        for g in groups:
            ch = g.chain

            @ch.block.vector
            def _(v):
                v.wait_ge(ch.steps_done, ch.steps)
                v.tensor_tensor(g.inv, over_heads(c.ident[:, :]), g.level, ALU.subtract)
                v.tensor_tensor(g.inv_t, over_heads(c.ident[:, :]), g.heads_of_bank(0), ALU.subtract).then_inc(ch.steps_done, 1)
            @ch.block.scalar
            def _(s):
                s.wait_ge(ch.steps_done, ch.steps)
                s.mul(g.minus_gv, g.bank(1, half_width), -1.0).then_inc(ch.steps_done, 1)
            ch.steps += 2
        for g in groups:
            ch = g.chain


            @ch.block.tensor
            def _(pe):
                pe.wait_ge(ch.steps_done, ch.steps)
                pe.matmul(g.bank(1), c.ident[:, :], flat(g.inv), start=True, stop=True)
                pe.matmul(g.bank(2), c.ident[:, :], flat(g.inv_t), start=True, stop=True).then_inc(ch.steps_done, 1)
            @ch.block.vector
            def _(v):
                v.wait_ge(ch.steps_done, ch.steps)
                v.tensor_tensor(g.level, g.lower, over_heads(merges[:, 1, :]), ALU.mult)
                v.tensor_tensor(g.g3_t, g.heads_of_bank(3), over_heads(incl_t), ALU.mult).then_inc(ch.steps_done, 1)
            ch.steps += 2
        for n in range(1, LEVELS):
            for g in groups:
                ch = g.chain

                @ch.block.tensor
                def _(pe):
                    pe.wait_ge(ch.steps_done, ch.steps)
                    g.by_head(0, lambda h: g.level[:, h, :], lambda h: g.inv_t[:, h, :], pe).then_inc(ch.steps_done, 1)
                ch.steps += 1
            for g in groups:
                ch = g.chain

                @ch.block.scalar
                def _(s):
                    s.wait_ge(ch.steps_done, ch.steps)
                    s.mul(flat(g.half), g.bank(0), -1.0).then_inc(ch.steps_done, 1)
                ch.steps += 1
            if n < LEVELS - 1:
                for g in groups:
                    ch = g.chain

                    @ch.block.tensor
                    def _(pe):
                        pe.wait_ge(ch.steps_done, ch.steps)
                        g.by_head(2, lambda h: g.inv[:, h, :], lambda h: g.half[:, h, :], pe, start=False)
                        g.by_head(1, lambda h: g.half[:, h, :], lambda h: g.inv[:, h, :], pe, start=False).then_inc(ch.steps_done, 1)
                    @ch.block.vector
                    def _(v):
                        v.wait_ge(ch.steps_done, ch.steps)
                        v.tensor_tensor(
g.level, g.lower, over_heads(merges[:, n + 1, :]), ALU.mult).then_inc(ch.steps_done, 1)
                    ch.steps += 2
                for g in groups:
                    ch = g.chain

                    @ch.block.scalar
                    def _(s):
                        s.wait_ge(ch.steps_done, ch.steps)
                        s.activation(flat(g.inv_t), g.bank(2), ACT.Copy).then_inc(ch.steps_done, 1)
                    @ch.block.vector
                    def _(v):
                        v.wait_ge(ch.steps_done, ch.steps)
                        v.tensor_copy(flat(g.inv), g.bank(1)).then_inc(ch.steps_done, 1)
                    ch.steps += 2
            else:
                for g in groups:
                    ch = g.chain

                    @ch.block.tensor
                    def _(pe):
                        pe.wait_ge(ch.steps_done, ch.steps)
                        g.by_head(2, lambda h: g.inv[:, h, :], lambda h: g.half[:, h, :], pe,
                                  start=False).then_inc(ch.steps_done, 1)
                    ch.steps += 1
                for g in groups:
                    ch = g.chain

                    @ch.block.scalar
                    def _(s):
                        s.wait_ge(ch.steps_done, ch.steps)
                        s.activation(flat(g.inv_t), g.bank(2), ACT.Copy).then_inc(ch.steps_done, 1)
                    ch.steps += 1

        for g in groups:
            ch = g.chain
            before, starts = state[:, d, g.heads, :], g.ends[:, :, d:d + 1]
            if first_of_scan:

                @ch.block.tensor
                def _(pe):
                    pe.wait_ge(ch.steps_done, ch.steps)
                    g.by_head(0, lambda h: head(g.alpha, h), lambda h: g.inv_t[:, h, :], pe,
                              parts=HD).then_inc(ch.steps_done, 1)
                ch.steps += 1
            else:

                @ch.block.tensor
                def _(pe):
                    pe.wait_ge(ch.steps_done, ch.steps)
                    g.by_head(0, lambda h: head(g.alpha, h), lambda h: g.inv_t[:, h, :], pe,
                              parts=HD).then_inc(ch.steps_done, 1)
                @ch.block.vector
                def _(v):
                    v.wait_ge(ch.steps_done, ch.steps)
                    v.tensor_tensor(before, before,
                                    starts.broadcast_to([HD, half_heads, HD]), ALU.mult).then_inc(ch.steps_done, 1)
                ch.steps += 2
        for g in groups:
            ch = g.chain

            @ch.block.scalar
            def _(s):
                s.wait_ge(ch.steps_done, ch.steps)
                s.mul(g.minus_w, g.heads_of_bank(0, P, HD), -1.0).then_inc(ch.steps_done, 1)
            ch.steps += 1
        for g in groups:
            ch = g.chain
            before = state[:, d, g.heads, :]

            @ch.block.tensor
            def _(pe):
                pe.wait_ge(ch.steps_done, ch.steps)
                for h in range(half_heads):
                    out = head(g.bank(3), h)
                    last = pe.matmul(out, g.inv_t[:, h, :], head(g.minus_gv, h), start=True, stop=first_of_scan)
                    if not first_of_scan:
                        last = pe.matmul(out, g.minus_w[:, h, :], before[:, h, :], start=False, stop=True)
                last.then_inc(ch.steps_done, 1)
            ch.steps += 1
        for g in groups:
            ch = g.chain

            @ch.block.scalar
            def _(s):
                s.wait_ge(ch.steps_done, ch.steps)
                s.activation(g.u, g.bank(3, half_width), ACT.Copy).then_inc(ch.steps_done, 1)
            ch.steps += 1
        for g in groups:
            ch = g.chain
            before = state[:, d, g.heads, :]

            @ch.block.tensor
            def _(pe):
                pe.wait_ge(ch.steps_done, ch.steps)
                values = v_tok[:, tile, g.columns]
                for h in range(half_heads):
                    out = head(g.bank(0), h)
                    if not first_of_scan:
                        pe.matmul(out, g.rho_t[:, h, :], before[:, h, :], start=True, stop=False)
                    pe.matmul(out, g.g2_t[:, h, :], head(g.u, h), start=first_of_scan, stop=False)
                    pe.matmul(out, g.g3_t[:, h, :], head(values, h), start=False, stop=True)
                for h in range(half_heads):
                    out = head(g.bank(1, BANK, HD), h)
                    pe.matmul(out, head(g.beta, h), head(g.u, h), start=True, stop=False)
                    last = pe.matmul(out, head(g.kappa, h), head(values, h), start=False, stop=True)
                last.then_inc(ch.steps_done, 1)
            ch.steps += 1
        for g in groups:
            ch = g.chain
            before, ending = state[:, d, g.heads, :], g.ends[:, :, 1 - d:2 - d]
            gained = g.heads_of_bank(1, HD, HD)
            y_g = y_all[:, tile, g.columns]

            @ch.block.vector
            def _(v):
                v.wait_ge(ch.steps_done, ch.steps)
                if first_of_tile:
                    v.tensor_copy(y_g, g.bank(0, half_width))
                else:
                    v.tensor_tensor(y_g, y_g, g.bank(0, half_width), ALU.add)
                if first_of_scan:
                    v.tensor_tensor(before, gained, ending.broadcast_to([HD, half_heads, HD]), ALU.mult).then_inc(ch.steps_done, 1)
                    return
                v.tensor_tensor(before, before, gained, ALU.add).then_inc(ch.steps_done, 1)
            ch.steps += 1
            if not first_of_scan:

                @ch.block.vector
                def _(v):
                    v.wait_ge(ch.steps_done, ch.steps)
                    v.tensor_tensor(before, before, ending.broadcast_to([HD, half_heads, HD]),
                                    ALU.mult).then_inc(ch.steps_done, 1)
                ch.steps += 1

    c.begin_chains()
    for d, order in enumerate(((2, 3, 0, 1), (3, 2, 1, 0))):
        for n, tile in enumerate(order):
            chunk(d, tile, n == 0, d == 0)
    c.end_chains()

    ln_w, ln_b = k_k, k_a
    c.load(ln_w, a["rwkv_ln_w_2"][0, :].partition_broadcast(P))
    c.load(ln_b, a["rwkv_ln_b_2"][0, :].partition_broadcast(P))
    c.loaded()
    y_h = heads_of(y_all)
    gd_t = cols(w, 2048, ROWS, P)

    def over_width(x):
        return x.unsqueeze(3).broadcast_to([P, ROWS, HEADS, HD])

    def over_rows(x):
        return x.unsqueeze(1).broadcast_to([P, ROWS, RW])

    @c.block.vector
    def _(v):
        v.wait_ge(c.steps_done, c.steps)
        v.reduce_sum(ss, y_h, AX).then_inc(c.steps_done, 1)
    @c.block.scalar
    def _(s):
        s.wait_ge(c.steps_done, c.steps)
        s.activation(gd, gd, ACT.Sigmoid).then_inc(c.steps_done, 1)
    c.steps += 2

    @c.block.vector
    def _(v):
        v.wait_ge(c.steps_done, c.steps)
        v.tensor_scalar(ss, ss, 1.0 / HD, None, ALU.mult).then_inc(c.steps_done, 1)
    c.steps += 1

    @c.block.vector
    def _(v):
        v.wait_ge(c.steps_done, c.steps)
        v.tensor_tensor(y_h, y_h, over_width(ss), ALU.subtract).then_inc(c.steps_done, 1)
    c.steps += 1

    @c.block.vector
    def _(v):
        v.wait_ge(c.steps_done, c.steps)
        v.tensor_tensor(square, y_all, y_all, ALU.mult).then_inc(c.steps_done, 1)
    c.steps += 1

    @c.block.vector
    def _(v):
        v.wait_ge(c.steps_done, c.steps)
        v.reduce_sum(ss, heads_of(square), AX).then_inc(c.steps_done, 1)
    c.steps += 1
    c.rstd(ss, 1.0 / HD, 64e-5)
    c.transposes([([gd[:, t, :] for t in range(ROWS)], gd_t)])

    @c.block.tensor
    def _(pe):
        pe.wait_ge(c.steps_done, c.steps)
        for t in range(ROWS):
            last = pe.matmul(ps[:, t, :], gd_t[:, t, :], g_up, start=True, stop=True)
        last.then_inc(c.steps_done, 1)
    @c.block.vector
    def _(v):
        v.wait_ge(c.steps_done, c.steps)
        v.tensor_tensor(y_h, y_h, over_width(ss), ALU.mult).then_inc(c.steps_done, 1)
    c.steps += 2

    @c.block.vector
    def _(v):
        v.wait_ge(c.steps_done, c.steps)
        v.tensor_tensor(y_all, y_all, over_rows(ln_w), ALU.mult).then_inc(c.steps_done, 1)
    c.steps += 1

    @c.block.vector
    def _(v):
        v.wait_ge(c.steps_done, c.steps)
        v.tensor_tensor(bonus[:, 0], bonus[:, 0], bonus[:, 1], ALU.add).then_inc(c.steps_done, 1)
    c.steps += 1

    @c.block.vector
    def _(v):
        v.wait_ge(c.steps_done, c.steps)
        v.tensor_scalar(bonus[:, 0], bonus[:, 0], 0.5, None, ALU.mult).then_inc(c.steps_done, 1)
    c.steps += 1

    @c.block.vector
    def _(v):
        v.wait_ge(c.steps_done, c.steps)
        v.tensor_tensor(y_all, y_all, over_rows(ln_b), ALU.add).then_inc(c.steps_done, 1)
    c.steps += 1

    @c.block.vector
    def _(v):
        v.wait_ge(c.steps_done, c.steps)
        v.tensor_tensor(heads_of(square), heads_of(v_tok), over_width(bonus[:, 0]), ALU.mult).then_inc(c.steps_done, 1)
    c.steps += 1

    @c.block.vector
    def _(v):
        v.wait_ge(c.steps_done, c.steps)
        v.tensor_tensor(y_all, y_all, square, ALU.add).then_inc(c.steps_done, 1)
    c.steps += 1

    @c.block.vector
    def _(v):
        v.wait_ge(c.steps_done, c.steps)
        v.tensor_tensor(y_all, y_all, ps[:, 0:ROWS, :], ALU.mult).then_inc(c.steps_done, 1)
    c.steps += 1
    return y_all


def cols_of(buf):
    return buf[:, :, :].rearrange("p a b -> p (a b)")


def differential_attention(c, a, rows):
    lam_init = 0.8 - 0.6 * math.exp(-0.3 * 0)
    scale = HD ** -0.5
    ps, small, w, x_t = c.ps, c.small, c.work, cols_of(c.x_t)
    q, k, v_tok = (rows[:, :, Q_AT + n * RW:Q_AT + (n + 1) * RW] for n in range(3))
    qr_t, qp_t, qc_t, kr_t, kc_t = (cols(w, n * 2048, HEADS, SEQ)[0:HD] for n in range(5))
    q_rot, k_rot, swapped = cols(x_t, 0, NT, RW), cols(x_t, 1024, NT, RW), cols(x_t, 2048, NT, RW)
    rope = cols(x_t, 3072, NT, 2, HD)
    lq = cols(small, 256, 4, HD)
    sub_g = cols(c.par, 0, P)
    for n, name in enumerate(("diff_lq1_2", "diff_lk1_2", "diff_lq2_2", "diff_lk2_2")):
        c.load(lq[:, n, :], a[name][0, :].partition_broadcast(P))
    c.load(rope, a["rope"])
    c.load(sub_g, a["diff_subln_g_2"][0, :].partition_broadcast(P))
    c.loaded()
    lam2 = cols(small, 0, 2)
    lam = cols(small, 2, 1)

    @c.block.vector
    def _(v):
        v.wait_ge(c.steps_done, c.steps)
        v.tensor_tensor(lq[:, 0:4:2, :], lq[:, 0:4:2, :], lq[:, 1:4:2, :], ALU.mult).then_inc(c.steps_done, 1)
    c.steps += 1

    @c.block.vector
    def _(v):
        v.wait_ge(c.steps_done, c.steps)
        v.reduce_sum(lam2, lq[:, 0:4:2, :], AX).then_inc(c.steps_done, 1)
    c.steps += 1

    @c.block.scalar
    def _(s):
        s.wait_ge(c.steps_done, c.steps)
        s.activation(lam2, lam2, ACT.Exp).then_inc(c.steps_done, 1)
    c.steps += 1

    @c.block.vector
    def _(v):
        v.wait_ge(c.steps_done, c.steps)
        v.tensor_tensor(lam, lam2[:, 0:1], lam2[:, 1:2], ALU.subtract).then_inc(c.steps_done, 1)
    c.steps += 1

    @c.block.vector
    def _(v):
        v.wait_ge(c.steps_done, c.steps)
        v.tensor_scalar(lam, lam, -1.0, -lam_init, ALU.mult, ALU.add).then_inc(c.steps_done, 1)
    c.steps += 1

    for src, dst in ((q, q_rot), (k, k_rot)):
        for t in range(NT):
            x = src[:, t, :].rearrange("p (b s i) -> p b s i", s=2, i=16)
            sw = swapped[:, t, :].rearrange("p (b s i) -> p b s i", s=2, i=16)
            cos = rope[:, t, 0:1, :].broadcast_to([P, HEADS, HD])
            sin = rope[:, t, 1:2, :].broadcast_to([P, HEADS, HD])
            x_h, d_h, s_h = heads_of(src[:, t, :]), heads_of(dst[:, t, :]), heads_of(swapped[:, t, :])

            @c.block.vector
            def _(v):
                v.wait_ge(c.steps_done, c.steps)
                v.tensor_copy(sw[:, :, 0, :], x[:, :, 1, :])
                v.tensor_copy(sw[:, :, 1, :], x[:, :, 0, :])
                v.tensor_tensor(d_h, x_h, cos, ALU.mult).then_inc(c.steps_done, 1)
            c.steps += 1

            @c.block.vector
            def _(v):
                v.wait_ge(c.steps_done, c.steps)
                v.tensor_tensor(s_h, s_h, sin, ALU.mult).then_inc(c.steps_done, 1)
            c.steps += 1

            @c.block.vector
            def _(v):
                v.wait_ge(c.steps_done, c.steps)
                v.tensor_tensor(dst[:, t, :], dst[:, t, :], swapped[:, t, :], ALU.add).then_inc(c.steps_done, 1)
            c.steps += 1

    c.transposes([([src(t)[:, (b + j) * HD:(b + j + 1) * HD] for j in range(4)],
                   dst[:, b:b + 4, t * P:(t + 1) * P])
                  for src, dst in ((lambda t: q_rot[:, t, :], qr_t), (lambda t: q[:, t, :], qp_t),
                                   (lambda t: q[:, NT + t, :], qc_t), (lambda t: k_rot[:, t, :], kr_t),
                                   (lambda t: k[:, NT + t, :], kc_t))
                  for t in range(NT) for b in (0, 4)])

    p_all = cols(x_t, 0, HEADS, 2 * SEQ)
    heads = HEADS // 2
    p_t = cols(c.z, ROWS * HYB, heads, ROWS, P)
    mx, total = cols(small, 8, HEADS), cols(small, 16, HEADS)
    mx2, total2 = mx, total
    for tile in range(ROWS):
        main = tile < NT
        tokens = slice(tile % NT * P, (tile % NT + 1) * P)
        keys = ROWS if main else NT
        n = keys * P
        first = 0 if main else NT

        @c.block.tensor
        def _(pe):
            pe.wait_ge(c.steps_done, c.steps)
            for b in range(HEADS):
                if main:
                    pe.matmul(ps[:, b, 0:SEQ], qr_t[:, b, tokens], kr_t[:, b, :], start=True, stop=True)
                    last = pe.matmul(ps[:, b, SEQ:2 * SEQ], qp_t[:, b, tokens], kc_t[:, b, :],
                                     start=True, stop=True)
                else:
                    last = pe.matmul(ps[:, b, 0:SEQ], qc_t[:, b, tokens], kc_t[:, b, :], start=True, stop=True)
            last.then_inc(c.steps_done, 1)
        c.steps += 1

        @c.block.vector
        def _(v):
            v.wait_ge(c.steps_done, c.steps)
            v.reduce_max(mx, ps[:, :, 0:n], AX).then_inc(c.steps_done, 1)
        c.steps += 1

        @c.block.vector
        def _(v):
            v.wait_ge(c.steps_done, c.steps)
            v.tensor_scalar(mx, mx, -scale, None, ALU.mult).then_inc(c.steps_done, 1)
        c.steps += 1

        @c.block.scalar
        def _(s):
            s.wait_ge(c.steps_done, c.steps)
            for b in range(HEADS):
                last = s.activation(p_all[:, b, 0:n], ps[:, b, 0:n], ACT.Exp, bias=mx[:, b:b + 1], scale=scale,
                                    accum_out=total[:, b:b + 1])
            last.then_inc(c.steps_done, 1)
        c.steps += 1

        @c.block.vector
        def _(v):
            v.wait_ge(c.steps_done, c.steps)
            v.reciprocal(total, total).then_inc(c.steps_done, 1)
        c.steps += 1
        pairs = total.rearrange("p (h m) -> p h m", m=2)

        @c.block.vector
        def _(v):
            v.wait_ge(c.steps_done, c.steps)
            v.tensor_scalar(pairs[:, :, 1], pairs[:, :, 1], lam, None, ALU.mult).then_inc(c.steps_done, 1)
        c.steps += 1

        @c.block.vector
        def _(v):
            v.wait_ge(c.steps_done, c.steps)
            for h in range(heads):
                last = v.tensor_scalar(p_all[:, 2 * h, 0:n], p_all[:, 2 * h, 0:n], total[:, 2 * h:2 * h + 1],
                                       None, ALU.mult)
            last.then_inc(c.steps_done, 1)
        c.steps += 1

        @c.block.vector
        def _(v):
            v.wait_ge(c.steps_done, c.steps)
            for h in range(heads):
                last = v.scalar_tensor_tensor(p_all[:, 2 * h, 0:n], p_all[:, 2 * h + 1, 0:n],
                                              total[:, 2 * h + 1:2 * h + 2], p_all[:, 2 * h, 0:n],
                                              ALU.mult, ALU.add)
            last.then_inc(c.steps_done, 1)
        c.steps += 1
        c.transposes([([p_all[:, 2 * h, j * P:(j + 1) * P] for j in range(keys)], p_t[:, h, 0:keys, :])
                      for h in range(heads)])

        @c.block.tensor
        def _(pe):
            pe.wait_ge(c.steps_done, c.steps)
            for h in range(heads):
                for j in range(keys):
                    last = pe.matmul(ps[:, 4, h * P:(h + 1) * P], p_t[:, h, j, :],
                                     v_tok[:, first + j, h * P:(h + 1) * P], start=(j == 0), stop=(j == keys - 1))
            last.then_inc(c.steps_done, 1)
        c.steps += 1

        @c.block.vector
        def _(v):
            v.wait_ge(c.steps_done, c.steps)
            v.tensor_copy(q[:, tile, :], ps[:, 4, :]).then_inc(c.steps_done, 1)
        c.steps += 1

    square = cols(w, 0, ROWS, RW)
    ss = cols(small, 32, ROWS, heads)
    q_h = heads_of(q, heads)

    @c.block.vector
    def _(v):
        v.wait_ge(c.steps_done, c.steps)
        v.tensor_tensor(square, q, q, ALU.mult).then_inc(c.steps_done, 1)
    c.steps += 1

    @c.block.vector
    def _(v):
        v.wait_ge(c.steps_done, c.steps)
        v.reduce_sum(ss, heads_of(square, heads), AX).then_inc(c.steps_done, 1)
    c.steps += 1
    c.rstd(ss, 1.0 / P, EPS)

    @c.block.vector
    def _(v):
        v.wait_ge(c.steps_done, c.steps)
        v.tensor_scalar(ss, ss, 1.0 - lam_init, None, ALU.mult).then_inc(c.steps_done, 1)
    c.steps += 1

    @c.block.vector
    def _(v):
        v.wait_ge(c.steps_done, c.steps)
        v.tensor_tensor(q_h, q_h, ss.unsqueeze(3).broadcast_to([P, ROWS, heads, P]), ALU.mult).then_inc(c.steps_done, 1)
    c.steps += 1
    for t in range(ROWS):

        @c.block.vector
        def _(v):
            v.wait_ge(c.steps_done, c.steps)
            v.tensor_tensor(q_h[:, t], q_h[:, t], sub_g.unsqueeze(1).broadcast_to([P, heads, P]),
                            ALU.mult).then_inc(c.steps_done, 1)
        c.steps += 1
    return q


def hybrid_mixer(c, a, out):
    rows = cols(c.z, 0, ROWS, HYB)
    c.gemm_token_major(range(ROWS), 6, column_chunks(a["hy_w_in_2"][0], 0), BANK,
                       *token_copies(c, rows, range(ROWS)), more=True)
    n = HYB - 6 * BANK
    c.gemm_token_major(range(ROWS), 1, column_chunks(a["hy_w_in_2"][0], 6 * BANK, n), n,
                       *token_copies(c, rows[:, :, 6 * BANK:], range(ROWS), n))
    y = rwkv(c, a, rows)
    o = differential_attention(c, a, rows)
    c.input_from(lambda t, k: y[:, t, k * P:(k + 1) * P] if k < 4 else o[:, t, (k - 4) * P:(k - 3) * P],
                 *wide(c, ROWS * P), ROWS)
    c.gemm_token_major(range(ROWS), 2, column_chunks(a["hy_w_out_2"][0], 0), BANK,
                       *token_copies(c, out, range(ROWS)))


def ssd_mixer(c, a, out):
    ps, small, w = c.ps, c.small, c.work
    x_t = c.x_t
    xs = cols(c.z, 0, ROWS, D_IN)
    b_tok = cols(c.z, 8192, ROWS, D)
    b_t = cols(c.z, 12288, SSD_G, SEQ)
    c_t = cols(c.z, 16384, SSD_G, SEQ)
    z = cols(w, 0, NT, D_IN)
    xs_t = cols(c.z, 8192, D_IN // P, 2, SEQ)
    b_both_t = cols(w, 0, SSD_G, 2, SEQ)
    pads = [cols(w, 4096, 4, 2, SEQ + 4), cols(c.par, 1024, 4, 2, SEQ + 4)]
    w_in = a["ssd_w_in_2"][0]
    taps = cols(c.par, 0, 32, 5)
    conv_b = cols(c.par, 160, 32)
    dt_bias = cols(c.par, 192, 2, SSD_HEADS)
    decay_rate = cols(c.par, 256, 2, SSD_HEADS)
    d_skip = cols(c.par, 320, SSD_HEADS)
    dt_raw = cols(small, 0, ROWS, SSD_HEADS)
    c.load(taps, a["ssd_conv_w_2"])
    c.load(conv_b, a["ssd_conv_b_2"])
    for d in range(2):
        c.load(dt_bias[:, d, :], a["ssd_dt_bias_2"][0, d, :].partition_broadcast(P))
        c.load(decay_rate[:, d, :], a["ssd_a_log_2"][0, d, :].partition_broadcast(P))
    c.load(d_skip, a["ssd_d_2"][0, :].partition_broadcast(P))
    c.loaded()

    @c.block.vector
    def _(v):
        v.wait_ge(c.steps_done, c.steps)
        v.memset(pads[0], 0.0)
        v.memset(pads[1], 0.0).then_inc(c.steps_done, 1)
    c.steps += 1
    taps_of_chunk = 2 * 5

    def convolved(i, seqs):
        if i < 4:
            return xs_t[:, i * 4:i * 4 + 4, :, :]
        if i < 6:
            return b_both_t[:, i * 4 - 16:i * 4 - 12, :, :]
        return c_t[:, i * 4 - 24:i * 4 - 20, :].unsqueeze(2)

    def convolution(first, count, seqs):
        tokens = seqs * SEQ
        per_bank = BANK // tokens
        banks = 4 // per_bank

        def fill(i, half, n, copy):
            src = ps[:, half * 4 + n, :].rearrange("p (g s t) -> p g s t", g=per_bank, s=seqs)
            return copy(pads[i % 2][:, n * per_bank:(n + 1) * per_bank, 0:seqs, 2:2 + SEQ], src)

        def silu(i, s):
            s.wait_ge(c.taps_done, taps_of_chunk * (i + 1))
            dst = convolved(i, seqs)
            for g in range(4):
                last = s.activation(dst[:, g], dst[:, g], ACT.Silu, bias=conv_b[:, i * 4 + g:i * 4 + g + 1])
            return last

        def take_scalar(chunk, half, s):
            i = first + chunk
            if i >= 2:
                s.wait_ge(c.taps_done, taps_of_chunk * (i - 1))
            for n in range(0, banks, 2):
                last = fill(i, half, n, lambda dst, src: s.activation(dst, src, ACT.Copy))
            last.then_inc(c.pads_filled, 1)
            if chunk:
                return silu(i - 1, s)
            s.wait_ge(c.pads_filled, 2 * (i + 1))

        def half_taps(i, part, v):
            dst, pad = convolved(i, seqs), pads[i % 2]
            for tap in range(5):
                if tap or part or i:
                    v.wait_ge(c.taps_done, taps_of_chunk * i + 5 * part + tap)
                for g in (2 * part, 2 * part + 1):
                    src, weight = pad[:, g, 0:seqs, tap:tap + SEQ], taps[:, i * 4 + g, tap:tap + 1]
                    if tap == 0:
                        last = v.tensor_scalar(dst[:, g], src, weight, None, ALU.mult)
                    else:
                        last = v.scalar_tensor_tensor(dst[:, g], src, weight, dst[:, g], ALU.mult, ALU.add)
                last.then_inc(c.taps_done, 1)

        def take_vector(chunk, half, v):
            i = first + chunk
            for n in range(1, banks, 2):
                last = fill(i, half, n, v.tensor_copy)
            last.then_inc(c.pads_filled, 1)
            v.wait_ge(c.pads_filled, 2 * (i + 1))
            half_taps(i, 0, v)

        def finish(chunk, v):
            half_taps(first + chunk, 1, v)
        c.gemm_feature_major(tokens, count, column_units(w_in, D_IN + first * BANK), take_scalar, take_vector,
                             finish=finish)

        @c.block.scalar
        def _(s):
            silu(first + count - 1, nc_scalar).then_inc(c.steps_done, 1)
        c.steps += 1
    nc_scalar = c.nc.scalar
    convolution(0, 6, 2)
    convolution(6, 2, 1)
    c.transposes([([xs_t[:, i + g, t // NT, t % NT * P:(t % NT + 1) * P] for g in range(4)],
                   xs[:, t, i * P:(i + 4) * P].rearrange("p (g n) -> p g n", g=4))
                  for i in range(0, D_IN // P, 4) for t in range(ROWS)])

    @c.block.vector
    def _(v):
        v.wait_ge(c.steps_done, c.steps)
        v.tensor_copy(b_t, b_both_t[:, :, 0, :]).then_inc(c.steps_done, 1)
    c.steps += 1
    c.transposes([([b_both_t[:, i + g, t // NT, t % NT * P:(t % NT + 1) * P] for g in range(4)],
                   b_tok[:, t, i * P:(i + 4) * P].rearrange("p (g n) -> p g n", g=4))
                  for i in range(0, SSD_G, 4) for t in range(ROWS)])
    c.gemm_token_major(range(ROWS), 1, column_chunks(w_in, 6144, SSD_HEADS), SSD_HEADS,
                       *token_copies(c, dt_raw, range(ROWS), SSD_HEADS), more=True)
    c.gemm_token_major(range(NT), 4, column_chunks(w_in, 0), BANK, *token_copies(c, z, range(NT)))
    y = cols(w, 4096, NT, D_IN)
    state = cols(w, 8192, SSD_HEADS, SSD_P)
    cb = cols(w, 10240, SSD_G, P)
    free = cols_of(c.x_t)
    xdt, xw = cols(free, 0, SSD_HEADS, SSD_P), cols(free, 2048, SSD_HEADS, SSD_P)
    dt = cols(small, 128, ROWS, SSD_HEADS)
    dta = cols(small, 256, ROWS, SSD_HEADS)
    before = cols_of(c.future)[:, 2 * P:3 * P]
    t1, t2, t3 = (cols(c.par, 3072 + n * P, ROWS, SSD_HEADS) for n in range(3))
    raw = cols(c.par, 3072 + 3 * P, ROWS, SSD_HEADS)

    half_heads, half_groups = SSD_HEADS // 2, SSD_G // 2

    def over_width(x):
        return x.unsqueeze(2).broadcast_to([P, x.shape[1], SSD_P])

    def as_heads(x):
        return x.rearrange("p (h d) -> p h d", d=SSD_P)

    class Half:

        def __init__(self, q):
            self.q, self.chain = q, c.chains[q]
            self.heads = slice(half_heads * q, half_heads * (q + 1))
            self.groups = slice(half_groups * q, half_groups * (q + 1))
            self.columns = slice(half_heads * SSD_P * q, half_heads * SSD_P * (q + 1))
            self.xdt, self.xw, self.state = (x[:, self.heads, :] for x in (xdt, xw, state))
            self.cb = cb[:, self.groups, :]
            self.ex = cols(small, 384 + 3 * half_heads * q, 3, half_heads)
            self.seg_l, self.seg_e = ([cols(c.par, 1024, 8, P), cols(c.par, 2048, 8, P)],
                                      [cols(c.z, 14336, 8, P), cols(c.z, 15360, 8, P)])[q]
            self.off = ([cols(c.par, 1024, half_heads, SSD_P), cols(c.z, 14336, half_heads, SSD_P)])[q]

        def bank(self, n):
            return ps[:, 4 * self.q + n, :]

        def two_banks(self, n, width):
            return ps[:, 4 * self.q + n:4 * self.q + n + 2, :].rearrange("p b (h d) -> p (b h) d", d=width)

    halves = [Half(q) for q in range(2)]

    @c.block.scalar
    def _(s):
        s.wait_ge(c.steps_done, c.steps)
        s.activation(z, z, ACT.Silu).then_inc(c.steps_done, 1)
    c.steps += 1

    @c.block.scalar
    def _(s):
        s.wait_ge(c.steps_done, c.steps)
        s.activation(decay_rate, decay_rate, ACT.Exp).then_inc(c.steps_done, 1)
    c.steps += 1

    @c.block.vector
    def _(v):
        v.wait_ge(c.steps_done, c.steps)
        v.tensor_scalar(decay_rate, decay_rate, -1.0, None, ALU.mult).then_inc(c.steps_done, 1)
    c.steps += 1

    @c.block.vector
    def _(v):
        v.wait_ge(c.steps_done, c.steps)
        for t in range(NT):
            last = v.tensor_tensor(as_heads(y[:, t, :]), as_heads(xs[:, t, :]), over_width(d_skip), ALU.mult)
        last.then_inc(c.steps_done, 1)
    c.steps += 1

    def chunk(tile, after, incl, first_of_scan, last_of_scan):
        for g in halves:
            ch = g.chain

            @ch.block.tensor
            def _(pe):
                pe.wait_ge(ch.steps_done, ch.steps)
                for n, mask in enumerate((after, incl, c.ones[:, :])):
                    last = pe.matmul(g.bank(0)[:, n * half_heads:(n + 1) * half_heads], mask,
                                     dta[:, tile, g.heads], start=True, stop=True)
                last.then_inc(ch.steps_done, 1)
            @ch.block.vector
            def _(v):
                v.wait_ge(ch.steps_done, ch.steps)
                v.tensor_tensor(
g.xdt, as_heads(xs[:, tile, g.columns]), over_width(dt[:, tile, g.heads]), ALU.mult).then_inc(ch.steps_done, 1)
            ch.steps += 2
        for g in halves:
            ch = g.chain

            @ch.block.scalar
            def _(s):
                s.wait_ge(ch.steps_done, ch.steps)
                s.activation(
g.ex, g.bank(0)[:, 0:3 * half_heads].rearrange("p (k h) -> p k h", k=3), ACT.Exp).then_inc(ch.steps_done, 1)
            ch.steps += 1
        for g in halves:
            ch = g.chain

            @ch.block.vector
            def _(v):
                v.wait_ge(ch.steps_done, ch.steps)
                v.tensor_tensor(g.xw, g.xdt, over_width(g.ex[:, 0, :]), ALU.mult).then_inc(ch.steps_done, 1)
            ch.steps += 1
        if tile < NT:
            tokens = slice(tile * P, (tile + 1) * P)
            for g in halves:
                ch = g.chain

                @ch.block.tensor
                def _(pe):
                    pe.wait_ge(ch.steps_done, ch.steps)
                    for n in range(half_groups):
                        group = g.q * half_groups + n
                        pe.matmul(g.bank(2)[:, n * P:(n + 1) * P], b_t[:, group, tokens], c_t[:, group, tokens],
                                  start=True, stop=True)
                    for n in range(half_groups):
                        last = pe.matmul(g.bank(n // 2)[:, n % 2 * SEQ:(n % 2 + 1) * SEQ],
                                         c_t[:, g.q * half_groups + n, tokens],
                                         g.state[:, n * 4:(n + 1) * 4, :].rearrange("p h d -> p (h d)"),
                                         start=True, stop=True)
                    last.then_inc(ch.steps_done, 1)
                ch.steps += 1
            for g in halves:
                ch = g.chain

                @ch.block.vector
                def _(v):
                    v.wait_ge(ch.steps_done, ch.steps)
                    v.tensor_tensor(g.cb, g.bank(2).rearrange("p (g l) -> p g l", l=P),
                                    incl.unsqueeze(1).broadcast_to([P, half_groups, P]), ALU.mult)
                    v.tensor_tensor(g.off, g.two_banks(0, SSD_P), over_width(g.ex[:, 1, :]), ALU.mult).then_inc(ch.steps_done, 1)
                ch.steps += 1
            for g in halves:
                ch = g.chain
                y_g = as_heads(y[:, tile, g.columns])

                @ch.block.vector
                def _(v):
                    v.wait_ge(ch.steps_done, ch.steps)
                    v.tensor_tensor(y_g, y_g, g.off, ALU.add).then_inc(ch.steps_done, 1)
                ch.steps += 1
            for part in range(2):
                for g in halves:
                    ch = g.chain
                    first = g.q * half_heads + part * 8

                    @ch.block.vector
                    def _(v):
                        v.wait_ge(ch.steps_done, ch.steps)
                        v.tensor_tensor(
   g.seg_l, after.unsqueeze(1).broadcast_to([P, 8, P]),
   dta[:, tile, first:first + 8].unsqueeze(2).broadcast_to([P, 8, P]), ALU.mult).then_inc(ch.steps_done, 1)
                    ch.steps += 1
                for g in halves:
                    ch = g.chain

                    @ch.block.tensor
                    def _(pe):
                        pe.wait_ge(ch.steps_done, ch.steps)
                        for h in range(8):
                            last = pe.matmul(g.bank(2 + h // 4)[:, h % 4 * P:(h % 4 + 1) * P], g.seg_l[:, h, :], incl,
                                             start=True, stop=True)
                        last.then_inc(ch.steps_done, 1)
                    ch.steps += 1
                for g in halves:
                    ch = g.chain

                    @ch.block.scalar
                    def _(s):
                        s.wait_ge(ch.steps_done, ch.steps)
                        s.activation(g.seg_e, g.two_banks(2, P), ACT.Exp).then_inc(ch.steps_done, 1)
                    ch.steps += 1
                for g in halves:
                    ch = g.chain
                    seg_g = g.seg_e.rearrange("p (g h) l -> p g h l", g=2)

                    @ch.block.vector
                    def _(v):
                        v.wait_ge(ch.steps_done, ch.steps)
                        v.tensor_tensor(
   seg_g, seg_g, g.cb[:, 2 * part:2 * part + 2, :].unsqueeze(2).broadcast_to([P, 2, 4, P]),
   ALU.mult).then_inc(ch.steps_done, 1)
                    ch.steps += 1
                for g in halves:
                    ch = g.chain

                    @ch.block.tensor
                    def _(pe):
                        pe.wait_ge(ch.steps_done, ch.steps)
                        for h in range(8):
                            last = pe.matmul(g.bank(part)[:, h * SSD_P:(h + 1) * SSD_P], g.seg_e[:, h, :],
                                             g.xdt[:, part * 8 + h, :], start=True, stop=True)
                        last.then_inc(ch.steps_done, 1)
                    ch.steps += 1
            for g in halves:
                ch = g.chain
                y_g = as_heads(y[:, tile, g.columns])

                @ch.block.vector
                def _(v):
                    v.wait_ge(ch.steps_done, ch.steps)
                    v.tensor_tensor(y_g, y_g, g.two_banks(0, SSD_P), ALU.add).then_inc(ch.steps_done, 1)
                ch.steps += 1
        if last_of_scan:
            return
        for g in halves:
            ch = g.chain

            def grow(pe):
                for n in range(half_groups):
                    group = g.q * half_groups + n
                    last = pe.matmul(g.bank(n // 2)[:, n % 2 * SEQ:(n % 2 + 1) * SEQ],
                                     b_tok[:, tile, group * P:(group + 1) * P],
                                     g.xw[:, n * 4:(n + 1) * 4, :].rearrange("p h d -> p (h d)"),
                                     start=True, stop=True)
                return last
            if first_of_scan:

                @ch.block.tensor
                def _(pe):
                    pe.wait_ge(ch.steps_done, ch.steps)
                    grow(pe).then_inc(ch.steps_done, 1)
                ch.steps += 1
            else:

                @ch.block.tensor
                def _(pe):
                    pe.wait_ge(ch.steps_done, ch.steps)
                    grow(pe).then_inc(ch.steps_done, 1)
                @ch.block.vector
                def _(v):
                    v.wait_ge(ch.steps_done, ch.steps)
                    v.tensor_tensor(g.state, g.state, over_width(g.ex[:, 2, :]),
                                    ALU.mult).then_inc(ch.steps_done, 1)
                ch.steps += 2
        for g in halves:
            ch = g.chain
            if first_of_scan:

                @ch.block.vector
                def _(v):
                    v.wait_ge(ch.steps_done, ch.steps)
                    v.tensor_copy(g.state, g.two_banks(0, SSD_P)).then_inc(ch.steps_done, 1)
                ch.steps += 1
            else:

                @ch.block.vector
                def _(v):
                    v.wait_ge(ch.steps_done, ch.steps)
                    v.tensor_tensor(g.state, g.state, g.two_banks(0, SSD_P), ALU.add).then_inc(ch.steps_done, 1)
                ch.steps += 1

    for d, order in enumerate(((2, 3, 0, 1), (3, 2, 1, 0))):

        @c.block.vector
        def _(v):
            v.wait_ge(c.steps_done, c.steps)
            v.tensor_tensor(
raw, dt_raw, dt_bias[:, d:d + 1, :].broadcast_to([P, ROWS, SSD_HEADS]), ALU.add).then_inc(c.steps_done, 1)
        c.steps += 1
        c.softplus(raw, dt, t1, t2, t3)

        @c.block.vector
        def _(v):
            v.wait_ge(c.steps_done, c.steps)
            v.tensor_tensor(
dta, dt, decay_rate[:, d:d + 1, :].broadcast_to([P, ROWS, SSD_HEADS]), ALU.mult).then_inc(c.steps_done, 1)
        c.steps += 1
        c.begin_chains()
        for n, tile in enumerate(order):
            if d == 0:
                chunk(tile, c.after[:, 0, 0:P], c.upto[:, :], n == 0, n == 3)
            else:
                chunk(tile, before, c.onward[:, :], n == 0, n == 3)
        c.end_chains()

    gain = cols(c.par, 1024, D_IN)
    c.load(gain, a["ssd_norm_g_2"][0, :].partition_broadcast(P))
    c.loaded()
    ss = cols(small, 0, NT, SSD_G)
    square = cols(free, 0, NT, D_IN)
    y_g = y.rearrange("p t (g d) -> p t g d", g=SSD_G)

    @c.block.vector
    def _(v):
        v.wait_ge(c.steps_done, c.steps)
        v.tensor_tensor(y, y, z, ALU.mult).then_inc(c.steps_done, 1)
    c.steps += 1

    @c.block.vector
    def _(v):
        v.wait_ge(c.steps_done, c.steps)
        v.tensor_tensor(square, y, y, ALU.mult).then_inc(c.steps_done, 1)
    c.steps += 1

    @c.block.vector
    def _(v):
        v.wait_ge(c.steps_done, c.steps)
        v.reduce_sum(ss, square.rearrange("p t (g d) -> p t g d", g=SSD_G), AX).then_inc(c.steps_done, 1)
    c.steps += 1
    c.rstd(ss, 1.0 / 256, EPS)

    @c.block.vector
    def _(v):
        v.wait_ge(c.steps_done, c.steps)
        v.tensor_tensor(y_g, y_g, ss.unsqueeze(3).broadcast_to([P, NT, SSD_G, 256]), ALU.mult).then_inc(c.steps_done, 1)
    c.steps += 1

    @c.block.vector
    def _(v):
        v.wait_ge(c.steps_done, c.steps)
        v.tensor_tensor(y, y, gain.unsqueeze(1).broadcast_to([P, NT, D_IN]), ALU.mult).then_inc(c.steps_done, 1)
    c.steps += 1
    y_t = cols(free, 0, D_IN // P, SEQ)
    c.to_feature_major(lambda t, k: y[:, t, k * P:(k + 1) * P], y_t, NT, D_IN // P)
    c.gemm_rows(y_t, D_IN // P, range(NT), a["ssd_w_out_2"][0], rows_stage(c.work_split))
    c.take_rows(out, NT)


def second_block(c, a):
    y4 = cols(c.work, 0, ROWS, D)
    gain = [c.par[:, n * D:(n + 1) * D] for n in range(4)]
    for layer in range(DEPTH):
        last_layer = layer == DEPTH - 1
        mods = cols(c.z, 0, 2, 2 * D)
        modulation(c, a, layer, [(0, 4, mods)], range(2))
        c.load(c.par[:, 0:2 * D], a["ada_b_2"][layer, 0:2 * D].partition_broadcast(P))
        c.load(gain[2], a["norm1_g_2"][layer, :].partition_broadcast(P))
        c.loaded()

        @c.block.vector
        def _(v):
            v.wait_ge(c.steps_done, c.steps)
            v.tensor_tensor(mods, mods, c.par[:, 0:2 * D].unsqueeze(1).broadcast_to(
[P, 2, 2 * D]), ALU.add).then_inc(c.steps_done, 1)
        c.steps += 1
        modulated_norms(c, [tiles_of(x) for x in (c.h, c.hc)], y4, gain[2], mods[:, :, 0:D], mods[:, :, D:2 * D])
        c.input_from(lambda t, k: y4[:, t, k * P:(k + 1) * P], *wide(c, ROWS * P), ROWS)
        if layer % 2 == 0:
            mixed = cols(c.work, 0, ROWS, D)
            hybrid_mixer(c, a, mixed)
        else:
            mixed = cols(c.work, 0, NT, D)
            ssd_mixer(c, a, mixed)

        seqs = 1 if last_layer else 2
        mods = cols(c.z, 0, 2, 3 * D)
        mod5 = cols(c.z, 16384, 2, D)
        modulation(c, a, layer, [(2 * D, 6, mods), (5 * D, 2, mod5)], range(seqs))
        c.load(c.par[:, :], a["ada_b_2"][layer, 2 * D:6 * D].partition_broadcast(P))
        norm2 = cols(c.z, 8192, D)
        c.load(norm2, a["norm2_g_2"][layer, :].partition_broadcast(P))
        c.loaded()

        @c.block.vector
        def _(v):
            v.wait_ge(c.steps_done, c.steps)
            v.tensor_tensor(mods[:, 0:seqs], mods[:, 0:seqs],
                            c.par[:, 0:3 * D].unsqueeze(1).broadcast_to([P, seqs, 3 * D]), ALU.add)
            v.tensor_tensor(mod5[:, 0:seqs], mod5[:, 0:seqs],
                            gain[3].unsqueeze(1).broadcast_to([P, seqs, D]), ALU.add).then_inc(c.steps_done, 1)
        c.steps += 1
        streams = (c.h, c.hc)[:seqs]

        def add_scaled(out, by):

            @c.block.vector
            def _(v):
                v.wait_ge(c.steps_done, c.steps)
                for n in range(seqs):
                    o = out[:, NT * n:NT * n + NT, :]
                    last = v.tensor_tensor(o, o, by(n).unsqueeze(1).broadcast_to([P, NT, D]), ALU.mult)
                last.then_inc(c.steps_done, 1)
            c.steps += 1

            @c.block.vector
            def _(v):
                v.wait_ge(c.steps_done, c.steps)
                for n, x in enumerate(streams):
                    last = v.tensor_tensor(x[:, :, :], x[:, :, :], out[:, NT * n:NT * n + NT, :], ALU.add)
                last.then_inc(c.steps_done, 1)
            c.steps += 1
        add_scaled(mixed, lambda n: mods[:, n, 0:D])
        modulated_norms(c, [tiles_of(x) for x in streams], y4, norm2, mods[:, 0:seqs, D:2 * D],
                        mods[:, 0:seqs, 2 * D:3 * D])
        tiles = seqs * NT
        tokens = tiles * P
        c.input_from(lambda t, k: y4[:, t, k * P:(k + 1) * P], *wide(c, tokens), tiles)

        k_hidden = 4 * KD
        hidden = cols(c.z, 0, k_hidden, tokens)
        banks = 4 * tokens // BANK

        def relu(i, half, s):
            src = c.ps[:, half * 4:half * 4 + banks, :].rearrange("p b n -> p (b n)")
            return s.activation(hidden[:, bass.ds(i * 4, 4), :].rearrange("p k n -> p (k n)"), src, ACT.Relu)

        def squared(i, half, v):
            part = hidden[:, bass.ds(i * 4, 4), :].rearrange("p k n -> p (k n)")
            return v.tensor_tensor(part, part, part, ALU.mult)
        c.gemm_feature_major(tokens, 8, column_units(a["mlp_w1_2"][layer], 0), relu, squared,
                             after_scalar=True)
        c.gemm_rows(hidden, k_hidden, range(tiles), a["mlp_w2_2"][layer], rows_stage(c.x_t_split))
        out = cols(c.work, 0, tiles, D)
        c.take_rows(out, tiles)
        add_scaled(out, lambda n: mod5[:, n, :])
    final_gain = c.par[:, 0:D]
    c.load(final_gain, a["norm_f_g_2"].partition_broadcast(P))
    c.loaded()
    result = cols(c.work, 0, NT, D)
    c.rmsnorm(tiles_of(c.h), tiles_of(result), final_gain)
    c.result = result


def program(nc, a, out):
    ctx = ExitStack()
    with ctx:
        block = ctx.enter_context(nc.Block())
        c = Core(nc, block, ctx)
        c.z = c.sb("wide", [P, 18560])
        c.h = c.sb("residual", [P, NT, D])
        c.hc = c.sb("context_residual", [P, NT, D])
        x_t_at = nc.sbuf_base
        c.x_t = c.sb("input_feature_major", [P, KD, 2 * SEQ])
        c.x_t_split = nc.alloc_sbuf_tensor_at("input_split", [P, KD, 2 * SEQ], F32R, offset=x_t_at)
        c.par = c.sb("parameters", [P, 4 * D])
        c.small = c.sb("small", [P, 512])
        work_at = nc.sbuf_base
        c.work = c.sb("work", [P, WORK])
        c.work_split = nc.alloc_sbuf_tensor_at("work_split", [P, KD, 2 * SEQ], F32R,
                                               offset=work_at + 4 * (WORK - 2 * KD * SEQ))
        c.result_stored = ctx.enter_context(nc.semaphore("result_stored"))
        c.prime()
        c.load(c.h[:, :, :], a["x"].rearrange("o (t p) d -> p (o t) d", p=P))
        c.load(c.hc[:, :, :], a["ctx_2"].rearrange("o (t p) d -> p (o t) d", p=P))
        c.loaded()
        make_constants(c)
        first_block(c, a)
        second_block(c, a)
        last = c.steps

        @block.sync
        def _(sp):
            sp.wait_ge(c.steps_done, last)
            sp.dma_start(out.rearrange("o (t p) d -> p (o t) d", p=P), c.result).then_inc(c.result_stored, 16)
            sp.wait_ge(c.result_stored, 16)


def kernel(**inputs):
    import numpy as _np
    import concourse.bacc as _bacc
    from concourse import mybir as _mybir
    from concourse.bass_utils import run_bass_kernel_spmd as _run

    laid = {name: _np.asarray(value) for name, value in inputs.items()}
    for name, order in LAYOUTS.items():
        laid[name] = order(laid[name])
    laid.update(shape_constants())
    nc = _bacc.Bacc("TRN2", target_bir_lowering=False, num_devices=1)
    arrays, a = {}, {}
    for name, value in laid.items():
        value = _np.ascontiguousarray(value)
        arrays[f"in_{name}"] = value
        a[name] = nc.dram_tensor(f"in_{name}", value.shape, _mybir.dt.from_np(value.dtype),
                                 kind="ExternalInput").ap()
    out = nc.dram_tensor("out_0", (1, SEQ, D), _mybir.dt.float32, kind="ExternalOutput").ap()
    program(nc, a, out)
    r = _run(nc, [arrays], core_ids=[0])
    return r.results[0]["out_0"]
```
